# Optimizing a Trainium2 kernel written in Bass

```python
import math
import jax, jax.numpy as jnp
from jax import lax
import numpy as np

D_MODEL = 1024
BATCH = 1
SEQ = 256
DEPTH = 2

N_MIXERS = 2
N_META = 16
GDN_HEADS = 8
GDN_HEAD_DIM = 128
GDN_WIDTH = GDN_HEADS * GDN_HEAD_DIM
GDN_CONV = 4
CHUNK = 64
META_PAD = (-N_META) % CHUNK
SC_WIDTH = D_MODEL
SC_CONV = 3
D_FF = 2816
FFN_CONV = 3
N_LAYERS_A = (DEPTH + 1) // 2
N_LAYERS_B = DEPTH // 2
ALPHA = (2.0 * DEPTH) ** 0.25
BETA_INIT = (8.0 * DEPTH) ** -0.25
LN_EPS = 1e-5
RMS_EPS = 1e-6
L2_EPS = 1e-6


def causal_dwconv(x, w):
    width, ch = w.shape
    return lax.conv_general_dilated(
        x, w[:, None, :].astype(x.dtype), window_strides=(1,), padding=[(width - 1, 0)],
        dimension_numbers=("NWC", "WIO", "NWC"), feature_group_count=ch)

def layer_norm(x, g, b):
    xf = x.astype(jnp.float32)
    mu = jnp.mean(xf, axis=-1, keepdims=True)
    var = jnp.mean(jnp.square(xf - mu), axis=-1, keepdims=True)
    y = (xf - mu) * lax.rsqrt(var + LN_EPS) * g.astype(jnp.float32) + b.astype(jnp.float32)
    return y.astype(x.dtype)

def l2norm(x):
    return x * lax.rsqrt(jnp.sum(x * x, axis=-1, keepdims=True) + L2_EPS)

def chunk_gated_delta_rule(q, k, v, g, beta):
    bsz, t_len, h, dk = q.shape
    n = t_len // CHUNK

    def to_chunks(t):
        return jnp.transpose(t.reshape(bsz, n, CHUNK, h, -1), (0, 3, 1, 2, 4))

    q, k, v = to_chunks(q), to_chunks(k), to_chunks(v)
    g = jnp.transpose(g.reshape(bsz, n, CHUNK, h), (0, 3, 1, 2))
    beta = jnp.transpose(beta.reshape(bsz, n, CHUNK, h), (0, 3, 1, 2))
    g = jnp.cumsum(g, axis=-1)

    causal = jnp.tril(jnp.ones((CHUNK, CHUNK), dtype=bool))
    strict = jnp.tril(jnp.ones((CHUNK, CHUNK), dtype=bool), -1)
    decay = jnp.exp(jnp.where(causal, g[..., :, None] - g[..., None, :], -jnp.inf))

    k_beta = k * beta[..., None]
    v_beta = v * beta[..., None]
    m = jnp.where(strict, jnp.einsum("bhnid,bhnjd->bhnij", k_beta, k) * decay, 0.0)
    a_mat = jnp.eye(CHUNK, dtype=q.dtype) + m
    u = lax.linalg.triangular_solve(a_mat, v_beta, left_side=True, lower=True)
    w = lax.linalg.triangular_solve(a_mat, k_beta * jnp.exp(g)[..., None], left_side=True, lower=True)

    qk = jnp.einsum("bhnid,bhnjd->bhnij", q, k) * decay
    q_g = q * jnp.exp(g)[..., None]
    g_last = g[..., -1]
    k_dec = k * jnp.exp(g_last[..., None] - g)[..., None]

    def step(state, inp):
        qg_i, kd_i, u_i, w_i, qk_i, gl_i = inp
        v_new = u_i - jnp.einsum("bhcd,bhde->bhce", w_i, state)
        o_i = jnp.einsum("bhcd,bhde->bhce", qg_i, state) + jnp.einsum("bhij,bhje->bhie", qk_i, v_new)
        state = state * jnp.exp(gl_i)[..., None, None] + jnp.einsum("bhcd,bhce->bhde", kd_i, v_new)
        return state, o_i

    xs = tuple(jnp.moveaxis(t, 2, 0) for t in (q_g, k_dec, u, w, qk, g_last))
    state0 = jnp.zeros((bsz, h, dk, v.shape[-1]), dtype=q.dtype)
    _, o = lax.scan(step, state0, xs)
    return jnp.transpose(o, (1, 0, 3, 2, 4)).reshape(bsz, t_len, h, -1)

def gated_deltanet(h, w_in, conv_w, a_log, dt_bias, norm_w, w_out):
    bsz, seq_len, _ = h.shape
    proj = h @ w_in
    qkv, z, b_raw, a_raw = jnp.split(
        proj, [3 * GDN_WIDTH, 4 * GDN_WIDTH, 4 * GDN_WIDTH + GDN_HEADS], axis=-1)
    qkv = jax.nn.silu(causal_dwconv(qkv, conv_w))
    q, k, v = [t.reshape(bsz, seq_len, GDN_HEADS, GDN_HEAD_DIM).astype(jnp.float32)
               for t in jnp.split(qkv, 3, axis=-1)]
    q = l2norm(q) * (GDN_HEAD_DIM ** -0.5)
    k = l2norm(k)
    beta = jax.nn.sigmoid(b_raw.astype(jnp.float32))
    g = -jnp.exp(a_log.astype(jnp.float32)) * jax.nn.softplus(
        a_raw.astype(jnp.float32) + dt_bias.astype(jnp.float32))
    pad4 = ((0, 0), (META_PAD, 0), (0, 0), (0, 0))
    pad3 = ((0, 0), (META_PAD, 0), (0, 0))
    o = chunk_gated_delta_rule(jnp.pad(q, pad4), jnp.pad(k, pad4), jnp.pad(v, pad4),
                               jnp.pad(g, pad3), jnp.pad(beta, pad3))[:, META_PAD:]
    o = o * lax.rsqrt(jnp.mean(o * o, axis=-1, keepdims=True) + RMS_EPS) * norm_w.astype(jnp.float32)
    o = o * jax.nn.silu(z.reshape(bsz, seq_len, GDN_HEADS, GDN_HEAD_DIM).astype(jnp.float32))
    return o.reshape(bsz, seq_len, GDN_WIDTH).astype(h.dtype) @ w_out

def short_conv_mixer(h, w_in, conv_w, w_out):
    b_gate, c_gate, xv = jnp.split(h @ w_in, 3, axis=-1)
    u = causal_dwconv(c_gate * xv, conv_w)
    return (b_gate * u) @ w_out

def conv_ffn(h, w_up, conv_w, w_down):
    u, gate = jnp.split(h @ w_up, 2, axis=-1)
    u = causal_dwconv(u, conv_w)
    return (jax.nn.silu(u) * gate) @ w_down

def first_inputs(seed: int = 0) -> dict:
    key = jax.random.key(seed)
    ks = iter(jax.random.split(key, 32))
    f32 = jnp.float32

    def nrm(shape, scale):
        return jax.random.normal(next(ks), shape, f32) * scale

    a_in_cols = 4 * GDN_WIDTH + 2 * GDN_HEADS
    dt = jnp.exp(jax.random.uniform(next(ks), (N_LAYERS_A, GDN_HEADS), f32,
                                    math.log(1e-3), math.log(1e-1)))
    return {
        "x": nrm((BATCH, SEQ, D_MODEL), 1.0),
        "meta": nrm((N_META, D_MODEL), 1.0),
        "a_w_in": nrm((N_LAYERS_A, D_MODEL, a_in_cols), D_MODEL ** -0.5),
        "a_conv": nrm((N_LAYERS_A, GDN_CONV, 3 * GDN_WIDTH), GDN_CONV ** -0.5),
        "a_log": jnp.log(jax.random.uniform(next(ks), (N_LAYERS_A, GDN_HEADS), f32, 1.0, 16.0)),
        "a_dt_bias": dt + jnp.log(-jnp.expm1(-dt)),
        "a_norm": 1.0 + nrm((N_LAYERS_A, GDN_HEAD_DIM), 0.02),
        "a_w_out": nrm((N_LAYERS_A, GDN_WIDTH, D_MODEL), BETA_INIT * GDN_WIDTH ** -0.5),
        "b_w_in": nrm((N_LAYERS_B, D_MODEL, 3 * SC_WIDTH), D_MODEL ** -0.5),
        "b_conv": nrm((N_LAYERS_B, SC_CONV, SC_WIDTH), SC_CONV ** -0.5),
        "b_w_out": nrm((N_LAYERS_B, SC_WIDTH, D_MODEL), BETA_INIT * SC_WIDTH ** -0.5),
        "ln_mix_g": 1.0 + nrm((DEPTH, D_MODEL), 0.02),
        "ln_mix_b": nrm((DEPTH, D_MODEL), 0.02),
        "ffn_w_up": nrm((DEPTH, D_MODEL, 2 * D_FF), D_MODEL ** -0.5),
        "ffn_conv": nrm((DEPTH, FFN_CONV, D_FF), FFN_CONV ** -0.5),
        "ffn_w_down": nrm((DEPTH, D_FF, D_MODEL), BETA_INIT * D_FF ** -0.5),
        "ln_ffn_g": 1.0 + nrm((DEPTH, D_MODEL), 0.02),
        "ln_ffn_b": nrm((DEPTH, D_MODEL), 0.02),
    }

def first_block(x, meta, a_w_in, a_conv, a_log, a_dt_bias, a_norm, a_w_out,
              b_w_in, b_conv, b_w_out, ln_mix_g, ln_mix_b,
              ffn_w_up, ffn_conv, ffn_w_down, ln_ffn_g, ln_ffn_b):
    bsz = x.shape[0]
    h = jnp.concatenate(
        [jnp.broadcast_to(meta.astype(x.dtype)[None], (bsz, N_META, D_MODEL)), x], axis=1)
    for i in range(DEPTH):
        j = i // N_MIXERS
        if i % N_MIXERS == 0:
            mix = gated_deltanet(h, a_w_in[j], a_conv[j], a_log[j], a_dt_bias[j], a_norm[j], a_w_out[j])
        else:
            mix = short_conv_mixer(h, b_w_in[j], b_conv[j], b_w_out[j])
        h = layer_norm(ALPHA * h + mix, ln_mix_g[i], ln_mix_b[i])
        h = layer_norm(ALPHA * h + conv_ffn(h, ffn_w_up[i], ffn_conv[i], ffn_w_down[i]),
                       ln_ffn_g[i], ln_ffn_b[i])
    return h[:, N_META:]


DEPTH_2 = 1

FOURIER_GROUPS = 4
FOURIER_WIDTH = D_MODEL // 2
FOURIER_GROUP_DIM = FOURIER_WIDTH // FOURIER_GROUPS
MLA_HEADS = 8
QK_NOPE_DIM = 64
QK_ROPE_DIM = 32
V_HEAD_DIM = (D_MODEL // 2) // MLA_HEADS
Q_LORA_RANK = 384
KV_LORA_RANK = 256
Q_BLOCK = 128
ROPE_THETA = 10000.0
NORM_EPS = 1e-6
N_ADA = 9
W_IN_COLS = FOURIER_WIDTH + Q_LORA_RANK + KV_LORA_RANK + QK_ROPE_DIM + 2 * D_MODEL
SPLIT_1 = FOURIER_WIDTH
SPLIT_2 = SPLIT_1 + Q_LORA_RANK
SPLIT_3 = SPLIT_2 + KV_LORA_RANK
SPLIT_4 = SPLIT_3 + QK_ROPE_DIM


def rms_norm(x, g):
    x32 = x.astype(jnp.float32)
    y = x32 * lax.rsqrt(jnp.mean(x32 * x32, axis=-1, keepdims=True) + NORM_EPS)
    return (y * g.astype(jnp.float32)).astype(x.dtype)

def modulate(h, shift, scale):
    return h * (1 + scale[:, None, :]) + shift[:, None, :]

def swiglu(h, w_gate, w_up, w_down):
    return (jax.nn.silu(h @ w_gate) * (h @ w_up)) @ w_down

def rope_tables(positions):
    half = QK_ROPE_DIM // 2
    inv_freq = 1.0 / (ROPE_THETA ** (jnp.arange(half, dtype=jnp.float32) * 2.0 / QK_ROPE_DIM))
    ang = positions.astype(jnp.float32)[..., None] * inv_freq
    return jnp.cos(ang), jnp.sin(ang)

def apply_rope(x, cos, sin):
    x32 = x.astype(jnp.float32)
    x1, x2 = jnp.split(x32, 2, axis=-1)
    out = jnp.concatenate([x1 * cos - x2 * sin, x2 * cos + x1 * sin], axis=-1)
    return out.astype(x.dtype)

def fourier_mix(u):
    b, s, _ = u.shape
    ug = u.reshape(b, s, FOURIER_GROUPS, FOURIER_GROUP_DIM).astype(jnp.float32)
    f = jnp.fft.fft2(ug, axes=(1, 3), norm="ortho").real
    return f.reshape(b, s, FOURIER_WIDTH).astype(u.dtype)

def mla_attention(q_lat, kv_lat, k_rope, positions, q_norm, w_q_up, kv_norm, w_kv_up):
    b, s, _ = q_lat.shape
    q = (rms_norm(q_lat, q_norm) @ w_q_up).reshape(b, s, MLA_HEADS, QK_NOPE_DIM + QK_ROPE_DIM)
    kv = (rms_norm(kv_lat, kv_norm) @ w_kv_up).reshape(b, s, MLA_HEADS, QK_NOPE_DIM + V_HEAD_DIM)
    q_nope, q_rot = q[..., :QK_NOPE_DIM], q[..., QK_NOPE_DIM:]
    k_nope, v = kv[..., :QK_NOPE_DIM], kv[..., QK_NOPE_DIM:]
    cos, sin = rope_tables(positions)
    q_rot = apply_rope(q_rot, cos[:, :, None, :], sin[:, :, None, :])
    k_rot = apply_rope(k_rope, cos, sin)
    sm_scale = (QK_NOPE_DIM + QK_ROPE_DIM) ** -0.5
    q_nope = q_nope * sm_scale
    q_rot = q_rot * sm_scale
    n_blk = s // Q_BLOCK
    qn_b = q_nope.reshape(b, n_blk, Q_BLOCK, MLA_HEADS, QK_NOPE_DIM).transpose(1, 0, 2, 3, 4)
    qr_b = q_rot.reshape(b, n_blk, Q_BLOCK, MLA_HEADS, QK_ROPE_DIM).transpose(1, 0, 2, 3, 4)

    def attend(blk):
        qn_i, qr_i = blk
        scores = (jnp.einsum('bqhd,bkhd->bhqk', qn_i, k_nope)
                  + jnp.einsum('bqhr,bkr->bhqk', qr_i, k_rot))
        p = jax.nn.softmax(scores.astype(jnp.float32), axis=-1).astype(v.dtype)
        return jnp.einsum('bhqk,bkhd->bqhd', p, v)

    o = lax.map(attend, (qn_b, qr_b))
    return o.transpose(1, 0, 2, 3, 4).reshape(b, s, MLA_HEADS * V_HEAD_DIM)

def second_inputs(seed: int = 0) -> dict:
    key = jax.random.key(seed)
    ks = jax.random.split(key, 24)
    f32 = jnp.float32

    def w(k, shape, fan_in, gain=1.0):
        return (jax.random.normal(k, shape, f32) * (gain * fan_in ** -0.5)).astype(f32)

    def gain(k, shape):
        return 1.0 + 0.02 * jax.random.normal(k, shape, f32)

    L, D = DEPTH_2, D_MODEL
    x = jax.random.normal(ks[0], (BATCH, SEQ, D), f32)
    c = jax.random.normal(ks[1], (BATCH, D), f32)
    offs = jax.random.randint(ks[2], (BATCH, 1), 0, 1024, dtype=jnp.int32)
    positions = (offs + jnp.arange(SEQ, dtype=jnp.int32)[None, :]).astype(jnp.int32)
    return {
        "x": x,
        "c": c,
        "positions": positions,
        "ada_w": w(ks[3], (L, D, N_ADA * D), D, 0.2),
        "ada_b": 0.02 * jax.random.normal(ks[4], (L, N_ADA * D), f32),
        "ffn1_norm": gain(ks[5], (L, D)),
        "ffn1_w_gate": w(ks[6], (L, D, D_FF), D),
        "ffn1_w_up": w(ks[7], (L, D, D_FF), D),
        "ffn1_w_down": w(ks[8], (L, D_FF, D), D_FF),
        "mix_norm": gain(ks[9], (L, D)),
        "w_in": w(ks[10], (L, D, W_IN_COLS), D),
        "q_norm": gain(ks[11], (L, Q_LORA_RANK)),
        "w_q_up": w(ks[12], (L, Q_LORA_RANK, MLA_HEADS * (QK_NOPE_DIM + QK_ROPE_DIM)), Q_LORA_RANK),
        "kv_norm": gain(ks[13], (L, KV_LORA_RANK)),
        "w_kv_up": w(ks[14], (L, KV_LORA_RANK, MLA_HEADS * (QK_NOPE_DIM + V_HEAD_DIM)), KV_LORA_RANK),
        "w_fourier_out": w(ks[15], (L, FOURIER_WIDTH, D), FOURIER_WIDTH),
        "w_mla_out": w(ks[16], (L, MLA_HEADS * V_HEAD_DIM, D), MLA_HEADS * V_HEAD_DIM),
        "w_out": w(ks[17], (L, D, D), D),
        "ffn2_norm": gain(ks[18], (L, D)),
        "ffn2_w_gate": w(ks[19], (L, D, D_FF), D),
        "ffn2_w_up": w(ks[20], (L, D, D_FF), D),
        "ffn2_w_down": w(ks[21], (L, D_FF, D), D_FF),
        "final_norm": gain(ks[22], (D,)),
    }

def second_block(x, c, positions, ada_w, ada_b, ffn1_norm, ffn1_w_gate, ffn1_w_up, ffn1_w_down,
              mix_norm, w_in, q_norm, w_q_up, kv_norm, w_kv_up, w_fourier_out, w_mla_out, w_out,
              ffn2_norm, ffn2_w_gate, ffn2_w_up, ffn2_w_down, final_norm):
    c_act = jax.nn.silu(c)
    for l in range(DEPTH_2):
        mod = c_act @ ada_w[l] + ada_b[l]
        (sh1, sc1, g1, sh2, sc2, g2, sh3, sc3, g3) = jnp.split(mod, N_ADA, axis=-1)

        h = modulate(rms_norm(x, ffn1_norm[l]), sh1, sc1)
        x = x + 0.5 * g1[:, None, :] * swiglu(h, ffn1_w_gate[l], ffn1_w_up[l], ffn1_w_down[l])

        h = modulate(rms_norm(x, mix_norm[l]), sh2, sc2)
        z = h @ w_in[l]
        u_f, q_lat, kv_lat, k_rope, gate_logits = jnp.split(
            z, [SPLIT_1, SPLIT_2, SPLIT_3, SPLIT_4], axis=-1)
        y_a = fourier_mix(u_f) @ w_fourier_out[l]
        y_b = mla_attention(q_lat, kv_lat, k_rope, positions, q_norm[l], w_q_up[l],
                            kv_norm[l], w_kv_up[l]) @ w_mla_out[l]
        gate_a, gate_b = jnp.split(jax.nn.sigmoid(gate_logits), 2, axis=-1)
        y = (gate_a * y_a + gate_b * y_b) @ w_out[l]
        x = x + g2[:, None, :] * y

        h = modulate(rms_norm(x, ffn2_norm[l]), sh3, sc3)
        x = x + 0.5 * g3[:, None, :] * swiglu(h, ffn2_w_gate[l], ffn2_w_up[l], ffn2_w_down[l])
    return rms_norm(x, final_norm)


def setup_inputs(seed=0):
    out = dict(first_inputs(seed))
    for name, value in second_inputs(seed + 1).items():
        if name != "x":
            out[name + "_2"] = value
    return out


def reference(
    x, meta, a_w_in, a_conv, a_log, a_dt_bias, a_norm, a_w_out, b_w_in, b_conv, b_w_out,
    ln_mix_g, ln_mix_b, ffn_w_up, ffn_conv, ffn_w_down, ln_ffn_g, ln_ffn_b, c_2, positions_2,
    ada_w_2, ada_b_2, ffn1_norm_2, ffn1_w_gate_2, ffn1_w_up_2, ffn1_w_down_2, mix_norm_2,
    w_in_2, q_norm_2, w_q_up_2, kv_norm_2, w_kv_up_2, w_fourier_out_2, w_mla_out_2, w_out_2,
    ffn2_norm_2, ffn2_w_gate_2, ffn2_w_up_2, ffn2_w_down_2, final_norm_2,
):
    x = first_block(
        x, meta, a_w_in, a_conv, a_log, a_dt_bias, a_norm, a_w_out, b_w_in, b_conv, b_w_out,
        ln_mix_g, ln_mix_b, ffn_w_up, ffn_conv, ffn_w_down, ln_ffn_g, ln_ffn_b,
    )
    return second_block(
        x, c_2, positions_2, ada_w_2, ada_b_2, ffn1_norm_2, ffn1_w_gate_2, ffn1_w_up_2,
        ffn1_w_down_2, mix_norm_2, w_in_2, q_norm_2, w_q_up_2, kv_norm_2, w_kv_up_2,
        w_fourier_out_2, w_mla_out_2, w_out_2, ffn2_norm_2, ffn2_w_gate_2, ffn2_w_up_2,
        ffn2_w_down_2, final_norm_2,
    )


_drawn_inputs = setup_inputs


def setup_inputs(seed=0):
    import zlib

    import numpy as np

    out = dict(_drawn_inputs(seed))
    spreads = {}
    factors = {'a_norm': 8.0,
     'ada_b_2': 4.644,
     'ffn1_norm_2': 8.0,
     'mix_norm_2': 8.0,
     'q_norm_2': 8.0,
     'w_q_up_2': 8.0,
     'kv_norm_2': 8.0,
     'w_kv_up_2': 4.573,
     'w_mla_out_2': 4.599,
     'ffn2_norm_2': 64.0,
     'final_norm_2': 8.847}
    for name, (base, spread) in spreads.items():
        noise = np.random.default_rng([zlib.crc32(name.encode()), seed]).standard_normal(out[name].shape)
        drawn = base * np.exp(spread * noise) if base else spread * noise
        out[name] = __import__('jax').numpy.asarray(drawn.astype(out[name].dtype))
    for name, factor in factors.items():
        out[name] = (out[name] * factor).astype(out[name].dtype)
    return out
```

```python
from contextlib import ExitStack

import numpy as np

import concourse.bass as bass
from concourse import mybir

F32 = mybir.dt.float32
F32R = mybir.dt.float32r
I32 = mybir.dt.int32
ALU = mybir.AluOpType
ACT = mybir.ActivationFunctionType
AX = mybir.AxisListType

P = 128
D = 1024
KT = D // P
SEQ = 256
META = 16
TOK = SEQ + META
D_FF = 2816
FT = D_FF // P
HEADS = 8
NBLK = 2 * HEADS + 1
MB = NBLK - 1
GROUPS = [(0, 4), (4, 4), (8, 4), (12, 4), (16, 1)]
ALPHA = (2.0 * 2) ** 0.25
LN_EPS, RMS_EPS, L2_EPS, NORM_EPS = 1e-5, 1e-6, 1e-6, 1e-6
SM_SCALE = 96 ** -0.5
PI_IN = float(np.nextafter(np.float32(np.pi), np.float32(0)))
TWO_PI = (6.28125, 0.0019350051879882812, 3.019916050e-7)
LEVELS = 7

N_A = 262
N_F0 = 260
N_B = 258
N_F1 = 256

SLOTS = 4
SLOT_BLOCKS = FT // 2
AHEAD = SLOTS


class Phase:

    def __init__(self, name, first, units, blocks):
        self.name, self.first, self.units, self.blocks = name, first, units, blocks


def plan():
    first, out = 0, []
    for name, units, blocks in [
        ("a_in", 32, KT), ("a_out", 8, KT), ("up0", 2 * FT, KT), ("down0", 16, SLOT_BLOCKS),
        ("b_cx", 16, KT), ("b_gate", 8, KT), ("b_out", 8, KT), ("up1", 2 * FT, KT), ("down1", 16, SLOT_BLOCKS),
        ("up2", 2 * FT, KT), ("down2", 16, SLOT_BLOCKS), ("mix", 48, KT),
        ("up3", 2 * FT, KT), ("down3", 16, SLOT_BLOCKS),
    ]:
        out.append(Phase(name, first, units, blocks))
        first += units
    return out


PHASES = plan()
PH = {p.name: p for p in PHASES}
UNITS = PHASES[-1].first + PHASES[-1].units
BLOCKS_AFTER = {p.name: q.blocks for p, q in zip(PHASES, PHASES[1:])}
ADA_OPS = 9 * KT
ADA_AT = {"up0": 0, "down0": FT, "b_cx": FT + 16, "b_gate": FT + 24, "up1": FT + 28}
CONV_AT = {"up0": 0, "b_cx": FT, "up1": FT + KT}
GATE_AT = {"up0": 0, "up1": FT, "up2": 2 * FT, "up3": 3 * FT}
HID_AT = {"up0": 0, "b_gate": FT, "up1": FT + KT, "up2": 2 * FT + KT, "up3": 3 * FT + KT}
RHS_AT = {"x": 0, "gdn": 8, "ln0": 16, "ln1": 24, "ln2": 32, "rms0": 40, "rms1": 48, "rms2": 56}

C_IDENT, C_MEAN, C_ONES, C_CAUSAL, C_CAUSAL_META, C_SAME_META, C_LEVEL = range(7)
N_CONST = C_LEVEL + LEVELS

_at = 0


def _place(n):
    global _at
    _at += n
    return _at - n


V_ACONV = _place(24 * 4)
V_FCONV = _place(2 * FT * 3)
V_BCONV = _place(KT * 3)
V_LN = _place(8 * KT)
V_ANORM = _place(1)
V_ALOG = _place(NBLK)
V_DT = _place(NBLK)
V_HEAD = _place(HEADS)
V_C = _place(KT)
V_ADAB = _place(9 * KT)
V_NORM = _place(4 * KT)
V_QN = _place(3)
V_KVN = _place(2)
V_INVF = _place(1)
V_SIGN = _place(1)
N_VEC = _at


def build(nc, io):
    ctx = ExitStack()
    with ctx:
        sem = lambda name: ctx.enter_context(nc.semaphore(name))

        base = (nc.sbuf_base + 63) // 32 * 32
        spot = [base]

        def at(name, shape, dt, offset):
            return nc.alloc_sbuf_tensor_at(name, shape, dt, offset=offset)

        def new(name, shape, dt=F32):
            size = int(np.prod(shape[1:])) * 4
            spot[0] += (size + 31) // 32 * 32
            return at(name, shape, dt, spot[0] - (size + 31) // 32 * 32)

        raw = new("raw", [P, SLOTS, SLOT_BLOCKS * P])
        whi = new("whi", [P, SLOTS, SLOT_BLOCKS * P], F32R)
        wlo = new("wlo", [P, SLOTS, SLOT_BLOCKS * P], F32R)
        hf = new("hf", [P, KT, TOK])
        xb_at = spot[0]
        xb = new("xb", [P, KT, TOK])
        hhi_at = spot[0]
        hhi = new("hhi", [P, KT, TOK], F32R)
        hlo_at = spot[0]
        hlo = new("hlo", [P, KT, TOK], F32R)
        sqb = at("sqb", [P, KT, TOK], F32, hlo_at)
        arena = spot[0]
        ahi = new("ahi", [P, FT, N_F0], F32R)
        alo = new("alo", [P, FT, N_F0], F32R)
        acc = new("acc", [P, 9, D])
        ring_at = spot[0]
        ring = new("ring", [P, 2, D])
        tb = new("tb", [P, 2, TOK])
        ab = new("ab", [P, 2, TOK])
        sb = new("sb", [P, 2, TOK])
        cm = new("cm", [P, N_CONST, P])
        vec = new("vec", [P, N_VEC])
        small = new("small", [P, 512])
        small_end = spot[0]
        spot[0] += 2 * SEQ * 4
        assert spot[0] <= nc.sbuf_usable_end, spot[0]

        spot[0] = arena
        kvq = new("kvq", [P, 24 * 2 * P])
        kvqm = new("kvqm", [P, 24 * META])
        zs = new("zs", [P, HEADS, N_A])
        gt = new("gt", [P, NBLK, P])
        bn = new("bn", [P, NBLK, P])
        ex = new("ex", [P, NBLK, P])
        ca = new("ca", [P, NBLK, P])
        gu = new("gu", [P, NBLK, P])
        st = new("st", [P, HEADS, P])
        assert spot[0] <= ring_at
        ktm = at("ktm", [P, NBLK, P], F32, hhi_at)
        vtm = at("vtm", [P, NBLK, P], F32, hlo_at)
        ot = at("ot", [P, NBLK, P], F32, xb_at)
        rr = at("rr", [P, HEADS, P], F32, ring_at)
        vn = at("vn", [P, HEADS, P], F32, ring_at + HEADS * P * 4)
        wab = at("wab", [P, KT, 2 * HEADS], F32, ring_at)
        xrep = at("xrep", [P, KT, P], F32, ring_at + 1024)

        spot[0] = arena
        krot = new("krot", [P, SEQ])
        lat = new("lat", [P, 5, SEQ])
        uf = new("uf", [P, 4, SEQ])
        dft = new("dft", [P, 5, SEQ])
        gates = new("gates", [P, 16, SEQ])
        lhi = new("lhi", [P, 5, SEQ], F32R)
        llo = new("llo", [P, 5, SEQ], F32R)
        qt = new("qt", [P, HEADS, SEQ])
        kt_ = new("kt", [P, HEADS, SEQ])
        vt = new("vt", [P, 2, 512])
        pf_at = spot[0]
        pf = new("pf", [P, 2, 4, SEQ])
        rot = at("rot", [P, HEADS, SEQ], F32, pf_at)
        lsq = at("lsq", [P, 5, SEQ], F32, spot[0])
        fhi = new("fhi", [P, 4, SEQ], F32R)
        flo = new("flo", [P, 4, SEQ], F32R)
        assert spot[0] <= ring_at, (spot[0], ring_at)
        spot[0] = arena + SEQ * 4
        ohi = new("ohi", [P, 4, SEQ], F32R)
        olo = new("olo", [P, 4, SEQ], F32R)
        pr = at("pr", [P, 2, 2, SEQ], F32, ring_at)
        pt = at("pt", [P, 2, 2, SEQ], F32, ring_at + 4 * SEQ * 4)
        outb = at("outb", [P, KT, SEQ], F32, arena)
        cs = at("cs", [P, 2, SEQ], F32, small_end)
        pos = at("pos", [P, SEQ], I32, small_end)

        ps = [ctx.enter_context(nc.psum_tensor(f"ps{i}", [P, 512], F32)) for i in range(8)]

        raw_loaded = [sem(f"raw_loaded{s}") for s in range(SLOTS)]
        hi_split = sem("hi_split")
        lo_split = sem("lo_split")
        unit_done = sem("unit_done")
        tiles_read = sem("tiles_read")
        ld_x, ld_small, ld_cm, ld_ada = sem("ld_x"), sem("ld_small"), sem("ld_cm"), [sem("ld_ada0"), sem("ld_ada1")]
        ada_done = sem("ada_done")
        rhs_hi, rhs_ready = sem("rhs_hi"), sem("rhs_ready")
        a_tap, a_conv = sem("a_tap"), sem("a_conv")
        f_tap, f_conv, f_gate, hid_hi, hid_ready = sem("f_tap"), sem("f_conv"), sem("f_gate"), sem("hid_hi"), sem("hid_ready")
        mean_mm, xc_ready, sq_ready, var_mm, y_ready, hf_ready = (sem(n) for n in ("mean_mm", "xc_ready", "sq_ready", "var_mm", "y_ready", "hf_ready"))
        dve_step, act_step = sem("dve_step"), sem("act_step")
        out_done = sem("out_done")

        ident = cm[:, C_IDENT, :]
        ones = cm[:, C_ONES, :]

        def v1(i):
            return vec[:, i:i + 1] if isinstance(i, int) else vec[:, bass.ds(i, 1)]

        xrep_ready, mm_gate, g_dve, g_act, gl_ready, mm_cum = (sem(n) for n in ("xrep_ready", "mm_gate", "g_dve", "g_act", "gl_ready", "mm_cum"))
        sq_gdn, mm_norm, cols_ready, d_diff, d_exp, m_ready = (sem(n) for n in ("sq_gdn", "mm_norm", "cols_ready", "d_diff", "d_exp", "m_ready"))
        mm_gb, mm_cb, mm_tr, tr_read, mm_x, x_ready, mm_y, tu_ready = (sem(n) for n in ("mm_gb", "mm_cb", "mm_tr", "tr_read", "mm_x", "x_ready", "mm_y", "tu_ready"))
        mm_v0, v0_read, vm_ready, mm_s0, mm_o0, s_ready = (sem(n) for n in ("mm_v0", "v0_read", "vm_ready", "mm_s0", "mm_o0", "s_ready"))
        mm_ks, r_ready, mm_vn, vn_ready, mm_ds, mm_o, o_read, og_ready = (sem(n) for n in ("mm_ks", "r_ready", "mm_vn", "vn_ready", "mm_ds", "mm_o", "o_read", "og_ready"))
        mods_mm, mods_ready, ls_sq, lat_mm, lat_y, lat_f, lat_hi, lat_ready = (sem(n) for n in ("mods_mm", "mods_ready", "ls_sq", "lat_mm", "lat_y", "lat_f", "lat_hi", "lat_ready"))
        four1, pf_ready, four2, f_hi, f_ready = (sem(n) for n in ("four1", "pf_ready", "four2", "f_hi", "f_ready"))
        q_mm, q_read, k_mm, k_read, v_mm, v_read = (sem(n) for n in ("q_mm", "q_read", "k_mm", "k_read", "v_mm", "v_read"))
        rope_ready, s_mm, m_ready2, p_exp, p_ready, t_mm, t_read, o_mm, o_hi, o_ready = (sem(n) for n in ("rope_ready", "s_mm", "m_ready2", "p_exp", "p_ready", "t_mm", "t_read", "o_mm", "o_hi", "o_ready"))
        ld_rope, ld_dft, ang_ready, cs_ready, y_hi, y_lo = (sem(n) for n in ("ld_rope", "ld_dft", "ang_ready", "cs_ready", "y_hi", "y_lo"))
        c_ready, b_tap = sem("c_ready"), sem("b_tap")
        ogb = at("ogb", [P, HEADS, N_A], F32, arena)

        def S_(i):
            return small[:, i * NBLK:(i + 1) * NBLK]


        def split_hi(act, t, s, blocks):
            if not blocks:
                return
            act.wait_ge(raw_loaded[s], t * 16 + 16)
            if not isinstance(t, int) or t:
                act.wait_ge(unit_done, t * SLOTS + (s + 1 - SLOTS))
            nc.scalar.activation(whi[:, s, 0:blocks * P], raw[:, s, 0:blocks * P], ACT.Copy).then_inc(hi_split, 1)

        def split_lo(dve, t, s, blocks):
            if not blocks:
                return
            dve.wait_ge(hi_split, t * SLOTS + (s + 1))
            nc.vector.tensor_tensor(wlo[:, s, 0:blocks * P], raw[:, s, 0:blocks * P],
                                    whi[:, s, 0:blocks * P], ALU.subtract).then_inc(lo_split, 1)

        def steps(eng, phase, body):
            t0, n = phase.first // SLOTS, phase.units // SLOTS
            after = BLOCKS_AFTER.get(phase.name, 0)
            whole = n if after == phase.blocks else n - 1
            with eng.Fori(0, whole) as i:
                body(i + t0, i, phase.blocks)
            if whole < n:
                body(n - 1 + t0, n - 1, after)

        def col(i):
            return vec[:, bass.ds(i, 1)]

        def bcast(row, n):
            return row.unsqueeze(1).to_broadcast([P, n, row.shape[-1]])

        class Steps:

            def __init__(self, eng, s):
                self.eng, self.s, self.n = eng, s, 0

            def __call__(self, instruction):
                instruction.then_inc(self.s, 1)
                self.n += 1
                return self.n

            def after(self, n=None):
                self.eng.wait_ge(self.s, self.n if n is None else n)


        block = ctx.enter_context(nc.Block())

        @block.sync
        def _(sp):
            for k in range(KT):
                sp.dma_start(hf[:, k, :], io["x"][:, k, :]).then_inc(ld_x, 16)
            sp.dma_start(wab[:], io["w_ab"]).then_inc(ld_small, 16)
            sp.dma_start(vec[:], io["vec"]).then_inc(ld_small, 16)
            sp.dma_start(pos[64:96, :], io["pos"]).then_inc(ld_rope, 16)

            def load(p, t, i):
                for s in range(SLOTS):
                    if not isinstance(t, int) or t:
                        sp.wait_ge(lo_split, t * SLOTS + (s + 1 - SLOTS))
                    sp.dma_start(raw[:, s, 0:p.blocks * P], io["w_" + p.name][i * SLOTS + s]).then_inc(raw_loaded[s], 16)

            for p in PHASES:
                t0, n = p.first // SLOTS, p.units // SLOTS
                begin = 0
                if p.first == 0:
                    load(p, 0, 0)
                    sp.dma_start(cm[:], io["cm"]).then_inc(ld_cm, 16)
                    begin = 1
                with sp.Fori(begin, n) as i:
                    load(p, i + t0, i)
            for m in range(KT):
                sp.wait_ge(hf_ready, 7 * KT + m + 1)
                sp.dma_start(io["out"][:, m, :], outb[:, m, :]).then_inc(out_done, 16)
            sp.wait_ge(out_done, 16 * KT)

        @block.gpsimd
        def _(pool):
            pool.wait_ge(tiles_read, 4 + PH["up0"].first)
            nc.gpsimd.memset(acc[:], 0.0).then_inc(ada_done, 1)
            for o in range(2):
                pool.dma_start(ring[:, o, :], io["ada_w"][o]).then_inc(ld_ada[o], 16)
            with pool.Fori(1, ADA_OPS // 2) as i:
                for o in range(2):
                    pool.wait_ge(ada_done, i * 2 + o)
                    pool.dma_start(ring[:, o, :], io["ada_w"][i * 2 + o]).then_inc(ld_ada[o], 16)
            pool.wait_ge(tiles_read, SLOTS + PH["mix"].first)
            pool.dma_start(dft[:], io["dft"]).then_inc(ld_dft, 16)

        @block.scalar
        def _(act):
            mine = Steps(act, act_step)

            def rhs_round(version, k, src, n):
                nc.scalar.activation(hhi[:, k, 0:n], src, ACT.Copy).then_inc(rhs_hi, 1)

            act.wait_ge(ld_small, 32)
            for k in range(KT):
                act.wait_ge(ld_x, 16 * KT)
                rhs_round("x", k, hf[:, k, :], TOK)
            for s in range(SLOTS):
                split_hi(act, 0, s, KT)

            act.wait_ge(g_dve, 1)
            nc.scalar.activation(S_(4), S_(3), ACT.Exp, scale=-1.0).then_inc(g_act, 1)
            nc.scalar.activation(S_(5), S_(1), ACT.Exp, scale=-1.0).then_inc(g_act, 1)
            nc.scalar.activation(S_(6), vec[:, V_ALOG:V_ALOG + NBLK], ACT.Exp).then_inc(g_act, 1)
            act.wait_ge(g_act, 1)
            nc.scalar.activation(S_(4), S_(4), ACT.Ln, bias=1.0).then_inc(g_act, 1)
            act.wait_ge(g_dve, 2)
            nc.scalar.activation(S_(9), S_(7), ACT.Exp).then_inc(g_act, 1)
            nc.scalar.activation(S_(10), S_(10), ACT.Exp).then_inc(g_act, 1)
            nc.scalar.activation(S_(11), S_(8), ACT.Exp).then_inc(g_act, 1)

            def a_kvq(t, i, blocks):
                for s in range(SLOTS):
                    u = i * SLOTS + s
                    act.wait_ge(unit_done, u + 1)
                    nc.scalar.activation(tb[:, s % 2, :], ps[s][:, 0:TOK], ACT.Copy,
                                         scale=col(u * 4 + (V_ACONV + 3))).then_inc(a_tap, 1)
                    split_hi(act, t + 1, s, blocks)
                    act.wait_ge(a_conv, u * 3 + 3)
                    nc.scalar.activation(kvq[:, bass.ds(u * 256, 256)], tb[:, s % 2, META:TOK], ACT.Silu)
                    nc.scalar.activation(kvqm[:, bass.ds(u * META, META)], tb[:, s % 2, 0:META],
                                         ACT.Silu).then_inc(tiles_read, 1)

            with act.Fori(0, 6) as i:
                a_kvq(i, i, KT)
            with act.Fori(6, 8) as i:
                for s in range(SLOTS):
                    act.wait_ge(unit_done, i * SLOTS + (s + 1))
                    nc.scalar.activation(zs[:, i * SLOTS + (s - 24), :], ps[s][:, TOK - N_A:TOK], ACT.Silu).then_inc(tiles_read, 1)
                    split_hi(act, i + 1, s, KT)

            nc.scalar.activation(ex[:, 0:MB, :], kvq[:, 0:MB * P].rearrange("p (b t) -> p b t", t=P), ACT.Square)
            nc.scalar.activation(ex[:, MB, :], kvqm[:, 0:P], ACT.Square).then_inc(sq_gdn, 1)
            nc.scalar.activation(ca[:, 0:MB, :], kvq[:, 16 * 256:24 * 256].rearrange("p (b t) -> p b t", t=P), ACT.Square)
            nc.scalar.activation(ca[:, MB, :], kvqm[:, 2 * P:3 * P], ACT.Square).then_inc(sq_gdn, 1)

            for g, (b0, n) in enumerate(GROUPS):
                act.wait_ge(d_diff, g + 1)
                nc.scalar.activation(ex[:, b0:b0 + n, :], ex[:, b0:b0 + n, :], ACT.Exp).then_inc(d_exp, 1)
                for kind, (dst, scales, m) in enumerate([(ktm, 15, "k"), (vtm, 2, "v")]):
                    act.wait_ge(mm_tr, 2 * g + kind + 1)
                    for j in range(n):
                        last = nc.scalar.activation(dst[:, b0 + j, :], ps[6 + kind][:, j * P:(j + 1) * P], ACT.Copy,
                                                    scale=S_(scales)[:, b0 + j:b0 + j + 1])
                    last.then_inc(tr_read, 1)

            act.wait_ge(mm_v0, 1)
            nc.scalar.activation(vn[:, 7, :], ps[0][:, 0:P], ACT.Copy).then_inc(v0_read, 1)
            for q in range(2):
                act.wait_ge(mm_s0, q + 1)
                nc.scalar.activation(st[:, 4 * q:4 * q + 4, :], ps[1 + q][:, :], ACT.Copy).then_inc(s_ready, 1)
            act.wait_ge(mm_o0, 1)
            nc.scalar.activation(ot[:, MB, :], ps[3][:, 0:P], ACT.Copy).then_inc(o_read, 1)
            for c in range(2):
                for q in range(2):
                    r = 2 * c + q
                    act.wait_ge(mm_vn, r + 1)
                    if r == 0:
                        act.wait_ge(mm_o0, 1)
                    nc.scalar.activation(vn[:, 4 * q:4 * q + 4, :], ps[2 + q][:, :], ACT.Copy).then_inc(vn_ready, 1)
                for q in range(2):
                    r = 2 * c + q
                    act.wait_ge(mm_o, r + 1)
                    nc.scalar.activation(ot[:, 8 * q + c:8 * q + 8:2, :],
                                         ps[6 + q][:, :].rearrange("p (b t) -> p b t", t=P), ACT.Copy).then_inc(o_read, 1)

            act.wait_ge(o_read, 5)
            nc.scalar.activation(ex[:], ot[:], ACT.Square).then_inc(sq_gdn, 1)
            for h in range(HEADS):
                act.wait_ge(og_ready, h + 1)
                nc.scalar.activation(hhi[:, h, 0:N_A], ogb[:, h, :], ACT.Copy).then_inc(rhs_hi, 1)

            def act_splits(phase):
                def body(t, i, blocks):
                    for s in range(SLOTS):
                        split_hi(act, t + 1, s, blocks)
                steps(act, phase, body)

            def act_hidden(name, n, taps=None):
                def body(t, i, blocks):
                    for p in range(2):
                        s0, s1 = 2 * p, 2 * p + 1
                        j = i * 2 + p
                        act.wait_ge(unit_done, t * SLOTS + (s0 + 1))
                        if taps is not None:
                            c = j + CONV_AT[name]
                            nc.scalar.activation(tb[:, p, 0:n], ps[s0][:, 0:n], ACT.Copy, scale=col(j * 3 + taps)).then_inc(f_tap, 1)
                            split_hi(act, t + 1, s0, blocks)
                            act.wait_ge(f_conv, c * 2 + 2)
                            nc.scalar.activation(sb[:, p, 0:n], tb[:, p, 0:n], ACT.Silu).then_inc(f_gate, 1)
                        else:
                            nc.scalar.activation(sb[:, p, 0:n], ps[s0][:, 0:n], ACT.Silu).then_inc(f_gate, 1)
                            split_hi(act, t + 1, s0, blocks)
                        split_hi(act, t + 1, s1, blocks)
                        act.wait_ge(tiles_read, t * SLOTS + (SLOTS + s0 + 2))
                        nc.scalar.activation(ahi[:, j, 0:n], ab[:, p, 0:n], ACT.Copy).then_inc(hid_hi, 1)
                steps(act, PH[name], body)

            def act_norm(i, n, src, ready, gain, shift, dst, version=None):
                for m in range(KT):
                    ready(m)
                    nc.scalar.activation(sqb[:, m, 0:n], src[:, m, 0:n], ACT.Square).then_inc(sq_ready, 1)
                for m in range(KT):
                    act.wait_ge(y_ready, i * KT + m + 1)
                    nc.scalar.activation(dst[:, m, 0:n], xb[:, m, 0:n], ACT.Identity, scale=gain(m),
                                         **({} if shift is None else {"bias": shift(m)})).then_inc(hf_ready, 1)
                    if version:
                        act.wait_ge(hf_ready, i * KT + m + 1)
                        rhs_round(version, m, dst[:, m, 0:n], n)

            def xc_is_there(i):
                return lambda m: act.wait_ge(xc_ready, i * KT + m + 1)

            def act_ln(i, n, version=None):
                act_norm(i, n, xb, xc_is_there(i), lambda m: col(V_LN + 2 * i * KT + m), lambda m: col(V_LN + (2 * i + 1) * KT + m), hf, version)

            nc.scalar.activation(small[:, 300:308], vec[:, V_C:V_C + KT], ACT.Silu).then_inc(c_ready, 1)
            act_splits(PH["a_out"])
            act_ln(0, N_A, "ln0")
            act_hidden("up0", N_F0, V_FCONV)
            act_splits(PH["down0"])
            act_ln(1, N_F0, "ln1")

            def b_cx(t, i, blocks):
                for p in range(2):
                    act.wait_ge(unit_done, t * SLOTS + (2 * p + 1))
                    act.wait_ge(tiles_read, t * SLOTS + (2 * p + SLOTS))
                    nc.scalar.activation(tb[:, p, 0:N_F0], ps[2 * p][:, 0:N_F0], ACT.Copy).then_inc(f_tap, 1)
                    split_hi(act, t + 1, 2 * p, blocks)
                    split_hi(act, t + 1, 2 * p + 1, blocks)

            def b_gate(t, i, blocks):
                for s in range(SLOTS):
                    act.wait_ge(tiles_read, t * SLOTS + (SLOTS + s + 1))
                    nc.scalar.activation(ahi[:, i * SLOTS + s, 0:N_B], ab[:, s % 2, 0:N_B], ACT.Copy).then_inc(hid_hi, 1)
                    split_hi(act, t + 1, s, blocks)

            steps(act, PH["b_cx"], b_cx)
            steps(act, PH["b_gate"], b_gate)
            act_splits(PH["b_out"])
            act_ln(2, N_B, "ln2")
            act_hidden("up1", N_F1, V_FCONV + FT * 3)
            act_splits(PH["down1"])
            act_ln(3, N_F1)

            MIX = PH["mix"]
            M0 = MIX.first // SLOTS

            def a_of(i):
                return lambda m: small[:, 72 + KT * i + m:73 + KT * i + m]

            def sh_of(i):
                return lambda m: small[:, 3 * KT * i + m:3 * KT * i + m + 1]

            def mix_splits(u, k=1):
                for v in range(u, u + k):
                    nxt = v + SLOTS
                    split_hi(act, M0 + nxt // SLOTS, nxt % SLOTS, KT)

            act.wait_ge(ang_ready, 1)
            nc.scalar.activation(cs[64:96, 1, :], tb[64:96, 1, 0:SEQ], ACT.Sin)
            nc.scalar.activation(cs[64:96, 0, :], ab[64:96, 1, 0:SEQ], ACT.Sin).then_inc(cs_ready, 1)

            act.wait_ge(mods_ready, 1)
            act_norm(4, SEQ, hf, lambda m: act.wait_ge(hf_ready, 3 * KT + m + 1), a_of(0), sh_of(0), xb, "rms0")
            act_hidden("up2", SEQ)
            act_splits(PH["down2"])
            act_norm(5, SEQ, hf, lambda m: act.wait_ge(tiles_read, SLOTS + PH["down2"].first + 2 * (m + 1)), a_of(1), sh_of(1), xb, "rms1")

            for u in range(10):
                act.wait_ge(unit_done, MIX.first + u + 1)
                b_ = ps[u % SLOTS]
                if u == 0:
                    nc.scalar.activation(krot[64:96, :], b_[64:96, 0:SEQ], ACT.Copy).then_inc(tiles_read, 1)
                elif u < 6:
                    nc.scalar.activation(lat[:, u - 1, :], b_[:, 0:SEQ], ACT.Copy).then_inc(tiles_read, 1)
                else:
                    nc.scalar.activation(uf[:, u - 6, :], b_[:, 0:SEQ], ACT.Copy).then_inc(tiles_read, 1)
                mix_splits(u)
            for j in range(5):
                act.wait_ge(tiles_read, SLOTS + MIX.first + 2 + j)
                nc.scalar.activation(lsq[:, j, :], lat[:, j, :], ACT.Square).then_inc(ls_sq, 1)

            def gate_unit(u):
                act.wait_ge(unit_done, MIX.first + u + 1)
                nc.scalar.activation(gates[:, u - 10, :], ps[u % SLOTS][:, 0:SEQ], ACT.Sigmoid).then_inc(tiles_read, 1)
                mix_splits(u)

            for u in range(10, 18):
                gate_unit(u)
            for j in range(5):
                act.wait_ge(lat_y, j + 1)
                nc.scalar.activation(lat[:, j, :], lat[:, j, :], ACT.Copy, scale=col(V_QN + j)).then_inc(lat_f, 1)
                act.wait_ge(lat_f, j + 1)
                nc.scalar.activation(lhi[:, j, :], lat[:, j, :], ACT.Copy).then_inc(lat_hi, 1)
            for u in range(18, 26):
                gate_unit(u)
            for j in range(4):
                act.wait_ge(four1, j + 1)
                nc.scalar.activation(pf[:, j // 2, 2 * (j % 2):2 * (j % 2) + 2, :],
                                     ps[4 + j][:, :].rearrange("p (g n) -> p g n", n=SEQ), ACT.Copy).then_inc(pf_ready, 1)
            for g in range(4):
                act.wait_ge(four2, g + 1)
                nc.scalar.activation(fhi[:, g, :], ps[g][:, 0:SEQ], ACT.Copy).then_inc(f_hi, 1)
            mix_splits(26, 3)
            for j in range(4):
                if j < 3:
                    act.wait_ge(q_mm, 2 * j + 2)
                else:
                    act.wait_ge(unit_done, MIX.first + 29)
                nc.scalar.activation(qt[0:96, 2 * j:2 * j + 2, :], ps[4 + j][0:96, :].rearrange("p (g n) -> p g n", n=SEQ), ACT.Copy).then_inc(q_read, 1)
            mix_splits(29, 3)
            for j in range(2):
                if j == 0:
                    act.wait_ge(v_mm, 1)
                else:
                    act.wait_ge(unit_done, MIX.first + 32)
                nc.scalar.activation(vt[:, j, :], ps[4 + j][:, :], ACT.Copy).then_inc(v_read, 1)
            mix_splits(32, 4)
            for h in range(HEADS + 1):
                if h < HEADS:
                    act.wait_ge(m_ready2, h + 1)
                    if h >= 2:
                        act.wait_ge(t_mm, h - 1)
                    for c in range(2):
                        last = nc.scalar.activation(pr[:, h % 2, c, :], ps[4 + h % 2][:, c * SEQ:(c + 1) * SEQ], ACT.Exp,
                                                    scale=SM_SCALE, bias=small[:, 112 + 2 * h + c:113 + 2 * h + c],
                                                    accum_out=small[:, 128 + 2 * h + c:129 + 2 * h + c])
                    last.then_inc(p_exp, 1)
                if h:
                    g = h - 1
                    act.wait_ge(t_mm, g + 1)
                    if g >= 2:
                        act.wait_ge(o_mm, g - 1)
                    nc.scalar.activation(pt[:, g % 2, :, :], ps[6 + g % 2][:, :].rearrange("p (c n) -> p c n", n=SEQ), ACT.Copy).then_inc(t_read, 1)
            for j in range(4):
                act.wait_ge(o_mm, 2 * j + 2)
                nc.scalar.activation(ohi[:, j, :], ps[j][:, 0:SEQ], ACT.Copy).then_inc(o_hi, 1)
            mix_splits(36, 4)
            for u in range(36, 40):
                act.wait_ge(tiles_read, SLOTS + MIX.first + u + 1)
                m = 2 * (u - 36)
                nc.scalar.activation(hhi[:, m:m + 2, 0:SEQ], xb[:, m:m + 2, 0:SEQ], ACT.Copy).then_inc(y_hi, 1)
            for u in range(40, 44):
                mix_splits(u)
            for s in range(SLOTS):
                split_hi(act, M0 + 12, s, KT)

            act_norm(6, SEQ, hf, lambda m: act.wait_ge(tiles_read, SLOTS + MIX.first + 40 + m + 1), a_of(2), sh_of(2), xb, "rms2")
            act_hidden("up3", SEQ)
            act_splits(PH["down3"])
            act_norm(7, SEQ, hf, lambda m: act.wait_ge(tiles_read, SLOTS + PH["down3"].first + 2 * (m + 1)),
                     lambda m: col(V_NORM + 3 * KT + m), None, outb)

        @block.vector
        def _(dve):
            mine = Steps(dve, dve_step)

            def step(instruction):
                mine(instruction)
                mine.after()

            def rsqrt(out, x, n, tmp):
                step(nc.vector.tensor_scalar(out.bitcast(I32), x.bitcast(I32), -0.5, 1597463007.0, ALU.mult, ALU.add))
                for _ in range(3):
                    step(nc.vector.tensor_tensor(tmp, out, out, ALU.mult))
                    step(nc.vector.scalar_tensor_tensor(tmp, tmp, -0.5, x, ALU.mult, ALU.mult))
                    step(nc.vector.scalar_tensor_tensor(out, tmp, 1.5, out, ALU.add, ALU.mult))

            def rhs_rest(version, k, src, n):
                dve.wait_ge(rhs_hi, RHS_AT[version] + k + 1)
                nc.vector.tensor_tensor(hlo[:, k, 0:n], src, hhi[:, k, 0:n], ALU.subtract).then_inc(rhs_ready, 1)

            nc.vector.memset(small[:, 0:1], 0.0).then_inc(tiles_read, SLOTS)
            dve.wait_ge(ld_x, 16 * KT)
            nc.vector.tensor_copy(xrep[:].rearrange("p k (h t) -> p k h t", t=META),
                                  hf[:, :, 0:META].unsqueeze(2).to_broadcast([P, KT, HEADS, META])).then_inc(xrep_ready, 1)
            for k in range(KT):
                rhs_rest("x", k, hf[:, k, :], TOK)
            for s in range(SLOTS):
                split_lo(dve, 0, s, KT)

            dve.wait_ge(ld_small, 32)
            dve.wait_ge(ld_cm, 16)
            dve.wait_ge(mm_gate, 1)
            for which, at_col in ((1, 0), (2, HEADS)):
                for c in range(2):
                    mine(nc.vector.tensor_copy(S_(which)[:, c:MB:2], ps[7][:, c * 16 + at_col:c * 16 + at_col + HEADS]))
                step(nc.vector.tensor_tensor(S_(12)[:, 0:HEADS], ps[7][:, 32 + at_col:32 + at_col + HEADS],
                                             vec[:, V_HEAD:V_HEAD + HEADS], ALU.mult))
                step(nc.vector.reduce_sum(S_(which)[:, MB:NBLK], S_(12)[:, 0:HEADS], AX.X))
            step(nc.vector.tensor_tensor(S_(2), S_(2), vec[:, V_DT:V_DT + NBLK], ALU.add))
            step(nc.vector.tensor_scalar(S_(3), S_(2), -1.0, None, ALU.mult))
            nc.vector.tensor_tensor(S_(3), S_(3), S_(2), ALU.max).then_inc(g_dve, 1)
            dve.wait_ge(g_act, 4)
            step(nc.vector.scalar_tensor_tensor(S_(4), S_(2), 0.0, S_(4), ALU.max, ALU.add))
            nc.vector.scalar_tensor_tensor(S_(6), S_(4), -1.0, S_(6), ALU.mult, ALU.mult).then_inc(gl_ready, 1)
            step(nc.vector.tensor_scalar(S_(5), S_(5), 1.0, None, ALU.add))
            step(nc.vector.reciprocal(S_(2), S_(5)))
            dve.wait_ge(mm_cum, 1)
            step(nc.vector.tensor_copy(S_(7), ps[7][:, 64:64 + NBLK]))
            step(nc.vector.tensor_copy(S_(8), ps[7][:, 96:96 + NBLK]))
            nc.vector.tensor_tensor(S_(10), S_(8), S_(7), ALU.subtract).then_inc(g_dve, 1)

            with dve.Fori(0, 6) as i:
                for s in range(SLOTS):
                    u = i * SLOTS + s
                    t_ = tb[:, s % 2, :]
                    dve.wait_ge(a_tap, u + 1)
                    for j, tap in enumerate((2, 1, 0)):
                        if j:
                            dve.wait_ge(a_conv, u * 3 + j)
                        nc.vector.scalar_tensor_tensor(t_[:, j + 1:TOK], ps[s][:, 0:TOK - 1 - j], col(u * 4 + (V_ACONV + tap)),
                                                       t_[:, j + 1:TOK], ALU.mult, ALU.add).then_inc(a_conv, 1)
                    split_lo(dve, i + 1, s, KT)
            with dve.Fori(6, 8) as i:
                for s in range(SLOTS):
                    split_lo(dve, i + 1, s, KT)

            dve.wait_ge(mm_norm, 1)
            dve.wait_ge(g_act, 7)
            nn = small[:, 320:320 + 2 * NBLK]
            step(nc.vector.tensor_scalar(nn, ps[7][:, 0:2 * NBLK], L2_EPS, None, ALU.add))
            rsqrt(small[:, 360:360 + 2 * NBLK], nn, 2 * NBLK, small[:, 400:400 + 2 * NBLK])
            rk, rq = small[:, 360:360 + NBLK], small[:, 360 + NBLK:360 + 2 * NBLK]
            step(nc.vector.tensor_scalar(S_(13), rq, float(P) ** -0.5, None, ALU.mult))
            step(nc.vector.tensor_tensor(S_(12), rk, S_(2), ALU.mult))
            step(nc.vector.tensor_tensor(S_(14), S_(13), S_(9), ALU.mult))
            step(nc.vector.tensor_tensor(S_(15), rk, S_(10), ALU.mult))
            step(nc.vector.tensor_tensor(S_(16), S_(12), S_(9), ALU.mult))
            nc.vector.tensor_scalar(S_(16), S_(16), -1.0, None, ALU.mult).then_inc(cols_ready, 1)

            for g, (b0, n) in enumerate(GROUPS):
                w = n * P
                dve.wait_ge(mm_gb, g + 1)
                for j in range(n):
                    last = nc.vector.tensor_scalar(ex[:, b0 + j, :], ps[0][:, j * P:(j + 1) * P], S_(7)[:, b0 + j:b0 + j + 1],
                                                   0.0, ALU.subtract, ALU.min)
                last.then_inc(d_diff, 1)
                dve.wait_ge(d_exp, g + 1)
                e_ = ex[:, b0:b0 + n, :]
                bank = lambda i: ps[i][:, 0:w].rearrange("p (b t) -> p b t", t=P)
                dve.wait_ge(mm_cb, g + 1)
                mine(nc.vector.tensor_tensor(bn[:, b0:b0 + n, :], e_, bank(1), ALU.mult))
                step(nc.vector.tensor_tensor(ca[:, b0:b0 + n, :], e_, bank(2), ALU.mult))
                mask = C_CAUSAL_META if b0 == MB else C_CAUSAL
                step(nc.vector.tensor_tensor(ca[:, b0:b0 + n, :], ca[:, b0:b0 + n, :], bcast(cm[:, mask, :], n), ALU.mult))
                if b0 == MB:
                    step(nc.vector.tensor_tensor(bn[:, MB, :], bn[:, MB, :], cm[:, C_SAME_META, :], ALU.mult))
                q_ = kvq[:, 16 * 256 + b0 * P:16 * 256 + b0 * P + w] if b0 < MB else kvqm[:, 2 * P:3 * P]
                mine(nc.vector.tensor_tensor(q_, q_, ps[3][:, 0:w], ALU.mult))
                for j in range(n):
                    b = b0 + j
                    nc.vector.scalar_tensor_tensor(bn[:, b, :], ps[4][:, j * P:(j + 1) * P], rk[:, b:b + 1], bn[:, b, :], ALU.mult, ALU.mult)
                    last = nc.vector.scalar_tensor_tensor(ca[:, b, :], ps[5][:, j * P:(j + 1) * P], rk[:, b:b + 1], ca[:, b, :], ALU.mult, ALU.mult)
                last.then_inc(m_ready, 1)

            mine(nc.vector.tensor_copy(gt[:], bcast(ident, NBLK)))
            nc.vector.tensor_copy(gu[:], bcast(ident, NBLK)).then_inc(tu_ready, 6)
            with dve.Fori(0, LEVELS) as l:
                def mask_x(g):
                    b0, n = GROUPS[g]
                    dve.wait_ge(mm_x, l * 5 + (g + 1))
                    nc.vector.tensor_tensor(ex[:, b0:b0 + n, :], ps[g % 2][:, 0:n * P].rearrange("p (b t) -> p b t", t=P),
                                            cm[:, bass.ds(l + C_LEVEL, 1), :].to_broadcast([P, n, P]), ALU.mult).then_inc(x_ready, 1)

                def add_y(g):
                    b0, n = GROUPS[g]
                    dve.wait_ge(mm_y, l * 5 + (g + 1))
                    nc.vector.tensor_tensor(gt[:, b0:b0 + n, :], gt[:, b0:b0 + n, :],
                                            ps[2 + g % 3][:, 0:n * P].rearrange("p (b t) -> p b t", t=P), ALU.add)
                    nc.vector.tensor_tensor(gu[:, b0:b0 + n, :], gu[:, b0:b0 + n, :],
                                            ps[5 + g % 3][:, 0:n * P].rearrange("p (b t) -> p b t", t=P), ALU.add).then_inc(tu_ready, 1)

                dve.wait_ge(tu_ready, l * 5 + 6)
                for g in range(len(GROUPS)):
                    mask_x(g)
                    if g:
                        add_y(g - 1)
                add_y(len(GROUPS) - 1)

            dve.wait_ge(v0_read, 1)
            for h in range(HEADS):
                last = nc.vector.tensor_scalar(rr[:, h, :], ps[0][:, 0:P], vec[:, V_HEAD + h:V_HEAD + h + 1], None, ALU.mult)
            last.then_inc(vm_ready, 1)
            for c in range(2):
                for q in range(2):
                    r = 2 * c + q
                    dve.wait_ge(mm_ks, r + 1)
                    for j in range(4):
                        h = 4 * q + j
                        b = 2 * h + c
                        last = nc.vector.scalar_tensor_tensor(rr[:, h, :], ps[q][:, j * P:(j + 1) * P], S_(16)[:, b:b + 1],
                                                              vtm[:, b, :], ALU.mult, ALU.add)
                    last.then_inc(r_ready, 1)
                if c == 0:
                    for q in range(2):
                        dve.wait_ge(mm_ds, q + 1)
                        dve.wait_ge(mm_o, q + 1)
                        for j in range(4):
                            h = 4 * q + j
                            last = nc.vector.scalar_tensor_tensor(st[:, h, :], st[:, h, :], S_(11)[:, 2 * h:2 * h + 1],
                                                                  ps[4 + q][:, j * P:(j + 1) * P], ALU.mult, ALU.add)
                        last.then_inc(s_ready, 1)

            dve.wait_ge(mm_norm, 2)
            nn = small[:, 320:320 + NBLK]
            step(nc.vector.tensor_scalar(nn, ps[7][:, 0:NBLK], 1.0 / P, RMS_EPS, ALU.mult, ALU.add))
            rsqrt(small[:, 360:360 + NBLK], nn, NBLK, small[:, 400:400 + NBLK])
            step(nc.vector.tensor_scalar(S_(12), small[:, 360:360 + NBLK], 1.0, None, ALU.mult))
            mine(nc.vector.memset(small[:, 319:320], 0.0))
            nc.vector.memset(small[:, 318:319], 0.0).then_inc(cols_ready, 1)
            for g in (4, 0, 1, 2, 3):
                b0, n = GROUPS[g]
                dve.wait_ge(mm_gb, len(GROUPS) + (1 if g == 4 else g + 2))
                step(nc.vector.tensor_tensor(bn[:, b0:b0 + n, :], ot[:, b0:b0 + n, :],
                                             ps[[1, 2, 3, 4, 0][g]][:, 0:n * P].rearrange("p (b t) -> p b t", t=P), ALU.mult))
                if g == 4:
                    step(nc.vector.scalar_tensor_tensor(
                        ogb[:, :, 0:6], bn[:, MB, :].rearrange("p (h t) -> p h t", t=META)[:, :, META - 6:META],
                        col(V_ANORM), zs[:, :, 0:6], ALU.mult, ALU.mult))
                else:
                    for h in (2 * g, 2 * g + 1):
                        nc.vector.scalar_tensor_tensor(
                            ogb[:, h, 6:N_A].rearrange("p (c t) -> p c t", t=P), bn[:, 2 * h:2 * h + 2, :], col(V_ANORM),
                            zs[:, h, 6:N_A].rearrange("p (c t) -> p c t", t=P), ALU.mult, ALU.mult).then_inc(og_ready, 1)
            for h in range(HEADS):
                rhs_rest("gdn", h, ogb[:, h, :], N_A)

            def dve_ada(o, r):
                dve.wait_ge(ld_ada[r], (o // 2) * 16 + 16)
                dve.wait_ge(ada_done, o + 1)
                a_ = acc[:, o // KT, :] if isinstance(o, int) else acc[:, bass.ds(o // KT, 1), :].rearrange("p a n -> p (a n)")
                nc.vector.scalar_tensor_tensor(a_, ring[:, r, :], small[:, bass.ds(o + 440, 1)], a_, ALU.mult, ALU.add).then_inc(ada_done, 1)

            def dve_residual(name, n, off):
                phase = PH[name]
                per = 2 if phase.blocks == SLOT_BLOCKS else 1

                def body(t, i, blocks):
                    for s in range(0, SLOTS, per):
                        m = i * (SLOTS // per) + s // per
                        dve.wait_ge(unit_done, t * SLOTS + (s + per))
                        nc.vector.scalar_tensor_tensor(xb[:, m, 0:n], hf[:, m, off:off + n], ALPHA, ps[s][:, 0:n],
                                                       ALU.mult, ALU.add).then_inc(tiles_read, per)
                        for j in range(per):
                            split_lo(dve, t + 1, s + j, blocks)
                        if name in ADA_AT:
                            for j in range(2):
                                dve_ada(i * 4 + (ADA_AT[name] + s + j), j)
                steps(dve, phase, body)

            def dve_hidden(name, n, taps=None):
                def body(t, i, blocks):
                    for p in range(2):
                        s0, s1 = 2 * p, 2 * p + 1
                        j = i * 2 + p
                        if taps is not None:
                            c = j + CONV_AT[name]
                            dve.wait_ge(f_tap, c + 1)
                            nc.vector.scalar_tensor_tensor(tb[:, p, 0:n], ps[s0][:, 1:n + 1], col(j * 3 + (taps + 1)),
                                                           tb[:, p, 0:n], ALU.mult, ALU.add).then_inc(f_conv, 1)
                            dve.wait_ge(f_conv, c * 2 + 1)
                            nc.vector.scalar_tensor_tensor(tb[:, p, 0:n], ps[s0][:, 2:n + 2], col(j * 3 + (taps + 2)),
                                                           tb[:, p, 0:n], ALU.mult, ALU.add).then_inc(f_conv, 1)
                        split_lo(dve, t + 1, s0, blocks)
                        dve.wait_ge(f_gate, j + (GATE_AT[name] + 1))
                        dve.wait_ge(unit_done, t * SLOTS + (s1 + 1))
                        off = 0 if taps is None else 2
                        nc.vector.tensor_tensor(ab[:, p, 0:n], sb[:, p, 0:n], ps[s1][:, off:off + n], ALU.mult).then_inc(tiles_read, 2)
                        split_lo(dve, t + 1, s1, blocks)
                        if name in ADA_AT:
                            dve_ada(i * 2 + (ADA_AT[name] + p), p)
                        dve.wait_ge(hid_hi, j + (HID_AT[name] + 1))
                        nc.vector.tensor_tensor(alo[:, j, 0:n], ab[:, p, 0:n], ahi[:, j, 0:n], ALU.subtract).then_inc(hid_ready, 1)
                steps(dve, PH[name], body)

            def dve_norm(i, n, src, dst, eps, version=None):
                if i < 4:
                    dve.wait_ge(mean_mm, i + 1)
                    for m in range(KT):
                        nc.vector.tensor_tensor(xb[:, m, 0:n], xb[:, m, 0:n], ps[4][:, 0:n], ALU.subtract).then_inc(xc_ready, 1)
                dve.wait_ge(var_mm, i + 1)
                x_, r_, t_ = tb[:, 0, 0:n], ab[:, 0, 0:n], sb[:, 0, 0:n]
                step(nc.vector.tensor_scalar(x_, ps[5][:, 0:n], eps, None, ALU.add))
                rsqrt(r_, x_, n, t_)
                for m in range(KT + 1):
                    if m < KT:
                        nc.vector.tensor_tensor(xb[:, m, 0:n], src[:, m, 0:n], r_, ALU.mult).then_inc(y_ready, 1)
                    if m and version:
                        rhs_rest(version, m - 1, dst[:, m - 1, 0:n], n)

            dve.wait_ge(c_ready, 1)
            step(nc.vector.tensor_copy(small[:, 440:512].rearrange("p (n k) -> p n k", k=KT), bcast(small[:, 300:308], 9)))
            dve_residual("a_out", N_A, TOK - N_A)
            dve_norm(0, N_A, xb, hf, LN_EPS, "ln0")
            dve_hidden("up0", N_F0, V_FCONV)
            dve_residual("down0", N_F0, N_A - N_F0)
            dve_norm(1, N_F0, xb, hf, LN_EPS, "ln1")

            def b_cx(t, i, blocks):
                for p in range(2):
                    m = i * 2 + p
                    c = m + CONV_AT["b_cx"]
                    dve.wait_ge(f_tap, c + 1)
                    dve.wait_ge(unit_done, t * SLOTS + (2 * p + 2))
                    nc.vector.tensor_tensor(tb[:, p, 0:N_F0], tb[:, p, 0:N_F0], ps[2 * p + 1][:, 0:N_F0], ALU.mult).then_inc(f_conv, 1)
                    split_lo(dve, t + 1, 2 * p, blocks)
                    dve.wait_ge(f_conv, c * 2 + 1)
                    nc.vector.tensor_scalar(xb[:, m, 0:N_B], tb[:, p, 0:N_B], col(m * 3 + V_BCONV), None, ALU.mult).then_inc(b_tap, 1)
                    dve.wait_ge(b_tap, m + 1)
                    nc.vector.scalar_tensor_tensor(xb[:, m, 0:N_B], tb[:, p, 1:N_B + 1], col(m * 3 + (V_BCONV + 1)),
                                                   xb[:, m, 0:N_B], ALU.mult, ALU.add).then_inc(f_conv, 1)
                    dve.wait_ge(f_conv, c * 2 + 2)
                    nc.vector.scalar_tensor_tensor(xb[:, m, 0:N_B], tb[:, p, 2:N_B + 2], col(m * 3 + (V_BCONV + 2)),
                                                   xb[:, m, 0:N_B], ALU.mult, ALU.add).then_inc(tiles_read, 2)
                    split_lo(dve, t + 1, 2 * p + 1, blocks)
                    dve_ada(i * 2 + (ADA_AT["b_cx"] + p), p)

            def b_gate(t, i, blocks):
                for s in range(SLOTS):
                    m = i * SLOTS + s
                    dve.wait_ge(unit_done, t * SLOTS + (s + 1))
                    nc.vector.tensor_tensor(ab[:, s % 2, 0:N_B], xb[:, m, 0:N_B], ps[s][:, 2:N_F0], ALU.mult).then_inc(tiles_read, 1)
                    split_lo(dve, t + 1, s, blocks)
                    if s % 2:
                        dve_ada(i * 2 + (ADA_AT["b_gate"] + s // 2), s // 2)
                    dve.wait_ge(hid_hi, m + (HID_AT["b_gate"] + 1))
                    nc.vector.tensor_tensor(alo[:, m, 0:N_B], ab[:, s % 2, 0:N_B], ahi[:, m, 0:N_B], ALU.subtract).then_inc(hid_ready, 1)

            steps(dve, PH["b_cx"], b_cx)
            dve.wait_ge(tiles_read, SLOTS + PH["b_gate"].first)
            steps(dve, PH["b_gate"], b_gate)
            dve_residual("b_out", N_B, N_F0 - N_B)
            dve_norm(2, N_B, xb, hf, LN_EPS, "ln2")
            dve_hidden("up1", N_F1, V_FCONV + FT * 3)
            dve_residual("down1", N_F1, N_B - N_F1)
            dve_norm(3, N_F1, xb, hf, LN_EPS)

            MIX = PH["mix"]
            M0 = MIX.first // SLOTS

            def mix_splits(u, k=1):
                for v in range(u, u + k):
                    nxt = v + SLOTS
                    split_lo(dve, M0 + nxt // SLOTS, nxt % SLOTS, KT)

            R = slice(64, 96)
            dve.wait_ge(ld_rope, 16)
            ang, n_i, n_f, wrap = tb[R, 0, 0:SEQ], sb[R, 0, 0:SEQ], ab[R, 0, 0:SEQ], sb[R, 1, 0:SEQ]
            step(nc.vector.tensor_copy(ang, pos[R, :]))
            step(nc.vector.tensor_scalar(ang, ang, vec[R, V_INVF:V_INVF + 1], None, ALU.mult))
            step(nc.vector.tensor_scalar(n_i.bitcast(I32), ang, 1.0 / (2 * np.pi), None, ALU.mult))
            step(nc.vector.tensor_copy(n_f, n_i.bitcast(I32)))
            for part in TWO_PI:
                step(nc.vector.scalar_tensor_tensor(ang, n_f, -part, ang, ALU.mult, ALU.add))

            def into_range(x):
                for sign, test in ((-1.0, ALU.is_gt), (1.0, ALU.is_lt)):
                    step(nc.vector.tensor_scalar(wrap, x, -sign * float(np.pi), sign * 2 * float(np.pi), test, ALU.mult))
                    step(nc.vector.tensor_tensor(x, x, wrap, ALU.add))

            into_range(ang)
            step(nc.vector.tensor_scalar(ab[R, 1, 0:SEQ], ang, float(np.pi) / 2, None, ALU.add))
            into_range(ab[R, 1, 0:SEQ])
            step(nc.vector.tensor_scalar(ab[R, 1, 0:SEQ], ab[R, 1, 0:SEQ], PI_IN, -PI_IN, ALU.min, ALU.max))
            nc.vector.tensor_scalar(tb[R, 1, 0:SEQ], ang, PI_IN, -PI_IN, ALU.min, ALU.max).then_inc(ang_ready, 1)
            dve.wait_ge(cs_ready, 1)
            step(nc.vector.tensor_scalar(cs[R, 1, :], cs[R, 1, :], vec[R, V_SIGN:V_SIGN + 1], None, ALU.mult))

            dve.wait_ge(mods_mm, 1)
            step(nc.vector.tensor_tensor(small[:, 0:72], ps[6][:, 0:72], vec[:, V_ADAB:V_ADAB + 72], ALU.add))
            for i in range(3):
                step(nc.vector.scalar_tensor_tensor(small[:, 72 + KT * i:80 + KT * i], small[:, (3 * i + 1) * KT:(3 * i + 2) * KT], 1.0,
                                                    vec[:, V_NORM + KT * i:V_NORM + KT * (i + 1)], ALU.add, ALU.mult))
            for g in (2, 8):
                last = nc.vector.tensor_scalar(small[:, g * KT:(g + 1) * KT], small[:, g * KT:(g + 1) * KT], 0.5, None, ALU.mult)
                if g == 2:
                    mine(last)
            last.then_inc(mods_ready, 1)
            dve.wait_ge(mods_ready, 1)

            def gated_residual(t, i, blocks, per, gate):
                for s in range(0, SLOTS, per):
                    m = i * (SLOTS // per) + s // per
                    dve.wait_ge(unit_done, t * SLOTS + (s + per))
                    nc.vector.scalar_tensor_tensor(hf[:, m, 0:SEQ], ps[s][:, 0:SEQ], small[:, bass.ds(m + gate * KT, 1)],
                                                   hf[:, m, 0:SEQ], ALU.mult, ALU.add).then_inc(tiles_read, per)
                    for j in range(per):
                        split_lo(dve, t + 1, s + j, blocks)

            dve_norm(4, SEQ, hf, xb, NORM_EPS, "rms0")
            dve_hidden("up2", SEQ)
            steps(dve, PH["down2"], lambda t, i, blocks: gated_residual(t, i, blocks, 2, 2))
            dve_norm(5, SEQ, hf, xb, NORM_EPS, "rms1")

            mix_splits(0, 14)
            dve.wait_ge(lat_mm, 1)
            for f0, f1, at_ in ((0, 3, 0), (3, 5, SEQ)):
                x_, r_, t_ = tb[:, 0, 0:SEQ], ab[:, 0, 0:SEQ], sb[:, 0, 0:SEQ]
                step(nc.vector.tensor_scalar(x_, ps[4][:, at_:at_ + SEQ], 1.0 / ((f1 - f0) * P), NORM_EPS, ALU.mult, ALU.add))
                rsqrt(r_, x_, SEQ, t_)
                for j in range(f0, f1):
                    nc.vector.tensor_tensor(lat[:, j, :], lat[:, j, :], r_, ALU.mult).then_inc(lat_y, 1)
                dve.wait_ge(lat_y, f1)
            mix_splits(14, 4)
            for j in range(5):
                dve.wait_ge(lat_hi, j + 1)
                nc.vector.tensor_tensor(llo[:, j, :], lat[:, j, :], lhi[:, j, :], ALU.subtract).then_inc(lat_ready, 1)
            mix_splits(18, 8)
            for g in range(4):
                dve.wait_ge(f_hi, g + 1)
                nc.vector.tensor_tensor(flo[:, g, :], ps[g][:, 0:SEQ], fhi[:, g, :], ALU.subtract).then_inc(f_ready, 1)
            mix_splits(26, 3)
            for j in range(4):
                if j % 2 == 0:
                    dve.wait_ge(k_mm, 3 * (j // 2) + 2)
                else:
                    dve.wait_ge(unit_done, MIX.first + 30 + j // 2)
                nc.vector.tensor_copy(kt_[0:64, 2 * j:2 * j + 2, :], ps[j][0:64, :].rearrange("p (g n) -> p g n", n=SEQ)).then_inc(k_read, 1)
            mix_splits(29, 2)
            dve.wait_ge(v_read, 2)
            dve.wait_ge(q_read, 4)
            nc.vector.memset(small[:, 310:311], 0.0).then_inc(tiles_read, 6)
            mix_splits(31, 1)
            swap = [(i + 16) % 32 for i in range(32)]
            c_, s_ = cs[R, 0, :], cs[R, 1, :]

            def bc(x, n):
                return x.unsqueeze(1).to_broadcast([32, n, SEQ])

            step(nc.vector.stream_shuffle(rot[R, 0, :], krot[R, :], swap))
            mine(nc.vector.tensor_tensor(rot[R, 0, :], rot[R, 0, :], s_, ALU.mult))
            step(nc.vector.tensor_tensor(krot[R, :], krot[R, :], c_, ALU.mult))
            step(nc.vector.tensor_tensor(krot[R, :], krot[R, :], rot[R, 0, :], ALU.add))
            mine(nc.vector.tensor_copy(kt_[R, :, :], bc(krot[R, :], HEADS)))
            for h in range(0, HEADS, 4):
                q_, r_ = qt[R, h:h + 4, :], rot[R, h:h + 4, :]
                step(nc.vector.stream_shuffle(r_.rearrange("p h n -> p (h n)"), q_.rearrange("p h n -> p (h n)"), swap))
                mine(nc.vector.tensor_tensor(r_, r_, bc(s_, 4), ALU.mult))
                step(nc.vector.tensor_tensor(q_, q_, bc(c_, 4), ALU.mult))
                nc.vector.tensor_tensor(q_, q_, r_, ALU.add).then_inc(rope_ready, 1)
            for u in range(32, 36):
                dve.wait_ge(unit_done, MIX.first + u + 1)
                m = 2 * (u - 32)
                nc.vector.tensor_tensor(xb[:, m:m + 2, 0:SEQ], gates[:, m:m + 2, :], ps[u % SLOTS][:, :].rearrange("p (g n) -> p g n", n=SEQ),
                                        ALU.mult).then_inc(tiles_read, 1)
                mix_splits(u)
            for h in range(HEADS + 1):
                if h < HEADS:
                    dve.wait_ge(s_mm, h + 1)
                    step(nc.vector.reduce_max(small[:, 144 + 2 * h:146 + 2 * h], ps[4 + h % 2][:, :].rearrange("p (c n) -> p c n", n=SEQ), AX.X))
                    nc.vector.tensor_scalar(small[:, 112 + 2 * h:114 + 2 * h], small[:, 144 + 2 * h:146 + 2 * h], -SM_SCALE, None,
                                            ALU.mult).then_inc(m_ready2, 1)
                if h:
                    g = h - 1
                    dve.wait_ge(p_exp, g + 1)
                    step(nc.vector.reciprocal(small[:, 160 + 2 * g:162 + 2 * g], small[:, 128 + 2 * g:130 + 2 * g]))
                    for c in range(2):
                        last = nc.vector.tensor_scalar(pr[:, g % 2, c, :], pr[:, g % 2, c, :], small[:, 160 + 2 * g + c:161 + 2 * g + c], None, ALU.mult)
                    last.then_inc(p_ready, 1)
            for j in range(4):
                dve.wait_ge(o_hi, j + 1)
                nc.vector.tensor_tensor(olo[:, j, :], ps[j][:, 0:SEQ], ohi[:, j, :], ALU.subtract).then_inc(o_ready, 1)
            for u in range(36, 41):
                if u < 40:
                    dve.wait_ge(unit_done, MIX.first + u + 1)
                    m = 2 * (u - 36)
                    t_ = gates[:, 8 + m:10 + m, :]
                    step(nc.vector.tensor_tensor(t_, t_, ps[u % SLOTS][:, :].rearrange("p (g n) -> p g n", n=SEQ), ALU.mult))
                    nc.vector.tensor_tensor(xb[:, m:m + 2, 0:SEQ], xb[:, m:m + 2, 0:SEQ], t_, ALU.add).then_inc(tiles_read, 1)
                    mix_splits(u)
                if u > 36:
                    m = 2 * (u - 37)
                    dve.wait_ge(y_hi, u - 36)
                    nc.vector.tensor_tensor(hlo[:, m:m + 2, 0:SEQ], xb[:, m:m + 2, 0:SEQ], hhi[:, m:m + 2, 0:SEQ], ALU.subtract).then_inc(y_lo, 1)
            for i in range(2):
                gated_residual(M0 + 10 + i, i, KT, 1, 5)
            dve_norm(6, SEQ, hf, xb, NORM_EPS, "rms2")
            dve_hidden("up3", SEQ)
            steps(dve, PH["down3"], lambda t, i, blocks: gated_residual(t, i, blocks, 2, 8))
            dve_norm(7, SEQ, hf, None, NORM_EPS)

        @block.tensor
        def _(pe):
            def unit(t, s, blocks, n, rhi, rlo, out=None, first=True, last=True, k0=0, k_wait=None):
                pe.wait_ge(lo_split, t * SLOTS + (s + 1))
                if first:
                    pe.wait_ge(tiles_read, t * SLOTS + (s + 1))
                out = ps[s][:, 0:n] if out is None else out
                for k in range(blocks):
                    if k_wait is not None:
                        k_wait(k)
                    w = slice(k * P, (k + 1) * P)
                    nc.tensor.matmul(out, whi[:, s, w], rhi(k0 + k), start=first and k == 0, stop=False)
                    nc.tensor.matmul(out, whi[:, s, w], rlo(k0 + k), start=False, stop=False)
                    ins = nc.tensor.matmul(out, wlo[:, s, w], rhi(k0 + k), start=False, stop=last and k == blocks - 1)
                ins.then_inc(unit_done, 1)

            def stream(phase, n, version):
                def k_wait(k):
                    pe.wait_ge(rhs_ready, RHS_AT[version] + k + 1)
                t0 = phase.first // SLOTS
                with pe.Fori(t0, t0 + phase.units // SLOTS) as t:
                    for s in range(SLOTS):
                        unit(t, s, KT, n, lambda k: hhi[:, k, 0:n], lambda k: hlo[:, k, 0:n], k_wait=None if s else k_wait)

            pe.wait_ge(xrep_ready, 1)
            pe.wait_ge(ld_small, 32)
            pe.wait_ge(ld_cm, 16)
            for j in range(3):
                for k in range(KT):
                    lhs = xrep[:, k, :] if j == 2 else hf[:, k, META + j * P:META + (j + 1) * P]
                    last = nc.tensor.matmul(ps[7][:, 16 * j:16 * j + 16], lhs, wab[:, k, :], start=(k == 0), stop=(k == KT - 1))
            last.then_inc(mm_gate, 1)
            pe.wait_ge(gl_ready, 1)
            g_ = S_(6)
            nc.tensor.matmul(ps[7][:, 64:64 + MB], cm[:, C_CAUSAL, :], g_[:, 0:MB], start=True, stop=True)
            nc.tensor.matmul(ps[7][:, 64 + MB:64 + NBLK], cm[:, C_CAUSAL_META, :], g_[:, MB:NBLK], start=True, stop=True)
            nc.tensor.matmul(ps[7][:, 96:96 + MB], ones, g_[:, 0:MB], start=True, stop=True)
            nc.tensor.matmul(ps[7][:, 96 + MB:96 + NBLK], cm[:, C_SAME_META, :], g_[:, MB:NBLK], start=True, stop=True).then_inc(mm_cum, 1)

            stream(PH["a_in"], TOK, "x")

            k_b = lambda b: kvq[:, b * P:(b + 1) * P] if b < MB else kvqm[:, 0:P]
            v_b = lambda b: kvq[:, (MB + b) * P:(MB + b + 1) * P] if b < MB else kvqm[:, P:2 * P]
            q_b = lambda b: kvq[:, (2 * MB + b) * P:(2 * MB + b + 1) * P] if b < MB else kvqm[:, 2 * P:3 * P]

            for i, sq in enumerate((ex, ca)):
                pe.wait_ge(sq_gdn, i + 1)
                for b in range(NBLK):
                    last = nc.tensor.matmul(ps[7][:, i * NBLK + b:i * NBLK + b + 1], sq[:, b, :], ones[:, 0:1], start=True, stop=True)
            last.then_inc(mm_norm, 1)
            pe.wait_ge(tiles_read, SLOTS + 32)
            pe.wait_ge(cols_ready, 1)

            def spread(bank, b0, n, which):
                for j in range(n):
                    last = nc.tensor.matmul(ps[bank][:, j * P:(j + 1) * P], S_(which)[:, b0 + j:b0 + j + 1].to_broadcast([P, P]),
                                            ident, start=True, stop=True)
                return last

            for g, (b0, n) in enumerate(GROUPS):
                if g:
                    pe.wait_ge(d_diff, g)
                spread(0, b0, n, 7).then_inc(mm_gb, 1)
                if g:
                    pe.wait_ge(m_ready, g)
                for bank, which in ((1, 12), (2, 13), (3, 14)):
                    spread(bank, b0, n, which)
                for j in range(n):
                    b = b0 + j
                    nc.tensor.matmul(ps[4][:, j * P:(j + 1) * P], k_b(b), k_b(b), start=True, stop=True)
                    last = nc.tensor.matmul(ps[5][:, j * P:(j + 1) * P], k_b(b), q_b(b), start=True, stop=True)
                last.then_inc(mm_cb, 1)
                for kind, x_b in enumerate((k_b, v_b)):
                    if g:
                        pe.wait_ge(tr_read, 2 * (g - 1) + kind + 1)
                    for j in range(n):
                        last = nc.tensor.transpose(ps[6 + kind][:, j * P:(j + 1) * P], x_b(b0 + j), ident)
                    last.then_inc(mm_tr, 1)

            pe.wait_ge(m_ready, len(GROUPS))
            pe.wait_ge(tr_read, 2 * len(GROUPS))
            with pe.Fori(0, LEVELS) as l:
                def x_mm(g):
                    b0, n = GROUPS[g]
                    pe.wait_ge(tu_ready, l * 5 + (g + 2))
                    for j in range(n):
                        last = nc.tensor.matmul(ps[g % 2][:, j * P:(j + 1) * P], bn[:, b0 + j, :], gt[:, b0 + j, :], start=True, stop=True)
                    last.then_inc(mm_x, 1)

                def y_mm(g):
                    b0, n = GROUPS[g]
                    pe.wait_ge(x_ready, l * 5 + (g + 1))
                    for j in range(n):
                        nc.tensor.matmul(ps[2 + g % 3][:, j * P:(j + 1) * P], gu[:, b0 + j, :], ex[:, b0 + j, :], start=True, stop=True)
                    for j in range(n):
                        last = nc.tensor.matmul(ps[5 + g % 3][:, j * P:(j + 1) * P], ex[:, b0 + j, :], gu[:, b0 + j, :], start=True, stop=True)
                    last.then_inc(mm_y, 1)

                pe.wait_ge(tu_ready, l * 5 + 6)
                x_mm(0)
                x_mm(1)
                for g in range(len(GROUPS)):
                    y_mm(g)
                    if g + 2 < len(GROUPS):
                        x_mm(g + 2)

            pe.wait_ge(tu_ready, LEVELS * 5 + 6)
            nc.tensor.matmul(ps[0][:, 0:P], gu[:, MB, :], vtm[:, MB, :], start=True, stop=True).then_inc(mm_v0, 1)
            pe.wait_ge(vm_ready, 1)
            for q in range(2):
                nc.tensor.matmul(ps[1 + q][:, :], ktm[:, MB, :], rr[:, 4 * q:4 * q + 4, :], start=True, stop=True).then_inc(mm_s0, 1)
            pe.wait_ge(v0_read, 1)
            nc.tensor.matmul(ps[3][:, 0:P], vn[:, 7, :], ca[:, MB, :], start=True, stop=True).then_inc(mm_o0, 1)
            for c in range(2):
                for q in range(2):
                    pe.wait_ge(s_ready, 2 * c + q + 1)
                    if c == 0 and q == 0:
                        pe.wait_ge(v0_read, 1)
                    for j in range(4):
                        h = 4 * q + j
                        last = nc.tensor.matmul(ps[q][:, j * P:(j + 1) * P], k_b(2 * h + c), st[:, h, :], start=True, stop=True)
                    last.then_inc(mm_ks, 1)
                for q in range(2):
                    pe.wait_ge(r_ready, 2 * c + q + 1)
                    if c == 0 and q == 1:
                        pe.wait_ge(o_read, 1)
                    for j in range(4):
                        h = 4 * q + j
                        last = nc.tensor.matmul(ps[2 + q][:, j * P:(j + 1) * P], gu[:, 2 * h + c, :], rr[:, h, :], start=True, stop=True)
                    last.then_inc(mm_vn, 1)
                for q in range(2):
                    pe.wait_ge(vn_ready, 2 * c + q + 1)
                    if c:
                        pe.wait_ge(o_read, 1 + q + 1)
                    for j in range(4):
                        h = 4 * q + j
                        if c == 0:
                            last = nc.tensor.matmul(ps[4 + q][:, j * P:(j + 1) * P], ktm[:, 2 * h, :], vn[:, h, :], start=True, stop=True)
                    if c == 0:
                        last.then_inc(mm_ds, 1)
                    for j in range(4):
                        h = 4 * q + j
                        nc.tensor.matmul(ps[6 + q][:, j * P:(j + 1) * P], st[:, h, :], q_b(2 * h + c), start=True, stop=False)
                        last = nc.tensor.matmul(ps[6 + q][:, j * P:(j + 1) * P], vn[:, h, :], ca[:, 2 * h + c, :], start=False, stop=True)
                    last.then_inc(mm_o, 1)

            pe.wait_ge(sq_gdn, 3)
            for b in range(NBLK):
                last = nc.tensor.matmul(ps[7][:, b:b + 1], ex[:, b, :], ones[:, 0:1], start=True, stop=True)
            last.then_inc(mm_norm, 1)
            pe.wait_ge(cols_ready, 2)
            for g in (4, 0, 1, 2, 3):
                spread([1, 2, 3, 4, 0][g], *GROUPS[g], 12).then_inc(mm_gb, 1)

            def down(name, n):
                t0 = PH[name].first // SLOTS

                def wait_for(h0, upto):
                    def k_wait(k):
                        if h0 + k in upto:
                            pe.wait_ge(hid_ready, HID_AT[name.replace("down", "up")] + h0 + k + 1)
                    return k_wait

                with pe.Fori(t0, t0 + PH[name].units // SLOTS) as t:
                    for s in range(SLOTS):
                        h0 = SLOT_BLOCKS * (s % 2)
                        unit(t, s, SLOT_BLOCKS, n, lambda k: ahi[:, k, 0:n], lambda k: alo[:, k, 0:n], out=ps[s - s % 2][:, 0:n],
                             first=s % 2 == 0, last=s % 2 == 1, k0=h0,
                             k_wait=wait_for(h0, range(FT)) if s < 2 else None)

            def pe_norm(i, n, name=None):
                if i < 4:
                    phase = PH[name]
                    per = 2 if phase.blocks == SLOT_BLOCKS else 1
                    for m in range(KT):
                        pe.wait_ge(tiles_read, SLOTS + phase.first + (m + 1) * per)
                        last = nc.tensor.matmul(ps[4][:, 0:n], cm[:, C_MEAN, :], xb[:, m, 0:n], start=m == 0, stop=m == KT - 1)
                    last.then_inc(mean_mm, 1)
                for m in range(KT):
                    pe.wait_ge(sq_ready, i * KT + m + 1)
                    last = nc.tensor.matmul(ps[5][:, 0:n], cm[:, C_MEAN, :], sqb[:, m, 0:n], start=m == 0, stop=m == KT - 1)
                last.then_inc(var_mm, 1)

            stream(PH["a_out"], N_A, "gdn")
            pe_norm(0, N_A, "a_out")
            stream(PH["up0"], N_A, "ln0")
            down("down0", N_F0)
            pe_norm(1, N_F0, "down0")
            stream(PH["b_cx"], N_F0, "ln1")
            stream(PH["b_gate"], N_F0, "ln1")
            t0 = PH["b_out"].first // SLOTS
            with pe.Fori(t0, t0 + 2) as t:
                for s in range(SLOTS):
                    unit(t, s, KT, N_B, lambda k: ahi[:, k, 0:N_B], lambda k: alo[:, k, 0:N_B],
                         k_wait=None if s else lambda k: pe.wait_ge(hid_ready, HID_AT["b_gate"] + k + 1))
            pe_norm(2, N_B, "b_out")
            stream(PH["up1"], N_B, "ln2")
            down("down1", N_F1)
            pe_norm(3, N_F1, "down1")

            MIX = PH["mix"]
            M0 = MIX.first // SLOTS
            pe.wait_ge(ada_done, ADA_OPS + 1)
            for i in range(9):
                for m in range(KT):
                    last = nc.tensor.matmul(ps[6][:, KT * i + m:KT * i + m + 1], acc[:, i, m * P:(m + 1) * P], ones[:, 0:1], start=True, stop=True)
            last.then_inc(mods_mm, 1)
            pe_norm(4, SEQ)
            stream(PH["up2"], SEQ, "rms0")
            down("down2", SEQ)
            pe_norm(5, SEQ)

            def mix_tile(u, version):
                def k_wait(k):
                    if version:
                        pe.wait_ge(rhs_ready, RHS_AT[version] + k + 1)
                    elif k % 2 == 0:
                        pe.wait_ge(y_lo, k // 2 + 1)
                unit(M0 + u // SLOTS, u % SLOTS, KT, SEQ, lambda k: hhi[:, k, 0:SEQ], lambda k: hlo[:, k, 0:SEQ],
                     k_wait=k_wait if u in (0, 40) else None)

            def mix_blocks(u, place, banks_free=None):
                s = u % SLOTS
                pe.wait_ge(lo_split, MIX.first + u + 1)
                if banks_free:
                    banks_free()
                for k in range(KT):
                    out, r_hi, r_lo, m, first, last, done = place(k)
                    w = slice(k * P, k * P + m)
                    nc.tensor.matmul(out, whi[:, s, w], r_hi, start=first, stop=False)
                    nc.tensor.matmul(out, whi[:, s, w], r_lo, start=False, stop=False)
                    ins = nc.tensor.matmul(out, wlo[:, s, w], r_hi, start=False, stop=last)
                    if done is not None and k < KT - 1:
                        ins.then_inc(done, 1)
                ins.then_inc(unit_done, 1)

            for u in range(26):
                if u == 14:
                    for j in range(5):
                        pe.wait_ge(ls_sq, j + 1)
                        at_ = 0 if j < 3 else SEQ
                        last = nc.tensor.matmul(ps[4][:, at_:at_ + SEQ], ones, lsq[:, j, :], start=j in (0, 3), stop=j in (2, 4))
                    last.then_inc(lat_mm, 1)
                mix_tile(u, "rms1")

            pe.wait_ge(ld_dft, 16)
            pe.wait_ge(tiles_read, SLOTS + MIX.first + 10)
            for j in range(4):
                for g in (2 * (j % 2), 2 * (j % 2) + 1):
                    if j == 0 and g == 0:
                        pe.wait_ge(lat_y, 5)
                    last = nc.tensor.matmul(ps[4 + j][:, (g % 2) * SEQ:(g % 2 + 1) * SEQ], uf[:, g, (j // 2) * P:(j // 2 + 1) * P], dft[:, 0, :], start=True, stop=True)
                last.then_inc(four1, 1)
            pe.wait_ge(tiles_read, SLOTS + MIX.first + 26)
            pe.wait_ge(pf_ready, 4)
            for g in range(4):
                for c in range(2):
                    nc.tensor.matmul(ps[g][:, 0:SEQ], pf[:, c, g, 0:P], dft[:, 1 + c, :], start=c == 0, stop=False)
                    last = nc.tensor.matmul(ps[g][:, 0:SEQ], pf[:, c, g, P:2 * P], dft[:, 3 + c, :], start=False, stop=c == 1)
                last.then_inc(four2, 1)

            pe.wait_ge(lat_ready, 5)

            def q_place(u):
                def place(k):
                    b = (u - 26) * KT + k
                    h, kt = b // 3, b % 3
                    return (ps[4 + h // 2][0:96, (h % 2) * SEQ:(h % 2 + 1) * SEQ], lhi[:, kt, :], llo[:, kt, :], 96, kt == 0, kt == 2, q_mm if kt == 2 else None)
                return place

            def k_place(u):
                def place(k):
                    b = (u - 29) * KT + k
                    h, kt = b // 2, b % 2
                    return (ps[h // 2][:, (h % 2) * SEQ:(h % 2 + 1) * SEQ], lhi[:, 3 + kt, :], llo[:, 3 + kt, :], P, kt == 0, kt == 1, k_mm if kt == 1 else None)
                return place

            for u in range(26, 29):
                mix_blocks(u, q_place(u))
            for u in range(29, 31):
                mix_blocks(u, k_place(u), lambda: pe.wait_ge(f_ready, 4))
            pe.wait_ge(lo_split, MIX.first + 32)
            s = 31 % SLOTS
            for c in range(2):
                pe.wait_ge(q_read, c + 1)
                out = ps[4 + c][:, :]
                cc = slice(c * P, (c + 1) * P)
                for kt in range(2):
                    w = slice(kt * 512, (kt + 1) * 512)
                    nc.tensor.matmul(out, lhi[:, 3 + kt, cc], whi[:, s, w], start=kt == 0, stop=False)
                    nc.tensor.matmul(out, llo[:, 3 + kt, cc], whi[:, s, w], start=False, stop=False)
                    last = nc.tensor.matmul(out, lhi[:, 3 + kt, cc], wlo[:, s, w], start=False, stop=kt == 1)
                if c == 0:
                    last.then_inc(v_mm, 1)
            last.then_inc(unit_done, 1)

            def out_place(u, r_hi, r_lo):
                def place(k):
                    kt = k % 4
                    return (ps[u % SLOTS][:, (k // 4) * SEQ:(k // 4 + 1) * SEQ], r_hi[:, kt, :], r_lo[:, kt, :], P, kt == 0, kt == 3, None)
                return place

            pe.wait_ge(k_read, 4)
            for u in range(32, 36):
                mix_blocks(u, out_place(u, fhi, flo), lambda: pe.wait_ge(tiles_read, SLOTS + MIX.first + 32))

            pe.wait_ge(v_read, 2)
            pe.wait_ge(tiles_read, SLOTS + MIX.first + 36)
            for h in range(HEADS + 2):
                if h < HEADS:
                    pe.wait_ge(rope_ready, h // 4 + 1)
                    if h >= 2:
                        pe.wait_ge(p_exp, h - 1)
                    for c in range(2):
                        last = nc.tensor.matmul(ps[4 + h % 2][:, c * SEQ:(c + 1) * SEQ], qt[0:96, h, c * P:(c + 1) * P], kt_[0:96, h, :], start=True, stop=True)
                    last.then_inc(s_mm, 1)
                if 0 <= h - 1 < HEADS:
                    g = h - 1
                    pe.wait_ge(p_ready, g + 1)
                    if g >= 2:
                        pe.wait_ge(t_read, g - 1)
                    for kc in range(2):
                        for c in range(2):
                            last = nc.tensor.transpose(ps[6 + g % 2][:, kc * SEQ + c * P:kc * SEQ + (c + 1) * P], pr[:, g % 2, c, kc * P:(kc + 1) * P], ident)
                    last.then_inc(t_mm, 1)
                if h >= 2:
                    g = h - 2
                    pe.wait_ge(t_read, g + 1)
                    half = (g % 2) * 64
                    for kc in range(2):
                        last = nc.tensor.matmul(ps[g // 2][half:half + 64, 0:SEQ], vt[:, kc, g * 64:(g + 1) * 64], pt[:, g % 2, kc, :], start=kc == 0, stop=kc == 1)
                    last.then_inc(o_mm, 1)
            pe.wait_ge(o_ready, 4)
            for u in range(36, 40):
                mix_blocks(u, out_place(u, ohi, olo))
            for u in range(40, 48):
                mix_tile(u, None)
            pe_norm(6, SEQ)
            stream(PH["up3"], SEQ, "rms2")
            down("down3", SEQ)
            pe_norm(7, SEQ)


def constants():
    i, j = np.arange(P)[:, None], np.arange(P)[None, :]
    same = i // META == j // META
    out = [i == j, np.full((P, P), 1.0 / D), np.ones((P, P)), i <= j, same & (i <= j), same]
    for l in range(LEVELS):
        out.append(-1.0 * ((i >> (l + 1) == j >> (l + 1)) & (i >> l & 1 == 1) & (j >> l & 1 == 0)))
    return np.ascontiguousarray(np.stack(out, 1).astype(np.float32))


def blocks_of(w):
    k, n = w.shape
    return w.reshape(k // P, P, n // P, P).transpose(2, 1, 0, 3).reshape(n // P, P, k)


def pairs_of(a, b):
    return np.stack([blocks_of(a), blocks_of(b)], 1).reshape(-1, P, a.shape[0])


def halves_of(w):
    n = w.shape[1] // P
    return blocks_of(w).reshape(n, P, 2, SLOT_BLOCKS * P).transpose(0, 2, 1, 3).reshape(2 * n, P, SLOT_BLOCKS * P)


def lay_out(a):
    f = {}
    x = np.concatenate([a["meta"], a["x"][0]], 0)
    f["x"] = x.T.reshape(KT, P, TOK).transpose(1, 0, 2)
    w = a["a_w_in"][0]
    q, k, v, z, ba = (w[:, 0:1024], w[:, 1024:2048], w[:, 2048:3072], w[:, 3072:4096], w[:, 4096:])
    f["w_a_in"] = np.concatenate([blocks_of(m) for m in (k, v, q, z)])
    f["w_ab"] = ba.reshape(KT, P, 16).transpose(1, 0, 2)
    f["w_a_out"] = blocks_of(a["a_w_out"][0])
    b, c, xv = np.split(a["b_w_in"][0], 3, axis=1)
    f["w_b_cx"] = pairs_of(c, xv)
    f["w_b_gate"] = blocks_of(b)
    f["w_b_out"] = blocks_of(a["b_w_out"][0])
    for l in range(2):
        u, g = np.split(a["ffn_w_up"][l], 2, axis=1)
        f[f"w_up{l}"] = pairs_of(u, g)
        f[f"w_down{l}"] = halves_of(a["ffn_w_down"][l])
    for l, n in ((2, "ffn1"), (3, "ffn2")):
        f[f"w_up{l}"] = pairs_of(a[n + "_w_gate_2"][0], a[n + "_w_up_2"][0])
        f[f"w_down{l}"] = halves_of(a[n + "_w_down_2"][0])
    f["ada_w"] = a["ada_w_2"][0].reshape(KT, P, 9, D).transpose(2, 0, 1, 3).reshape(ADA_OPS, P, D)

    vec = np.zeros((P, N_VEC), np.float32)
    conv = a["a_conv"][0]
    kvq = np.concatenate([conv[:, 1024:3072], conv[:, 0:1024]], 1)
    vec[:, V_ACONV:V_ACONV + 96] = kvq.reshape(4, 24, P).transpose(2, 1, 0).reshape(P, 96)
    vec[:, V_FCONV:V_FCONV + 132] = a["ffn_conv"].reshape(2, 3, FT, P).transpose(3, 0, 2, 1).reshape(P, 132)
    vec[:, V_BCONV:V_BCONV + 24] = a["b_conv"][0].reshape(3, KT, P).transpose(2, 1, 0).reshape(P, 24)
    ln = np.stack([a["ln_mix_g"], a["ln_mix_b"], a["ln_ffn_g"], a["ln_ffn_b"]], 1)
    vec[:, V_LN:V_LN + 64] = ln.reshape(8 * KT, P).T
    vec[:, V_ANORM] = a["a_norm"][0]
    rows = np.arange(P) // META
    for at_, v_ in ((V_ALOG, a["a_log"][0]), (V_DT, a["a_dt_bias"][0])):
        vec[:, at_:at_ + MB] = np.repeat(v_, 2)[None]
        vec[:, at_ + MB] = v_[rows]
    vec[:, V_HEAD:V_HEAD + HEADS] = rows[:, None] == np.arange(HEADS)[None]
    vec[:, V_C:V_C + KT] = a["c_2"].reshape(KT, P).T
    vec[:, V_ADAB:V_ADAB + 72] = a["ada_b_2"][0].reshape(72, P).T
    norms = np.stack([a["ffn1_norm_2"][0], a["mix_norm_2"][0], a["ffn2_norm_2"][0], a["final_norm_2"]])
    vec[:, V_NORM:V_NORM + 32] = norms.reshape(32, P).T
    vec[:, V_QN:V_QN + 3] = a["q_norm_2"][0].reshape(3, P).T
    vec[:, V_KVN:V_KVN + 2] = a["kv_norm_2"][0].reshape(2, P).T
    f["vec"] = vec
    f["cm"] = constants()
    mixing_layout(a, f)
    return {k_: np.ascontiguousarray(v_) for k_, v_ in f.items()}


def mixing_layout(a, f):
    w = a["w_in_2"][0]
    u_f, q_lat, kv_lat, k_rope, gate = np.split(w, [512, 896, 1152, 1184], axis=1)
    rope = np.zeros((D, P), np.float32)
    rope[:, 64:96] = k_rope
    q_up = a["w_q_up_2"][0].reshape(3, P, HEADS, 96)
    q_blk = np.zeros((HEADS, 3, P, P), np.float32)
    q_blk[..., 0:96] = q_up.transpose(2, 0, 1, 3)
    kv = a["w_kv_up_2"][0].reshape(2, P, HEADS, P)
    k_blk = kv.transpose(2, 0, 1, 3)
    v_blk = kv[..., 64:].reshape(2, P, 4, P).transpose(0, 2, 1, 3)

    def units(blk):
        return blk.reshape(-1, KT, P, P).transpose(0, 2, 1, 3).reshape(-1, P, KT * P)

    def out_blocks(m):
        return m.reshape(4, P, KT, P).transpose(2, 0, 1, 3)

    f["w_mix"] = np.concatenate([
        blocks_of(rope), blocks_of(q_lat), blocks_of(kv_lat), blocks_of(u_f), blocks_of(gate),
        units(q_blk), units(k_blk), units(v_blk),
        units(out_blocks(a["w_fourier_out_2"][0])), units(out_blocks(a["w_mla_out_2"][0])),
        blocks_of(a["w_out_2"][0]),
    ])
    f["pos"] = np.tile(a["positions_2"].astype(np.int32), (32, 1))
    d, s = np.arange(P), np.arange(SEQ)
    fd = 2 * np.pi * (d[:, None] * d[None] % P) / P
    fs = 2 * np.pi * (s[:, None] * s[None] % SEQ) / SEQ
    f["dft"] = np.stack([
        np.concatenate([np.cos(fd), np.sin(fd)], 1) / np.sqrt(P),
        *(np.cos(fs) / np.sqrt(SEQ)).reshape(2, P, SEQ), *(-np.sin(fs) / np.sqrt(SEQ)).reshape(2, P, SEQ),
    ], 1).astype(np.float32)
    inv = 1.0 / (np.float32(10000.0) ** (np.arange(16, dtype=np.float32) * np.float32(2.0) / np.float32(32)))
    f["vec"][64:96, V_INVF] = np.tile(inv.astype(np.float32), 2)
    f["vec"][64:80, V_SIGN] = -1.0
    f["vec"][80:96, V_SIGN] = 1.0
    f["vec"][:, V_QN:V_QN + 3] = a["q_norm_2"][0].reshape(3, P).T
    f["vec"][:, V_KVN:V_KVN + 2] = a["kv_norm_2"][0].reshape(2, P).T


def kernel(**inputs):
    import concourse.bacc as bacc
    from concourse.bass_utils import run_bass_kernel_spmd

    arrays = lay_out({k: np.asarray(v) for k, v in inputs.items()})
    nc = bacc.Bacc("TRN2", target_bir_lowering=False, num_devices=1)
    io = {n: nc.dram_tensor("in_" + n, v.shape, mybir.dt.from_np(v.dtype), kind="ExternalInput").ap() for n, v in arrays.items()}
    io["out"] = nc.dram_tensor("out", (P, KT, SEQ), F32, kind="ExternalOutput").ap()
    build(nc, io)
    r = run_bass_kernel_spmd(nc, [{"in_" + n: v for n, v in arrays.items()}], core_ids=[0])
    out = r.results[0]["out"]
    return np.ascontiguousarray(out.transpose(2, 1, 0)).reshape(1, SEQ, D)
```

```python
from contextlib import ExitStack

import numpy as np

import concourse.bass as bass
from concourse import mybir

F32 = mybir.dt.float32
F32R = mybir.dt.float32r
I32 = mybir.dt.int32
ALU = mybir.AluOpType
ACT = mybir.ActivationFunctionType
AX = mybir.AxisListType

P = 128
D = 1024
KT = D // P
SEQ = 256
META = 16
TOK = SEQ + META
D_FF = 2816
FT = D_FF // P
HEADS = 8
NBLK = 2 * HEADS + 1
MB = NBLK - 1
GROUPS = [(0, 4), (4, 4), (8, 4), (12, 4), (16, 1)]
ALPHA = (2.0 * 2) ** 0.25
LN_EPS, RMS_EPS, L2_EPS, NORM_EPS = 1e-5, 1e-6, 1e-6, 1e-6
SM_SCALE = 96 ** -0.5
PI_IN = float(np.nextafter(np.float32(np.pi), np.float32(0)))
TWO_PI = (6.28125, 0.0019350051879882812, 3.019916050e-7)
LEVELS = 7

N_A = 262
N_F0 = 260
N_B = 258
N_F1 = 256

SLOTS = 4
SLOT_BLOCKS = FT // 2

U_V, U_Z = 2 * KT, 3 * KT
U_TWO, U_THIRD = (U_V, U_V + 1), U_V + 2


class Phase:

    def __init__(self, name, first, units, blocks):
        self.name, self.first, self.units, self.blocks = name, first, units, blocks


def plan():
    first, out = 0, []
    for name, units, blocks in [
        ("a_in", 32, KT), ("a_out", 8, KT), ("up0", 2 * FT, KT), ("down0", 16, SLOT_BLOCKS),
        ("b_cx", 16, KT), ("b_gate", 8, KT), ("b_out", 8, KT), ("up1", 2 * FT, KT), ("down1", 16, SLOT_BLOCKS),
        ("up2", 2 * FT, KT), ("down2", 16, SLOT_BLOCKS), ("mix", 48, KT),
        ("up3", 2 * FT, KT), ("down3", 16, SLOT_BLOCKS),
    ]:
        out.append(Phase(name, first, units, blocks))
        first += units
    return out


PHASES = plan()
PH = {p.name: p for p in PHASES}
UNITS = PHASES[-1].first + PHASES[-1].units
BLOCKS_AFTER = {p.name: q.blocks for p, q in zip(PHASES, PHASES[1:])}
ADA_OPS = 9 * KT
ADA_AT = {"up0": 0, "down0": FT, "b_cx": FT + 16, "b_gate": FT + 24, "up1": FT + 28}
CONV_AT = {"up0": 0, "b_cx": FT, "up1": FT + KT}
GATE_AT = {"up0": 0, "up1": FT, "up2": 2 * FT, "up3": 3 * FT}
HID_AT = {"up0": 0, "b_gate": FT, "up1": FT + KT, "up2": 2 * FT + KT, "up3": 3 * FT + KT}
SUMS_AT = {0: 0, 1: 8, 2: 16, 3: 24, 5: 32, 7: 40}
RHS_AT = {"x": 0, "gdn": 8, "ln0": 16, "ln1": 24, "ln2": 32, "rms0": 40, "rms1": 48, "rms2": 56}

C_IDENT, C_MEAN, C_ONES, C_CAUSAL, C_CAUSAL_META, C_SAME_META, C_LEVEL = range(7)
C_PAIR = C_LEVEL
N_CONST = C_LEVEL + LEVELS

_at = 0


def _place(n):
    global _at
    _at += n
    return _at - n


V_ACONV = _place(24 * 4)
V_FCONV = _place(2 * FT * 3)
V_BCONV = _place(KT * 3)
V_LN = _place(8 * KT)
V_ANORM = _place(1)
V_ALOG = _place(NBLK)
V_DT = _place(NBLK)
V_HEAD = _place(HEADS)
V_C = _place(KT)
V_ADAB = _place(9 * KT)
V_NORM = _place(4 * KT)
V_QN = _place(3)
V_KVN = _place(2)
V_INVF = _place(1)
V_SIGN = _place(1)
N_VEC = _at


def build(nc, io):
    ctx = ExitStack()
    with ctx:
        sem = lambda name: ctx.enter_context(nc.semaphore(name))

        base = (nc.sbuf_base + 63) // 32 * 32
        spot = [base]

        def at(name, shape, dt, offset):
            return nc.alloc_sbuf_tensor_at(name, shape, dt, offset=offset)

        def new(name, shape, dt=F32):
            size = int(np.prod(shape[1:])) * 4
            spot[0] += (size + 31) // 32 * 32
            return at(name, shape, dt, spot[0] - (size + 31) // 32 * 32)

        raw = new("raw", [P, SLOTS, SLOT_BLOCKS * P])
        whi = new("whi", [P, SLOTS, SLOT_BLOCKS * P], F32R)
        wlo = new("wlo", [P, SLOTS, SLOT_BLOCKS * P], F32R)
        hf = new("hf", [P, KT, TOK])
        xb_at = spot[0]
        xb = new("xb", [P, KT, TOK])
        hhi_at = spot[0]
        hhi = new("hhi", [P, KT, TOK], F32R)
        hlo_at = spot[0]
        hlo = new("hlo", [P, KT, TOK], F32R)
        sqb = at("sqb", [P, KT, TOK], F32, hlo_at)
        arena = spot[0]
        ahi = new("ahi", [P, FT, N_F0], F32R)
        alo = new("alo", [P, FT, N_F0], F32R)
        acc = new("acc", [P, 9, D])
        ring_at = spot[0]
        ring = new("ring", [P, 2, D])
        tb = new("tb", [P, 2, TOK])
        ab = new("ab", [P, 2, TOK])
        sb = new("sb", [P, 2, TOK])
        cm = new("cm", [P, N_CONST, P])
        vec = new("vec", [P, N_VEC])
        small = new("small", [P, 512])
        small_end = spot[0]
        spot[0] += 2 * SEQ * 4
        assert spot[0] <= nc.sbuf_usable_end, spot[0]

        spot[0] = arena
        kvq = new("kvq", [P, 24 * 2 * P])
        kvqm = new("kvqm", [P, 24 * META])
        zs = new("zs", [P, HEADS, N_A])
        gt = new("gt", [P, NBLK, P])
        bn = new("bn", [P, NBLK, P])
        ex = new("ex", [P, NBLK, P])
        ca = new("ca", [P, NBLK, P])
        gu = new("gu", [P, NBLK, P])
        st = new("st", [P, HEADS, P])
        assert spot[0] <= ring_at
        ktm = at("ktm", [P, NBLK, P], F32, xb_at)
        ot = gt
        rr = at("rr", [P, HEADS, P], F32, ring_at)
        vn = at("vn", [P, HEADS, P], F32, ring_at + HEADS * P * 4)
        wab = at("wab", [P, KT, 2 * HEADS], F32, ring_at)
        xrep = at("xrep", [P, KT, P], F32, ring_at + 1024)

        spot[0] = arena
        krot = new("krot", [P, SEQ])
        lat = new("lat", [P, 5, SEQ])
        uf = new("uf", [P, 4, SEQ])
        dft = new("dft", [P, 5, SEQ])
        gates = new("gates", [P, 16, SEQ])
        lhi = new("lhi", [P, 5, SEQ], F32R)
        llo = new("llo", [P, 5, SEQ], F32R)
        qt = new("qt", [P, HEADS, SEQ])
        kt_ = new("kt", [P, HEADS, SEQ])
        vt = new("vt", [P, 2, 512])
        pf_at = spot[0]
        pf = new("pf", [P, 2, 4, SEQ])
        rot = at("rot", [P, HEADS, SEQ], F32, pf_at)
        lsq = at("lsq", [P, 5, SEQ], F32, spot[0])
        fhi = new("fhi", [P, 4, SEQ], F32R)
        flo = new("flo", [P, 4, SEQ], F32R)
        assert spot[0] <= ring_at, (spot[0], ring_at)
        spot[0] = arena + SEQ * 4
        ohi = new("ohi", [P, 4, SEQ], F32R)
        olo = new("olo", [P, 4, SEQ], F32R)
        pr = at("pr", [P, 2, 2, SEQ], F32, ring_at)
        pt = at("pt", [P, 2, 2, SEQ], F32, ring_at + 4 * SEQ * 4)
        outb = at("outb", [P, KT, SEQ], F32, arena)
        cs = at("cs", [P, 2, SEQ], F32, small_end)
        pos = at("pos", [P, SEQ], I32, small_end)

        ps = [ctx.enter_context(nc.psum_tensor(f"ps{i}", [P, 512], F32)) for i in range(8)]

        raw_loaded = [sem(f"raw_loaded{s}") for s in range(SLOTS)]
        hi_split = sem("hi_split")
        lo_split = sem("lo_split")
        unit_done = sem("unit_done")
        tiles_read = sem("tiles_read")
        ld_x, ld_small, ld_cm, ld_ada = sem("ld_x"), sem("ld_small"), sem("ld_cm"), [sem("ld_ada0"), sem("ld_ada1")]
        ada_done = sem("ada_done")
        rhs_hi, rhs_ready = sem("rhs_hi"), sem("rhs_ready")
        a_tap, a_conv, a_act = sem("a_tap"), sem("a_conv"), sem("a_act")
        f_tap, f_conv, f_gate, hid_hi, hid_ready = sem("f_tap"), sem("f_conv"), sem("f_gate"), sem("hid_hi"), sem("hid_ready")
        mean_mm, xc_ready, sq_ready, var_mm, y_ready, hf_ready = (sem(n) for n in ("mean_mm", "xc_ready", "sq_ready", "var_mm", "y_ready", "hf_ready"))
        sum_ready, guess_ready, eps_ready = sem("sum_ready"), sem("guess_ready"), sem("eps_ready")
        dve_step, act_step = sem("dve_step"), sem("act_step")
        out_done = sem("out_done")

        sums = sb[:, 1, :]
        ident = cm[:, C_IDENT, :]
        ones = cm[:, C_ONES, :]

        def v1(i):
            return vec[:, i:i + 1] if isinstance(i, int) else vec[:, bass.ds(i, 1)]

        xrep_ready, mm_gate, g_dve, g_act, gl_ready, mm_cum = (sem(n) for n in ("xrep_ready", "mm_gate", "g_dve", "g_act", "gl_ready", "mm_cum"))
        sq_gdn, mm_norm, cols_ready, d_diff, d_exp, m_ready = (sem(n) for n in ("sq_gdn", "mm_norm", "cols_ready", "d_diff", "d_exp", "m_ready"))
        mm_gb, mm_cb, mm_tr, tr_read, mm_x, x_ready, mm_y, tu_ready, gu0_ready, mm_t0 = (sem(n) for n in ("mm_gb", "mm_cb", "mm_tr", "tr_read", "mm_x", "x_ready", "mm_y", "tu_ready", "gu0_ready", "mm_t0"))
        mm_v0, v0_read, vm_ready, mm_s0, mm_o0, s_ready = (sem(n) for n in ("mm_v0", "v0_read", "vm_ready", "mm_s0", "mm_o0", "s_ready"))
        mm_ks, r_ready, mm_vn, vn_ready, mm_ds, mm_o, o_read, og_ready = (sem(n) for n in ("mm_ks", "r_ready", "mm_vn", "vn_ready", "mm_ds", "mm_o", "o_read", "og_ready"))
        mods_mm, mods_ready, ls_sq, lat_mm, lat_y, lat_f, lat_hi, lat_ready = (sem(n) for n in ("mods_mm", "mods_ready", "ls_sq", "lat_mm", "lat_y", "lat_f", "lat_hi", "lat_ready"))
        four1, pf_ready, four2, f_hi, f_ready = (sem(n) for n in ("four1", "pf_ready", "four2", "f_hi", "f_ready"))
        q_mm, q_read, k_mm, k_read, v_mm, v_read = (sem(n) for n in ("q_mm", "q_read", "k_mm", "k_read", "v_mm", "v_read"))
        rope_ready, s_mm, m_ready2, p_exp, p_ready, t_mm, t_read, o_mm, o_hi, o_ready = (sem(n) for n in ("rope_ready", "s_mm", "m_ready2", "p_exp", "p_ready", "t_mm", "t_read", "o_mm", "o_hi", "o_ready"))
        ld_rope, ld_dft, ang_ready, cs_ready, y_hi, y_lo = (sem(n) for n in ("ld_rope", "ld_dft", "ang_ready", "cs_ready", "y_hi", "y_lo"))
        c_ready, b_tap = sem("c_ready"), sem("b_tap")
        ogb = at("ogb", [P, HEADS, N_A], F32, arena)

        def col(i):
            return vec[:, bass.ds(i, 1)]

        def eps_of(eps):
            c = 316 + (eps == RMS_EPS)
            return small[:, c:c + 1]

        def ln_shift(i):
            return lambda m: col(V_LN + (2 * i + 1) * KT + m)

        def ln_gain(i):
            return lambda m: col(V_LN + 2 * i * KT + m)

        def a_of(i):
            return lambda m: small[:, 72 + KT * i + m:73 + KT * i + m]

        def sh_of(i):
            return lambda m: small[:, 3 * KT * i + m:3 * KT * i + m + 1]

        def blocks_at(kind, b0, n):
            at_ = kind * MB * P + b0 * P
            return kvq[:, at_:at_ + n * P] if b0 < MB else kvqm[:, kind * P:(kind + 1) * P]

        def S_(i):
            return small[:, i * NBLK:(i + 1) * NBLK]


        def split_hi(act, t, s, blocks):
            if not blocks:
                return
            act.wait_ge(raw_loaded[s], t * 16 + 16)
            if not isinstance(t, int) or t:
                act.wait_ge(unit_done, t * SLOTS + (s + 1 - SLOTS))
            nc.scalar.activation(whi[:, s, 0:blocks * P], raw[:, s, 0:blocks * P], ACT.Copy).then_inc(hi_split, 1)

        def split_lo(dve, t, s, blocks):
            if not blocks:
                return
            dve.wait_ge(hi_split, t * SLOTS + (s + 1))
            nc.vector.tensor_tensor(wlo[:, s, 0:blocks * P], raw[:, s, 0:blocks * P],
                                    whi[:, s, 0:blocks * P], ALU.subtract).then_inc(lo_split, 1)

        def steps(eng, phase, body):
            t0, n = phase.first // SLOTS, phase.units // SLOTS
            after = BLOCKS_AFTER.get(phase.name, 0)
            whole = n if after == phase.blocks else n - 1
            with eng.Fori(0, whole) as i:
                body(i + t0, i, phase.blocks)
            if whole < n:
                body(n - 1 + t0, n - 1, after)

        def bcast(row, n):
            return row.unsqueeze(1).to_broadcast([P, n, row.shape[-1]])

        class Steps:

            def __init__(self, eng, s):
                self.eng, self.s, self.n = eng, s, 0

            def __call__(self, instruction):
                instruction.then_inc(self.s, 1)
                self.n += 1
                return self.n

            def after(self, n=None):
                self.eng.wait_ge(self.s, self.n if n is None else n)


        block = ctx.enter_context(nc.Block())

        @block.sync
        def _(sp):
            for k in range(KT):
                sp.dma_start(hf[:, k, :], io["x"][:, k, :]).then_inc(ld_x, 16)
            sp.dma_start(wab[:], io["w_ab"]).then_inc(ld_small, 16)
            sp.dma_start(vec[:], io["vec"]).then_inc(ld_small, 16)
            sp.dma_start(pos[64:96, :], io["pos"]).then_inc(ld_rope, 16)

            def load(p, t, i):
                for s in range(SLOTS):
                    if not isinstance(t, int) or t:
                        sp.wait_ge(lo_split, t * SLOTS + (s + 1 - SLOTS))
                    sp.dma_start(raw[:, s, 0:p.blocks * P], io["w_" + p.name][i * SLOTS + s]).then_inc(raw_loaded[s], 16)

            for p in PHASES:
                t0, n = p.first // SLOTS, p.units // SLOTS
                begin = 0
                if p.first == 0:
                    load(p, 0, 0)
                    sp.dma_start(cm[:], io["cm"]).then_inc(ld_cm, 16)
                    begin = 1
                with sp.Fori(begin, n) as i:
                    load(p, i + t0, i)
            for m in range(KT):
                sp.wait_ge(y_ready, 7 * KT + m + 1)
                sp.dma_start(io["out"][:, m, :], outb[:, m, :]).then_inc(out_done, 16)
            sp.wait_ge(out_done, 16 * KT)

        @block.gpsimd
        def _(pool):
            pool.wait_ge(tiles_read, 4 + PH["up0"].first)
            nc.gpsimd.memset(acc[:], 0.0).then_inc(ada_done, 1)
            for o in range(2):
                pool.dma_start(ring[:, o, :], io["ada_w"][o]).then_inc(ld_ada[o], 16)
            with pool.Fori(1, ADA_OPS // 2) as i:
                for o in range(2):
                    pool.wait_ge(ada_done, i * 2 + o)
                    pool.dma_start(ring[:, o, :], io["ada_w"][i * 2 + o]).then_inc(ld_ada[o], 16)
            pool.wait_ge(tiles_read, SLOTS + PH["mix"].first)
            pool.dma_start(dft[:], io["dft"]).then_inc(ld_dft, 16)

        @block.scalar
        def _(act):
            mine = Steps(act, act_step)

            def rhs_round(version, k, src, n):
                nc.scalar.activation(hhi[:, k, 0:n], src, ACT.Copy).then_inc(rhs_hi, 1)

            act.wait_ge(ang_ready, 1)
            nc.scalar.activation(cs[64:96, 1, :], tb[64:96, 1, 0:SEQ], ACT.Sin)
            nc.scalar.activation(cs[64:96, 0, :], ab[64:96, 1, 0:SEQ], ACT.Sin).then_inc(cs_ready, 1)
            for k in range(KT):
                act.wait_ge(ld_x, 16 * KT)
                rhs_round("x", k, hf[:, k, :], TOK)
            for s in range(SLOTS):
                split_hi(act, 0, s, KT)

            act.wait_ge(g_dve, 1)
            nc.scalar.activation(S_(4), S_(3), ACT.Exp, scale=-1.0).then_inc(g_act, 1)
            nc.scalar.activation(S_(5), S_(1), ACT.Exp, scale=-1.0).then_inc(g_act, 1)
            nc.scalar.activation(S_(6), vec[:, V_ALOG:V_ALOG + NBLK], ACT.Exp).then_inc(g_act, 1)
            act.wait_ge(g_act, 1)
            nc.scalar.activation(S_(4), S_(4), ACT.Ln, bias=1.0).then_inc(g_act, 1)
            act.wait_ge(g_dve, 2)
            nc.scalar.activation(S_(9), S_(7), ACT.Exp).then_inc(g_act, 1)
            nc.scalar.activation(S_(10), S_(10), ACT.Exp).then_inc(g_act, 1)
            nc.scalar.activation(S_(11), S_(8), ACT.Exp).then_inc(g_act, 1)

            def a_silu(u, p):
                act.wait_ge(tiles_read, u + (SLOTS + 1))
                nc.scalar.activation(kvq[:, bass.ds(u * 256, 256)], tb[:, p, META:TOK], ACT.Silu)
                nc.scalar.activation(kvqm[:, bass.ds(u * META, META)], tb[:, p, 0:META], ACT.Silu).then_inc(a_act, 1)

            def a_kvq(i, before=True):
                for s in range(SLOTS):
                    u = i * SLOTS + s
                    if s or before:
                        a_silu(u - 1, (s - 1) % 2)
                    act.wait_ge(unit_done, u + 1)
                    nc.scalar.activation(tb[:, s % 2, :], ps[s][:, 0:TOK], ACT.Copy,
                                         scale=col(u * 4 + (V_ACONV + 3))).then_inc(a_tap, 1)
                    split_hi(act, i + 1, s, KT)

            a_kvq(0, before=False)
            with act.Fori(1, U_V // SLOTS) as i:
                a_kvq(i)
            a_silu(U_V - 1, 1)

            act.wait_ge(a_act, U_V)
            for kind, dst in enumerate((ex, ca)):
                nc.scalar.activation(dst[:, 0:MB, :], blocks_at(kind, 0, MB).rearrange("p (b t) -> p b t", t=P), ACT.Square)
                nc.scalar.activation(dst[:, MB, :], blocks_at(kind, MB, 1), ACT.Square).then_inc(sq_gdn, 1)

            def a_v(u):
                s = u % SLOTS
                act.wait_ge(unit_done, u + 1)
                nc.scalar.activation(tb[:, s % 2, :], ps[s][:, 0:TOK], ACT.Copy, scale=col(u * 4 + (V_ACONV + 3))).then_inc(a_tap, 1)
                split_hi(act, u // SLOTS + 1, s, KT)

            for u in (*U_TWO, U_THIRD):
                a_v(u)
                a_silu(u, u % 2)
            for g, (b0, n) in enumerate(GROUPS):
                act.wait_ge(d_diff, g + 1)
                nc.scalar.activation(ex[:, b0:b0 + n, :], ex[:, b0:b0 + n, :], ACT.Exp).then_inc(d_exp, 1)
                nc.scalar.activation(gt[:, b0:b0 + n, :], ps[4][:, 0:n * P].rearrange("p (b t) -> p b t", t=P), ACT.Exp).then_inc(d_exp, 1)
                u = U_THIRD + 1 + g
                a_v(u)
                a_silu(u, u % 2)

            for g, (b0, n) in enumerate(GROUPS):
                for kind, (dst, scales) in enumerate([(lambda b: ktm[:, b, :], 15), (lambda b: blocks_at(2, b, 1), 2)]):
                    act.wait_ge(mm_tr, 2 * g + kind + 1)
                    for j in range(n):
                        last = nc.scalar.activation(dst(b0 + j), ps[2 * (g % 2) + kind][:, j * P:(j + 1) * P], ACT.Copy,
                                                    scale=S_(scales)[:, b0 + j:b0 + j + 1])
                    last.then_inc(tr_read, 1)
            for g, (b0, n) in enumerate(GROUPS):
                act.wait_ge(mm_t0, g + 1)
                nc.scalar.activation(gt[:, b0:b0 + n, :], ps[4 + g % 4][:, 0:n * P].rearrange("p (b t) -> p b t", t=P), ACT.Copy).then_inc(tu_ready, 1)

            def a_z(u):
                s = u % SLOTS
                act.wait_ge(unit_done, u + 1)
                nc.scalar.activation(zs[:, u - U_Z, :], ps[s][:, TOK - N_A:TOK], ACT.Silu).then_inc(tiles_read, 1)
                split_hi(act, u // SLOTS + 1, s, KT)

            act.wait_ge(mm_v0, 1)
            nc.scalar.activation(vn[:, 7, :], ps[4][:, 0:P], ACT.Copy).then_inc(v0_read, 1)
            a_z(U_Z)
            for q in range(2):
                act.wait_ge(mm_s0, q + 1)
                nc.scalar.activation(st[:, 4 * q:4 * q + 4, :], ps[5 + q][:, :], ACT.Copy).then_inc(s_ready, 1)
            a_z(U_Z + 1)
            act.wait_ge(mm_o0, 1)
            nc.scalar.activation(ot[:, MB, :], ps[7][:, 0:P], ACT.Copy).then_inc(o_read, 1)
            for c in range(2):
                a_z(U_Z + 2 * c + 2)
                for q in range(2):
                    act.wait_ge(mm_vn, 2 * c + q + 1)
                    nc.scalar.activation(vn[:, 4 * q:4 * q + 4, :], ps[6 + q][:, :], ACT.Copy).then_inc(vn_ready, 1)
                a_z(U_Z + 2 * c + 3)
                for q in range(2):
                    act.wait_ge(mm_o, 2 * c + q + 1)
                    nc.scalar.activation(ot[:, 8 * q + c:8 * q + 8:2, :],
                                         ps[6 + q][:, :].rearrange("p (b t) -> p b t", t=P), ACT.Copy).then_inc(o_read, 1)

            act.wait_ge(o_read, 5)
            nc.scalar.activation(ex[:], ot[:], ACT.Square).then_inc(sq_gdn, 1)
            a_z(U_Z + 6)
            a_z(U_Z + 7)
            for h in range(HEADS):
                act.wait_ge(og_ready, h + 1)
                nc.scalar.activation(hhi[:, h, 0:N_A], ogb[:, h, :], ACT.Copy).then_inc(rhs_hi, 1)

            def act_splits(phase):
                def body(t, i, blocks):
                    for s in range(SLOTS):
                        split_hi(act, t + 1, s, blocks)
                steps(act, phase, body)

            def act_hidden(name, n, taps=None):
                def body(t, i, blocks):
                    for p in range(2):
                        s0, s1 = 2 * p, 2 * p + 1
                        j = i * 2 + p
                        act.wait_ge(unit_done, t * SLOTS + (s0 + 1))
                        if taps is not None:
                            c = j + CONV_AT[name]
                            nc.scalar.activation(tb[:, p, 0:n], ps[s0][:, 0:n], ACT.Copy, scale=col(j * 3 + taps)).then_inc(f_tap, 1)
                            split_hi(act, t + 1, s0, blocks)
                            act.wait_ge(f_conv, c * 2 + 2)
                            nc.scalar.activation(sb[:, p, 0:n], tb[:, p, 0:n], ACT.Silu).then_inc(f_gate, 1)
                        else:
                            nc.scalar.activation(sb[:, p, 0:n], ps[s0][:, 0:n], ACT.Silu).then_inc(f_gate, 1)
                            split_hi(act, t + 1, s0, blocks)
                        split_hi(act, t + 1, s1, blocks)
                        act.wait_ge(tiles_read, t * SLOTS + (SLOTS + s0 + 2))
                        nc.scalar.activation(ahi[:, j, 0:n], ab[:, p, 0:n], ACT.Copy).then_inc(hid_hi, 1)
                steps(act, PH[name], body)

            def act_square(m, n, src):
                nc.scalar.activation(sqb[:, m, 0:n], src[:, m, 0:n], ACT.Square).then_inc(sq_ready, 1)

            def act_norm(i, n, eps, shift, version=None, src=None, ready=None):
                mine(nc.scalar.activation(small[:, 314:315], eps_of(eps), ACT.Abs_reciprocal_sqrt))
                if src is not None:
                    for m in range(KT):
                        ready(m)
                        act_square(m, n, src)
                act.wait_ge(var_mm, i + 1)
                nc.scalar.activation(ab[:, 0, 0:n], ps[5][:, 0:n], ACT.Abs_reciprocal_sqrt, bias=eps_of(eps)).then_inc(guess_ready, 1)
                if version:
                    for m in range(KT):
                        act.wait_ge(y_ready, i * KT + m + 1)
                        nc.scalar.activation(hhi[:, m, 0:n], xb[:, m, 0:n], ACT.Identity, bias=shift(m)).then_inc(rhs_hi, 1)
                if i < 4:
                    for m in range(KT):
                        act.wait_ge(y_ready, i * KT + m + 1)
                        nc.scalar.activation(hf[:, m, 0:n], xb[:, m, 0:n], ACT.Identity, bias=shift(m)).then_inc(hf_ready, 1)

            def act_ln(i, n, version=None):
                act_norm(i, n, LN_EPS, ln_shift(i), version, xb, lambda m: act.wait_ge(xc_ready, i * KT + m + 1))

            def act_down_squares(name, i):
                def body(t, j, blocks):
                    for s in range(0, SLOTS, 2):
                        for k in range(2):
                            split_hi(act, t + 1, s + k, blocks)
                        m = j * 2 + s // 2
                        act.wait_ge(tiles_read, t * SLOTS + (SLOTS + s + 2))
                        nc.scalar.activation(sqb[:, m, 0:SEQ], hf[:, m, 0:SEQ], ACT.Square).then_inc(sq_ready, 1)
                steps(act, PH[name], body)

            act.wait_ge(eps_ready, 1)
            nc.scalar.activation(small[:, 300:308], vec[:, V_C:V_C + KT], ACT.Silu).then_inc(c_ready, 1)
            act_splits(PH["a_out"])
            act_ln(0, N_A, "ln0")
            act_hidden("up0", N_F0, V_FCONV)
            act_splits(PH["down0"])
            act_ln(1, N_F0, "ln1")

            def b_cx(t, i, blocks):
                for p in range(2):
                    act.wait_ge(unit_done, t * SLOTS + (2 * p + 1))
                    act.wait_ge(tiles_read, t * SLOTS + (2 * p + SLOTS))
                    nc.scalar.activation(tb[:, p, 0:N_F0], ps[2 * p][:, 0:N_F0], ACT.Copy).then_inc(f_tap, 1)
                    split_hi(act, t + 1, 2 * p, blocks)
                    split_hi(act, t + 1, 2 * p + 1, blocks)

            def b_gate(t, i, blocks):
                for s in range(SLOTS):
                    act.wait_ge(tiles_read, t * SLOTS + (SLOTS + s + 1))
                    nc.scalar.activation(ahi[:, i * SLOTS + s, 0:N_B], ab[:, s % 2, 0:N_B], ACT.Copy).then_inc(hid_hi, 1)
                    split_hi(act, t + 1, s, blocks)

            steps(act, PH["b_cx"], b_cx)
            steps(act, PH["b_gate"], b_gate)
            act_splits(PH["b_out"])
            act_ln(2, N_B, "ln2")
            act_hidden("up1", N_F1, V_FCONV + FT * 3)
            act_splits(PH["down1"])
            act_ln(3, N_F1)

            MIX = PH["mix"]
            M0 = MIX.first // SLOTS

            def mix_splits(u, k=1):
                for v in range(u, u + k):
                    nxt = v + SLOTS
                    split_hi(act, M0 + nxt // SLOTS, nxt % SLOTS, KT)

            act_norm(4, SEQ, RMS_EPS, sh_of(0), "rms0", hf, lambda m: act.wait_ge(hf_ready, 3 * KT + m + 1))
            act_hidden("up2", SEQ)
            act_down_squares("down2", 5)
            act_norm(5, SEQ, RMS_EPS, sh_of(1), "rms1")

            for u in range(10):
                act.wait_ge(unit_done, MIX.first + u + 1)
                b_ = ps[u % SLOTS]
                if u == 0:
                    nc.scalar.activation(krot[64:96, :], b_[64:96, 0:SEQ], ACT.Copy).then_inc(tiles_read, 1)
                elif u < 6:
                    nc.scalar.activation(lat[:, u - 1, :], b_[:, 0:SEQ], ACT.Copy).then_inc(tiles_read, 1)
                else:
                    nc.scalar.activation(uf[:, u - 6, :], b_[:, 0:SEQ], ACT.Copy).then_inc(tiles_read, 1)
                mix_splits(u)
            for j in range(5):
                act.wait_ge(tiles_read, SLOTS + MIX.first + 2 + j)
                nc.scalar.activation(lsq[:, j, :], lat[:, j, :], ACT.Square).then_inc(ls_sq, 1)

            def gate_unit(u):
                act.wait_ge(unit_done, MIX.first + u + 1)
                nc.scalar.activation(gates[:, u - 10, :], ps[u % SLOTS][:, 0:SEQ], ACT.Sigmoid).then_inc(tiles_read, 1)
                mix_splits(u)

            for u in range(10, 18):
                gate_unit(u)
            for j in range(5):
                act.wait_ge(lat_y, j + 1)
                nc.scalar.activation(lat[:, j, :], lat[:, j, :], ACT.Copy, scale=col(V_QN + j)).then_inc(lat_f, 1)
                act.wait_ge(lat_f, j + 1)
                nc.scalar.activation(lhi[:, j, :], lat[:, j, :], ACT.Copy).then_inc(lat_hi, 1)
            for u in range(18, 26):
                gate_unit(u)
            for j in range(4):
                act.wait_ge(four1, j + 1)
                nc.scalar.activation(pf[:, j // 2, 2 * (j % 2):2 * (j % 2) + 2, :],
                                     ps[4 + j][:, :].rearrange("p (g n) -> p g n", n=SEQ), ACT.Copy).then_inc(pf_ready, 1)
            for g in range(4):
                act.wait_ge(four2, g + 1)
                nc.scalar.activation(fhi[:, g, :], ps[g][:, 0:SEQ], ACT.Copy).then_inc(f_hi, 1)
            mix_splits(26, 3)
            for j in range(4):
                if j < 3:
                    act.wait_ge(q_mm, 2 * j + 2)
                else:
                    act.wait_ge(unit_done, MIX.first + 29)
                nc.scalar.activation(qt[0:96, 2 * j:2 * j + 2, :], ps[4 + j][0:96, :].rearrange("p (g n) -> p g n", n=SEQ), ACT.Copy).then_inc(q_read, 1)
            mix_splits(29, 3)
            for j in range(2):
                if j == 0:
                    act.wait_ge(v_mm, 1)
                else:
                    act.wait_ge(unit_done, MIX.first + 32)
                nc.scalar.activation(vt[:, j, :], ps[4 + j][:, :], ACT.Copy).then_inc(v_read, 1)
            mix_splits(32, 4)
            for h in range(HEADS + 1):
                if h < HEADS:
                    act.wait_ge(m_ready2, h + 1)
                    if h >= 2:
                        act.wait_ge(t_mm, h - 1)
                    for c in range(2):
                        last = nc.scalar.activation(pr[:, h % 2, c, :], ps[4 + h % 2][:, c * SEQ:(c + 1) * SEQ], ACT.Exp,
                                                    scale=SM_SCALE, bias=small[:, 112 + 2 * h + c:113 + 2 * h + c],
                                                    accum_out=small[:, 128 + 2 * h + c:129 + 2 * h + c])
                    last.then_inc(p_exp, 1)
                if h:
                    g = h - 1
                    act.wait_ge(t_mm, g + 1)
                    if g >= 2:
                        act.wait_ge(o_mm, g - 1)
                    nc.scalar.activation(pt[:, g % 2, :, :], ps[6 + g % 2][:, :].rearrange("p (c n) -> p c n", n=SEQ), ACT.Copy).then_inc(t_read, 1)
            for j in range(4):
                act.wait_ge(o_mm, 2 * j + 2)
                nc.scalar.activation(ohi[:, j, :], ps[j][:, 0:SEQ], ACT.Copy).then_inc(o_hi, 1)
            mix_splits(36, 4)
            for u in range(36, 40):
                act.wait_ge(tiles_read, SLOTS + MIX.first + u + 1)
                m = 2 * (u - 36)
                nc.scalar.activation(hhi[:, m:m + 2, 0:SEQ], xb[:, m:m + 2, 0:SEQ], ACT.Copy).then_inc(y_hi, 1)
            for u in range(40, 44):
                mix_splits(u)
            for s in range(SLOTS):
                split_hi(act, M0 + 12, s, KT)

            act_norm(6, SEQ, RMS_EPS, sh_of(2), "rms2", hf, lambda m: act.wait_ge(tiles_read, SLOTS + MIX.first + 40 + m + 1))
            act_hidden("up3", SEQ)
            act_down_squares("down3", 7)
            act_norm(7, SEQ, RMS_EPS, None)

        @block.vector
        def _(dve):
            mine = Steps(dve, dve_step)

            def step(instruction):
                mine(instruction)
                mine.after()

            def rsqrt(out, x, n, tmp):
                step(nc.vector.tensor_scalar(out.bitcast(I32), x.bitcast(I32), -0.5, 1597463007.0, ALU.mult, ALU.add))
                for _ in range(3):
                    step(nc.vector.tensor_tensor(tmp, out, out, ALU.mult))
                    step(nc.vector.scalar_tensor_tensor(tmp, tmp, -0.5, x, ALU.mult, ALU.mult))
                    step(nc.vector.scalar_tensor_tensor(out, tmp, 1.5, out, ALU.add, ALU.mult))

            def rhs_rest(version, k, src, n):
                dve.wait_ge(rhs_hi, RHS_AT[version] + k + 1)
                nc.vector.tensor_tensor(hlo[:, k, 0:n], src, hhi[:, k, 0:n], ALU.subtract).then_inc(rhs_ready, 1)

            nc.vector.memset(small[:, 0:1], 0.0).then_inc(tiles_read, SLOTS)
            R = slice(64, 96)
            dve.wait_ge(ld_rope, 16)
            dve.wait_ge(ld_small, 32)
            ang, n_i, n_f, wrap = tb[R, 0, 0:SEQ], sb[R, 0, 0:SEQ], ab[R, 0, 0:SEQ], sb[R, 1, 0:SEQ]
            step(nc.vector.tensor_copy(ang, pos[R, :]))
            step(nc.vector.tensor_scalar(ang, ang, vec[R, V_INVF:V_INVF + 1], None, ALU.mult))
            step(nc.vector.tensor_scalar(n_i.bitcast(I32), ang, 1.0 / (2 * np.pi), None, ALU.mult))
            step(nc.vector.tensor_copy(n_f, n_i.bitcast(I32)))
            for part in TWO_PI:
                step(nc.vector.scalar_tensor_tensor(ang, n_f, -part, ang, ALU.mult, ALU.add))

            def into_range(x):
                for sign, test in ((-1.0, ALU.is_gt), (1.0, ALU.is_lt)):
                    step(nc.vector.tensor_scalar(wrap, x, -sign * float(np.pi), sign * 2 * float(np.pi), test, ALU.mult))
                    step(nc.vector.tensor_tensor(x, x, wrap, ALU.add))

            into_range(ang)
            step(nc.vector.tensor_scalar(ab[R, 1, 0:SEQ], ang, float(np.pi) / 2, None, ALU.add))
            into_range(ab[R, 1, 0:SEQ])
            step(nc.vector.tensor_scalar(ab[R, 1, 0:SEQ], ab[R, 1, 0:SEQ], PI_IN, -PI_IN, ALU.min, ALU.max))
            nc.vector.tensor_scalar(tb[R, 1, 0:SEQ], ang, PI_IN, -PI_IN, ALU.min, ALU.max).then_inc(ang_ready, 1)
            dve.wait_ge(cs_ready, 1)
            step(nc.vector.tensor_scalar(cs[R, 1, :], cs[R, 1, :], vec[R, V_SIGN:V_SIGN + 1], None, ALU.mult))

            nc.vector.memset(small[:, 316:317], LN_EPS)
            nc.vector.memset(small[:, 317:318], RMS_EPS).then_inc(eps_ready, 1)
            dve.wait_ge(ld_x, 16 * KT)
            nc.vector.tensor_copy(xrep[:].rearrange("p k (h t) -> p k h t", t=META),
                                  hf[:, :, 0:META].unsqueeze(2).to_broadcast([P, KT, HEADS, META])).then_inc(xrep_ready, 1)
            for k in range(KT):
                rhs_rest("x", k, hf[:, k, :], TOK)
            for s in range(SLOTS):
                split_lo(dve, 0, s, KT)

            dve.wait_ge(ld_small, 32)
            dve.wait_ge(ld_cm, 16)
            dve.wait_ge(mm_gate, 1)
            for which, at_col in ((1, 0), (2, HEADS)):
                for c in range(2):
                    mine(nc.vector.tensor_copy(S_(which)[:, c:MB:2], ps[7][:, c * 16 + at_col:c * 16 + at_col + HEADS]))
                step(nc.vector.tensor_tensor(S_(12)[:, 0:HEADS], ps[7][:, 32 + at_col:32 + at_col + HEADS],
                                             vec[:, V_HEAD:V_HEAD + HEADS], ALU.mult))
                step(nc.vector.reduce_sum(S_(which)[:, MB:NBLK], S_(12)[:, 0:HEADS], AX.X))
            step(nc.vector.tensor_tensor(S_(2), S_(2), vec[:, V_DT:V_DT + NBLK], ALU.add))
            step(nc.vector.tensor_scalar(S_(3), S_(2), -1.0, None, ALU.mult))
            nc.vector.tensor_tensor(S_(3), S_(3), S_(2), ALU.max).then_inc(g_dve, 1)
            dve.wait_ge(g_act, 4)
            step(nc.vector.scalar_tensor_tensor(S_(4), S_(2), 0.0, S_(4), ALU.max, ALU.add))
            nc.vector.scalar_tensor_tensor(S_(6), S_(4), -1.0, S_(6), ALU.mult, ALU.mult).then_inc(gl_ready, 1)
            step(nc.vector.tensor_scalar(S_(5), S_(5), 1.0, None, ALU.add))
            step(nc.vector.reciprocal(S_(2), S_(5)))
            dve.wait_ge(mm_cum, 1)
            step(nc.vector.tensor_copy(S_(7), ps[7][:, 64:64 + NBLK]))
            step(nc.vector.tensor_copy(S_(8), ps[7][:, 96:96 + NBLK]))
            nc.vector.tensor_tensor(S_(10), S_(8), S_(7), ALU.subtract).then_inc(g_dve, 1)

            def conv(u, i, s):
                t_ = tb[:, s % 2, :]
                dve.wait_ge(a_tap, u + 1)
                for j, tap in enumerate((2, 1, 0)):
                    if j:
                        dve.wait_ge(a_conv, u * 2 + j)
                    nc.vector.scalar_tensor_tensor(t_[:, j + 1:TOK], ps[s][:, 0:TOK - 1 - j], col(u * 4 + (V_ACONV + tap)),
                                                   t_[:, j + 1:TOK], ALU.mult, ALU.add).then_inc(a_conv if j < 2 else tiles_read, 1)
                split_lo(dve, i + 1, s, KT)

            def d_v(u):
                conv(u, u // SLOTS, u % SLOTS)

            def d_z(u):
                split_lo(dve, u // SLOTS + 1, u % SLOTS, KT)

            with dve.Fori(0, U_V // SLOTS) as i:
                for s in range(SLOTS):
                    conv(i * SLOTS + s, i, s)
            for u in U_TWO:
                d_v(u)

            dve.wait_ge(mm_norm, 1)
            dve.wait_ge(g_act, 7)
            nn = small[:, 320:320 + 2 * NBLK]
            step(nc.vector.tensor_scalar(nn, ps[7][:, 0:2 * NBLK], L2_EPS, None, ALU.add))
            rsqrt(small[:, 360:360 + 2 * NBLK], nn, 2 * NBLK, small[:, 400:400 + 2 * NBLK])
            rk, rq = small[:, 360:360 + NBLK], small[:, 360 + NBLK:360 + 2 * NBLK]
            mine(nc.vector.tensor_tensor(S_(12), rk, S_(2), ALU.mult))
            mine(nc.vector.tensor_scalar(S_(13), rq, float(P) ** -0.5, None, ALU.mult))
            step(nc.vector.tensor_tensor(S_(15), rk, S_(10), ALU.mult))
            nc.vector.scalar_tensor_tensor(S_(16), S_(12), -1.0, S_(9), ALU.mult, ALU.mult).then_inc(cols_ready, 1)
            d_v(U_THIRD)

            for g, (b0, n) in enumerate(GROUPS):
                w = n * P
                dve.wait_ge(mm_gb, g + 1)
                for j in range(n):
                    last = nc.vector.tensor_scalar(ex[:, b0 + j, :], ps[4][:, j * P:(j + 1) * P], S_(7)[:, b0 + j:b0 + j + 1],
                                                   0.0, ALU.subtract, ALU.min)
                last.then_inc(d_diff, 1)
                dve.wait_ge(d_exp, 2 * g + 1)
                e_ = ex[:, b0:b0 + n, :]
                step(nc.vector.tensor_tensor(e_, e_, bcast(cm[:, C_CAUSAL_META if b0 == MB else C_CAUSAL, :], n), ALU.mult))
                dve.wait_ge(mm_cb, g + 1)
                for j in range(n):
                    b = b0 + j
                    nc.vector.scalar_tensor_tensor(bn[:, b, :], ps[6][:, j * P:(j + 1) * P], rk[:, b:b + 1], ex[:, b, :], ALU.mult, ALU.mult)
                    last = nc.vector.scalar_tensor_tensor(ca[:, b, :], ps[7][:, j * P:(j + 1) * P], rk[:, b:b + 1], ex[:, b, :], ALU.mult, ALU.mult)
                step(last)
                mine(nc.vector.tensor_tensor(bn[:, b0:b0 + n, :], bn[:, b0:b0 + n, :], ps[5][:, 0:w].rearrange("p (b t) -> p b t", t=P), ALU.mult))
                q_ = blocks_at(1, b0, n)
                dve.wait_ge(d_exp, 2 * g + 2)
                nc.vector.tensor_tensor(q_, q_, gt[:, b0:b0 + n, :].rearrange("p b t -> p (b t)"), ALU.mult).then_inc(m_ready, 1)
                d_v(U_THIRD + 1 + g)

            for g, (b0, n) in enumerate(GROUPS):
                step(nc.vector.tensor_tensor(gu[:, b0:b0 + n, :], bn[:, b0:b0 + n, :], bcast(cm[:, C_PAIR, :], n), ALU.mult))
                nc.vector.tensor_tensor(gu[:, b0:b0 + n, :], gu[:, b0:b0 + n, :], bcast(ident, n), ALU.add).then_inc(gu0_ready, 1)

            def mask_x(l, g):
                b0, n = GROUPS[g]
                dve.wait_ge(mm_x, (l - 1) * 5 + (g + 1))
                nc.vector.tensor_tensor(ex[:, b0:b0 + n, :], ps[g % 2][:, 0:n * P].rearrange("p (b t) -> p b t", t=P),
                                        cm[:, bass.ds(l + C_LEVEL, 1), :].to_broadcast([P, n, P]), ALU.mult).then_inc(x_ready, 1)

            def add_y(l, g, both=True):
                b0, n = GROUPS[g]
                dve.wait_ge(mm_y, (l - 1) * 5 + (g + 1))
                if both:
                    nc.vector.tensor_tensor(gt[:, b0:b0 + n, :], gt[:, b0:b0 + n, :],
                                            ps[2 + g % 3][:, 0:n * P].rearrange("p (b t) -> p b t", t=P), ALU.add)
                nc.vector.tensor_tensor(gu[:, b0:b0 + n, :], gu[:, b0:b0 + n, :],
                                        ps[5 + g % 3][:, 0:n * P].rearrange("p (b t) -> p b t", t=P), ALU.add).then_inc(tu_ready, 1)

            with dve.Fori(1, LEVELS - 1) as l:
                dve.wait_ge(tu_ready, l * 5)
                for g in range(len(GROUPS)):
                    mask_x(l, g)
                    if g:
                        add_y(l, g - 1)
                add_y(l, len(GROUPS) - 1)
            dve.wait_ge(tu_ready, (LEVELS - 1) * 5)
            for g in range(4):
                mask_x(LEVELS - 1, g)
                if g:
                    add_y(LEVELS - 1, g - 1, both=False)
            add_y(LEVELS - 1, 3, both=False)

            dve.wait_ge(v0_read, 1)
            for h in range(HEADS):
                last = nc.vector.tensor_scalar(rr[:, h, :], ps[4][:, 0:P], vec[:, V_HEAD + h:V_HEAD + h + 1], None, ALU.mult)
            last.then_inc(vm_ready, 1)
            d_z(U_Z)
            d_z(U_Z + 1)
            for c in range(2):
                for q in range(2):
                    r = 2 * c + q
                    dve.wait_ge(mm_ks, r + 1)
                    for j in range(4):
                        h = 4 * q + j
                        b = 2 * h + c
                        last = nc.vector.scalar_tensor_tensor(rr[:, h, :], ps[4 + q][:, j * P:(j + 1) * P], S_(16)[:, b:b + 1],
                                                              blocks_at(2, b, 1), ALU.mult, ALU.add)
                    last.then_inc(r_ready, 1)
                d_z(U_Z + 2 * c + 2)
                d_z(U_Z + 2 * c + 3)
                if c == 0:
                    for q in range(2):
                        dve.wait_ge(mm_ds, q + 1)
                        dve.wait_ge(mm_o, q + 1)
                        for j in range(4):
                            h = 4 * q + j
                            last = nc.vector.scalar_tensor_tensor(st[:, h, :], st[:, h, :], S_(11)[:, 2 * h:2 * h + 1],
                                                                  ps[4 + q][:, j * P:(j + 1) * P], ALU.mult, ALU.add)
                        last.then_inc(s_ready, 1)
            d_z(U_Z + 6)
            d_z(U_Z + 7)

            dve.wait_ge(mm_norm, 2)
            nn = small[:, 320:320 + NBLK]
            step(nc.vector.tensor_tensor(nn, ps[7][:, 0:NBLK], S_(13), ALU.mult))
            step(nc.vector.tensor_tensor(nn, nn, S_(13), ALU.mult))
            step(nc.vector.tensor_scalar(nn, nn, 1.0 / P, RMS_EPS, ALU.mult, ALU.add))
            rsqrt(small[:, 360:360 + NBLK], nn, NBLK, small[:, 400:400 + NBLK])
            nc.vector.tensor_tensor(S_(12), small[:, 360:360 + NBLK], S_(13), ALU.mult).then_inc(cols_ready, 1)
            for g in (4, 0, 1, 2, 3):
                b0, n = GROUPS[g]
                dve.wait_ge(mm_gb, len(GROUPS) + (1 if g == 4 else g + 2))
                step(nc.vector.tensor_tensor(bn[:, b0:b0 + n, :], ot[:, b0:b0 + n, :],
                                             ps[[1, 2, 3, 4, 0][g]][:, 0:n * P].rearrange("p (b t) -> p b t", t=P), ALU.mult))
                if g == 4:
                    step(nc.vector.scalar_tensor_tensor(
                        ogb[:, :, 0:6], bn[:, MB, :].rearrange("p (h t) -> p h t", t=META)[:, :, META - 6:META],
                        col(V_ANORM), zs[:, :, 0:6], ALU.mult, ALU.mult))
                else:
                    for h in (2 * g, 2 * g + 1):
                        nc.vector.scalar_tensor_tensor(
                            ogb[:, h, 6:N_A].rearrange("p (c t) -> p c t", t=P), bn[:, 2 * h:2 * h + 2, :], col(V_ANORM),
                            zs[:, h, 6:N_A].rearrange("p (c t) -> p c t", t=P), ALU.mult, ALU.mult).then_inc(og_ready, 1)
            for h in range(HEADS):
                rhs_rest("gdn", h, ogb[:, h, :], N_A)

            def dve_ada(o, r):
                dve.wait_ge(ld_ada[r], (o // 2) * 16 + 16)
                dve.wait_ge(ada_done, o + 1)
                a_ = acc[:, o // KT, :] if isinstance(o, int) else acc[:, bass.ds(o // KT, 1), :].rearrange("p a n -> p (a n)")
                nc.vector.scalar_tensor_tensor(a_, ring[:, r, :], small[:, bass.ds(o + 440, 1)], a_, ALU.mult, ALU.add).then_inc(ada_done, 1)

            def dve_residual(name, n, off):
                phase = PH[name]
                per = 2 if phase.blocks == SLOT_BLOCKS else 1

                def body(t, i, blocks):
                    for s in range(0, SLOTS, per):
                        m = i * (SLOTS // per) + s // per
                        dve.wait_ge(unit_done, t * SLOTS + (s + per))
                        nc.vector.scalar_tensor_tensor(xb[:, m, 0:n], hf[:, m, off:off + n], ALPHA, ps[s][:, 0:n],
                                                       ALU.mult, ALU.add).then_inc(tiles_read, per)
                        dve.wait_ge(tiles_read, t * SLOTS + (SLOTS + s + per))
                        nc.vector.tensor_tensor(sums[:, 0:n], sums[:, 0:n], xb[:, m, 0:n], ALU.add).then_inc(sum_ready, 1)
                        for j in range(per):
                            split_lo(dve, t + 1, s + j, blocks)
                        if name in ADA_AT:
                            for j in range(2):
                                dve_ada(i * 4 + (ADA_AT[name] + s + j), j)
                step(nc.vector.memset(sums[:, 0:n], 0.0))
                steps(dve, phase, body)

            def dve_hidden(name, n, taps=None):
                def body(t, i, blocks):
                    for p in range(2):
                        s0, s1 = 2 * p, 2 * p + 1
                        j = i * 2 + p
                        if taps is not None:
                            c = j + CONV_AT[name]
                            dve.wait_ge(f_tap, c + 1)
                            nc.vector.scalar_tensor_tensor(tb[:, p, 0:n], ps[s0][:, 1:n + 1], col(j * 3 + (taps + 1)),
                                                           tb[:, p, 0:n], ALU.mult, ALU.add).then_inc(f_conv, 1)
                            dve.wait_ge(f_conv, c * 2 + 1)
                            nc.vector.scalar_tensor_tensor(tb[:, p, 0:n], ps[s0][:, 2:n + 2], col(j * 3 + (taps + 2)),
                                                           tb[:, p, 0:n], ALU.mult, ALU.add).then_inc(f_conv, 1)
                        split_lo(dve, t + 1, s0, blocks)
                        dve.wait_ge(f_gate, j + (GATE_AT[name] + 1))
                        dve.wait_ge(unit_done, t * SLOTS + (s1 + 1))
                        off = 0 if taps is None else 2
                        nc.vector.tensor_tensor(ab[:, p, 0:n], sb[:, p, 0:n], ps[s1][:, off:off + n], ALU.mult).then_inc(tiles_read, 2)
                        split_lo(dve, t + 1, s1, blocks)
                        if name in ADA_AT:
                            dve_ada(i * 2 + (ADA_AT[name] + p), p)
                        dve.wait_ge(hid_hi, j + (HID_AT[name] + 1))
                        nc.vector.tensor_tensor(alo[:, j, 0:n], ab[:, p, 0:n], ahi[:, j, 0:n], ALU.subtract).then_inc(hid_ready, 1)
                steps(dve, PH[name], body)

            def dve_norm(i, n, src, eps, gain, shift, version=None, dst=None):
                if i < 4:
                    dve.wait_ge(mean_mm, i + 1)
                    for m in range(KT):
                        nc.vector.tensor_tensor(xb[:, m, 0:n], xb[:, m, 0:n], ps[4][:, 0:n], ALU.subtract).then_inc(xc_ready, 1)
                dve.wait_ge(guess_ready, i + 1)
                v_, y_, t_ = tb[:, 0, 0:n], ab[:, 0, 0:n], sb[:, 0, 0:n]
                step(nc.vector.tensor_tensor(t_, y_, y_, ALU.mult))
                step(nc.vector.scalar_tensor_tensor(v_, ps[5][:, 0:n], eps, t_, ALU.add, ALU.mult))
                step(nc.vector.scalar_tensor_tensor(y_, v_, 3.0, y_, ALU.subtract, ALU.mult))
                dst = xb if dst is None else dst
                for m in range(KT + 1):
                    if m < KT:
                        nc.vector.scalar_tensor_tensor(dst[:, m, 0:n], src[:, m, 0:n], gain(m), y_, ALU.mult, ALU.mult).then_inc(y_ready, 1)
                    if m and version:
                        dve.wait_ge(rhs_hi, RHS_AT[version] + m)
                        nc.vector.scalar_tensor_tensor(hlo[:, m - 1, 0:n], xb[:, m - 1, 0:n], shift(m - 1), hhi[:, m - 1, 0:n],
                                                       ALU.add, ALU.subtract).then_inc(rhs_ready, 1)

            def dve_ln(i, n, version=None):
                dve_norm(i, n, xb, LN_EPS, ln_gain(i), ln_shift(i), version)

            for i in range(4):
                mine(nc.vector.tensor_scalar(vec[:, V_LN + 2 * i * KT:V_LN + (2 * i + 1) * KT], vec[:, V_LN + 2 * i * KT:V_LN + (2 * i + 1) * KT],
                                             -0.5, None, ALU.mult))
            step(nc.vector.tensor_scalar(vec[:, V_NORM + 3 * KT:V_NORM + 4 * KT], vec[:, V_NORM + 3 * KT:V_NORM + 4 * KT], -0.5, None, ALU.mult))
            dve.wait_ge(c_ready, 1)
            step(nc.vector.tensor_copy(small[:, 440:512].rearrange("p (n k) -> p n k", k=KT), bcast(small[:, 300:308], 9)))
            dve_residual("a_out", N_A, TOK - N_A)
            dve_ln(0, N_A, "ln0")
            dve_hidden("up0", N_F0, V_FCONV)
            dve_residual("down0", N_F0, N_A - N_F0)
            dve_ln(1, N_F0, "ln1")

            def b_cx(t, i, blocks):
                for p in range(2):
                    m = i * 2 + p
                    c = m + CONV_AT["b_cx"]
                    dve.wait_ge(f_tap, c + 1)
                    dve.wait_ge(unit_done, t * SLOTS + (2 * p + 2))
                    nc.vector.tensor_tensor(tb[:, p, 0:N_F0], tb[:, p, 0:N_F0], ps[2 * p + 1][:, 0:N_F0], ALU.mult).then_inc(f_conv, 1)
                    split_lo(dve, t + 1, 2 * p, blocks)
                    dve.wait_ge(f_conv, c * 2 + 1)
                    nc.vector.tensor_scalar(xb[:, m, 0:N_B], tb[:, p, 0:N_B], col(m * 3 + V_BCONV), None, ALU.mult).then_inc(b_tap, 1)
                    dve.wait_ge(b_tap, m + 1)
                    nc.vector.scalar_tensor_tensor(xb[:, m, 0:N_B], tb[:, p, 1:N_B + 1], col(m * 3 + (V_BCONV + 1)),
                                                   xb[:, m, 0:N_B], ALU.mult, ALU.add).then_inc(f_conv, 1)
                    dve.wait_ge(f_conv, c * 2 + 2)
                    nc.vector.scalar_tensor_tensor(xb[:, m, 0:N_B], tb[:, p, 2:N_B + 2], col(m * 3 + (V_BCONV + 2)),
                                                   xb[:, m, 0:N_B], ALU.mult, ALU.add).then_inc(tiles_read, 2)
                    split_lo(dve, t + 1, 2 * p + 1, blocks)
                    dve_ada(i * 2 + (ADA_AT["b_cx"] + p), p)

            def b_gate(t, i, blocks):
                for s in range(SLOTS):
                    m = i * SLOTS + s
                    dve.wait_ge(unit_done, t * SLOTS + (s + 1))
                    nc.vector.tensor_tensor(ab[:, s % 2, 0:N_B], xb[:, m, 0:N_B], ps[s][:, 2:N_F0], ALU.mult).then_inc(tiles_read, 1)
                    split_lo(dve, t + 1, s, blocks)
                    if s % 2:
                        dve_ada(i * 2 + (ADA_AT["b_gate"] + s // 2), s // 2)
                    dve.wait_ge(hid_hi, m + (HID_AT["b_gate"] + 1))
                    nc.vector.tensor_tensor(alo[:, m, 0:N_B], ab[:, s % 2, 0:N_B], ahi[:, m, 0:N_B], ALU.subtract).then_inc(hid_ready, 1)

            steps(dve, PH["b_cx"], b_cx)
            dve.wait_ge(tiles_read, SLOTS + PH["b_gate"].first)
            steps(dve, PH["b_gate"], b_gate)
            dve_residual("b_out", N_B, N_F0 - N_B)
            dve_ln(2, N_B, "ln2")
            dve_hidden("up1", N_F1, V_FCONV + FT * 3)
            dve_residual("down1", N_F1, N_B - N_F1)
            dve_ln(3, N_F1)

            MIX = PH["mix"]
            M0 = MIX.first // SLOTS

            def mix_splits(u, k=1):
                for v in range(u, u + k):
                    nxt = v + SLOTS
                    split_lo(dve, M0 + nxt // SLOTS, nxt % SLOTS, KT)

            dve.wait_ge(mods_mm, 3)
            step(nc.vector.tensor_tensor(small[:, 0:72], ps[6][:, 0:72], vec[:, V_ADAB:V_ADAB + 72], ALU.add))
            for i in range(3):
                step(nc.vector.scalar_tensor_tensor(small[:, 72 + KT * i:80 + KT * i], small[:, (3 * i + 1) * KT:(3 * i + 2) * KT], 1.0,
                                                    vec[:, V_NORM + KT * i:V_NORM + KT * (i + 1)], ALU.add, ALU.mult))
            step(nc.vector.tensor_scalar(small[:, 72:72 + 3 * KT], small[:, 72:72 + 3 * KT], -0.5, None, ALU.mult))
            for g in (2, 8):
                last = nc.vector.tensor_scalar(small[:, g * KT:(g + 1) * KT], small[:, g * KT:(g + 1) * KT], 0.5, None, ALU.mult)
                if g == 2:
                    mine(last)
            last.then_inc(mods_ready, 1)
            dve.wait_ge(mods_ready, 1)

            def gated_residual(t, i, blocks, per, gate, squares=None):
                for s in range(0, SLOTS, per):
                    m = i * (SLOTS // per) + s // per
                    dve.wait_ge(unit_done, t * SLOTS + (s + per))
                    nc.vector.scalar_tensor_tensor(hf[:, m, 0:SEQ], ps[s][:, 0:SEQ], small[:, bass.ds(m + gate * KT, 1)],
                                                   hf[:, m, 0:SEQ], ALU.mult, ALU.add).then_inc(tiles_read, per)
                    for j in range(per):
                        split_lo(dve, t + 1, s + j, blocks)
                    if squares is not None:
                        add_squares(squares, m)

            def add_squares(norm, m):
                dve.wait_ge(sq_ready, m + (norm * KT + 1))
                dve.wait_ge(sum_ready, m + (SUMS_AT[norm]))
                nc.vector.tensor_tensor(sums[:, 0:SEQ], sums[:, 0:SEQ], sqb[:, m, 0:SEQ], ALU.add).then_inc(sum_ready, 1)

            def down_squares(name, gate, norm):
                step(nc.vector.memset(sums[:, 0:SEQ], 0.0))
                steps(dve, PH[name], lambda t, i, blocks: gated_residual(t, i, blocks, 2, gate, norm))

            dve_norm(4, SEQ, hf, NORM_EPS, a_of(0), sh_of(0), "rms0")
            dve_hidden("up2", SEQ)
            down_squares("down2", 2, 5)
            dve_norm(5, SEQ, hf, NORM_EPS, a_of(1), sh_of(1), "rms1")

            mix_splits(0, 14)
            dve.wait_ge(lat_mm, 1)
            for f0, f1, at_ in ((0, 3, 0), (3, 5, SEQ)):
                x_, r_, t_ = tb[:, 0, 0:SEQ], ab[:, 0, 0:SEQ], sb[:, 0, 0:SEQ]
                step(nc.vector.tensor_scalar(x_, ps[4][:, at_:at_ + SEQ], 1.0 / ((f1 - f0) * P), NORM_EPS, ALU.mult, ALU.add))
                rsqrt(r_, x_, SEQ, t_)
                for j in range(f0, f1):
                    nc.vector.tensor_tensor(lat[:, j, :], lat[:, j, :], r_, ALU.mult).then_inc(lat_y, 1)
                dve.wait_ge(lat_y, f1)
            mix_splits(14, 4)
            for j in range(5):
                dve.wait_ge(lat_hi, j + 1)
                nc.vector.tensor_tensor(llo[:, j, :], lat[:, j, :], lhi[:, j, :], ALU.subtract).then_inc(lat_ready, 1)
            mix_splits(18, 8)
            for g in range(4):
                dve.wait_ge(f_hi, g + 1)
                nc.vector.tensor_tensor(flo[:, g, :], ps[g][:, 0:SEQ], fhi[:, g, :], ALU.subtract).then_inc(f_ready, 1)
            mix_splits(26, 3)
            for j in range(4):
                if j % 2 == 0:
                    dve.wait_ge(k_mm, 3 * (j // 2) + 2)
                else:
                    dve.wait_ge(unit_done, MIX.first + 30 + j // 2)
                nc.vector.tensor_copy(kt_[0:64, 2 * j:2 * j + 2, :], ps[j][0:64, :].rearrange("p (g n) -> p g n", n=SEQ)).then_inc(k_read, 1)
            mix_splits(29, 2)
            dve.wait_ge(v_read, 2)
            dve.wait_ge(q_read, 4)
            nc.vector.memset(small[:, 310:311], 0.0).then_inc(tiles_read, 6)
            mix_splits(31, 1)
            swap = [(i + 16) % 32 for i in range(32)]
            c_, s_ = cs[R, 0, :], cs[R, 1, :]

            def bc(x, n):
                return x.unsqueeze(1).to_broadcast([32, n, SEQ])

            step(nc.vector.stream_shuffle(rot[R, 0, :], krot[R, :], swap))
            mine(nc.vector.tensor_tensor(rot[R, 0, :], rot[R, 0, :], s_, ALU.mult))
            step(nc.vector.tensor_tensor(krot[R, :], krot[R, :], c_, ALU.mult))
            step(nc.vector.tensor_tensor(krot[R, :], krot[R, :], rot[R, 0, :], ALU.add))
            mine(nc.vector.tensor_copy(kt_[R, :, :], bc(krot[R, :], HEADS)))
            for h in range(0, HEADS, 4):
                q_, r_ = qt[R, h:h + 4, :], rot[R, h:h + 4, :]
                step(nc.vector.stream_shuffle(r_.rearrange("p h n -> p (h n)"), q_.rearrange("p h n -> p (h n)"), swap))
                mine(nc.vector.tensor_tensor(r_, r_, bc(s_, 4), ALU.mult))
                step(nc.vector.tensor_tensor(q_, q_, bc(c_, 4), ALU.mult))
                nc.vector.tensor_tensor(q_, q_, r_, ALU.add).then_inc(rope_ready, 1)
            for u in range(32, 36):
                dve.wait_ge(unit_done, MIX.first + u + 1)
                m = 2 * (u - 32)
                nc.vector.tensor_tensor(xb[:, m:m + 2, 0:SEQ], gates[:, m:m + 2, :], ps[u % SLOTS][:, :].rearrange("p (g n) -> p g n", n=SEQ),
                                        ALU.mult).then_inc(tiles_read, 1)
                mix_splits(u)
            for h in range(HEADS + 1):
                if h < HEADS:
                    dve.wait_ge(s_mm, h + 1)
                    step(nc.vector.reduce_max(small[:, 144 + 2 * h:146 + 2 * h], ps[4 + h % 2][:, :].rearrange("p (c n) -> p c n", n=SEQ), AX.X))
                    nc.vector.tensor_scalar(small[:, 112 + 2 * h:114 + 2 * h], small[:, 144 + 2 * h:146 + 2 * h], -SM_SCALE, None,
                                            ALU.mult).then_inc(m_ready2, 1)
                if h:
                    g = h - 1
                    dve.wait_ge(p_exp, g + 1)
                    step(nc.vector.reciprocal(small[:, 160 + 2 * g:162 + 2 * g], small[:, 128 + 2 * g:130 + 2 * g]))
                    for c in range(2):
                        last = nc.vector.tensor_scalar(pr[:, g % 2, c, :], pr[:, g % 2, c, :], small[:, 160 + 2 * g + c:161 + 2 * g + c], None, ALU.mult)
                    last.then_inc(p_ready, 1)
            for j in range(4):
                dve.wait_ge(o_hi, j + 1)
                nc.vector.tensor_tensor(olo[:, j, :], ps[j][:, 0:SEQ], ohi[:, j, :], ALU.subtract).then_inc(o_ready, 1)
            for u in range(36, 41):
                if u < 40:
                    dve.wait_ge(unit_done, MIX.first + u + 1)
                    m = 2 * (u - 36)
                    t_ = gates[:, 8 + m:10 + m, :]
                    step(nc.vector.tensor_tensor(t_, t_, ps[u % SLOTS][:, :].rearrange("p (g n) -> p g n", n=SEQ), ALU.mult))
                    nc.vector.tensor_tensor(xb[:, m:m + 2, 0:SEQ], xb[:, m:m + 2, 0:SEQ], t_, ALU.add).then_inc(tiles_read, 1)
                    mix_splits(u)
                if u > 36:
                    m = 2 * (u - 37)
                    dve.wait_ge(y_hi, u - 36)
                    nc.vector.tensor_tensor(hlo[:, m:m + 2, 0:SEQ], xb[:, m:m + 2, 0:SEQ], hhi[:, m:m + 2, 0:SEQ], ALU.subtract).then_inc(y_lo, 1)
            for i in range(2):
                gated_residual(M0 + 10 + i, i, KT, 1, 5)
            dve_norm(6, SEQ, hf, NORM_EPS, a_of(2), sh_of(2), "rms2")
            dve_hidden("up3", SEQ)
            down_squares("down3", 8, 7)
            dve_norm(7, SEQ, hf, NORM_EPS, lambda m: col(V_NORM + 3 * KT + m), None, dst=outb)

        @block.tensor
        def _(pe):
            def unit(t, s, blocks, n, rhi, rlo, out=None, first=True, last=True, k0=0, k_wait=None):
                pe.wait_ge(lo_split, t * SLOTS + (s + 1))
                if first:
                    pe.wait_ge(tiles_read, t * SLOTS + (s + 1))
                out = ps[s][:, 0:n] if out is None else out
                for k in range(blocks):
                    if k_wait is not None:
                        k_wait(k)
                    w = slice(k * P, (k + 1) * P)
                    nc.tensor.matmul(out, whi[:, s, w], rhi(k0 + k), start=first and k == 0, stop=False)
                    nc.tensor.matmul(out, whi[:, s, w], rlo(k0 + k), start=False, stop=False)
                    ins = nc.tensor.matmul(out, wlo[:, s, w], rhi(k0 + k), start=False, stop=last and k == blocks - 1)
                ins.then_inc(unit_done, 1)

            def stream(phase, n, version):
                def k_wait(k):
                    pe.wait_ge(rhs_ready, RHS_AT[version] + k + 1)
                t0 = phase.first // SLOTS
                with pe.Fori(t0, t0 + phase.units // SLOTS) as t:
                    for s in range(SLOTS):
                        unit(t, s, KT, n, lambda k: hhi[:, k, 0:n], lambda k: hlo[:, k, 0:n], k_wait=None if s else k_wait)

            pe.wait_ge(xrep_ready, 1)
            pe.wait_ge(ld_small, 32)
            pe.wait_ge(ld_cm, 16)
            for j in range(3):
                for k in range(KT):
                    lhs = xrep[:, k, :] if j == 2 else hf[:, k, META + j * P:META + (j + 1) * P]
                    last = nc.tensor.matmul(ps[7][:, 16 * j:16 * j + 16], lhs, wab[:, k, :], start=(k == 0), stop=(k == KT - 1))
            last.then_inc(mm_gate, 1)
            pe.wait_ge(gl_ready, 1)
            g_ = S_(6)
            nc.tensor.matmul(ps[7][:, 64:64 + MB], cm[:, C_CAUSAL, :], g_[:, 0:MB], start=True, stop=True)
            nc.tensor.matmul(ps[7][:, 64 + MB:64 + NBLK], cm[:, C_CAUSAL_META, :], g_[:, MB:NBLK], start=True, stop=True)
            nc.tensor.matmul(ps[7][:, 96:96 + MB], ones, g_[:, 0:MB], start=True, stop=True)
            nc.tensor.matmul(ps[7][:, 96 + MB:96 + NBLK], cm[:, C_SAME_META, :], g_[:, MB:NBLK], start=True, stop=True).then_inc(mm_cum, 1)

            def a_unit(t, s, k_wait=None):
                unit(t, s, KT, TOK, lambda k: hhi[:, k, 0:TOK], lambda k: hlo[:, k, 0:TOK], k_wait=k_wait)

            def one(u):
                a_unit(u // SLOTS, u % SLOTS)

            with pe.Fori(0, U_V // SLOTS) as t:
                for s in range(SLOTS):
                    a_unit(t, s, k_wait=None if s else lambda k: pe.wait_ge(rhs_ready, RHS_AT["x"] + k + 1))

            k_b = lambda b: blocks_at(0, b, 1)
            q_b = lambda b: blocks_at(1, b, 1)
            v_b = lambda b: blocks_at(2, b, 1)

            for u in U_TWO:
                one(u)
            for i, sq in enumerate((ex, ca)):
                pe.wait_ge(sq_gdn, i + 1)
                for b in range(NBLK):
                    last = nc.tensor.matmul(ps[7][:, i * NBLK + b:i * NBLK + b + 1], sq[:, b, :], ones[:, 0:1], start=True, stop=True)
            last.then_inc(mm_norm, 1)
            one(U_THIRD)

            def spread(bank, b0, n, which):
                for j in range(n):
                    last = nc.tensor.matmul(ps[bank][:, j * P:(j + 1) * P], S_(which)[:, b0 + j:b0 + j + 1].to_broadcast([P, P]),
                                            ident, start=True, stop=True)
                return last

            pe.wait_ge(cols_ready, 1)
            for g, (b0, n) in enumerate(GROUPS):
                if g:
                    pe.wait_ge(m_ready, g)
                spread(4, b0, n, 7).then_inc(mm_gb, 1)
                spread(5, b0, n, 12)
                for j in range(n):
                    b = b0 + j
                    nc.tensor.matmul(ps[6][:, j * P:(j + 1) * P], k_b(b), k_b(b), start=True, stop=True)
                    last = nc.tensor.matmul(ps[7][:, j * P:(j + 1) * P], k_b(b), q_b(b), start=True, stop=True)
                last.then_inc(mm_cb, 1)
                one(U_THIRD + 1 + g)

            pe.wait_ge(a_act, 3 * KT)
            for g, (b0, n) in enumerate(GROUPS):
                for kind, x_b in enumerate((k_b, v_b)):
                    if g > 1:
                        pe.wait_ge(tr_read, 2 * (g - 2) + kind + 1)
                    for j in range(n):
                        last = nc.tensor.transpose(ps[2 * (g % 2) + kind][:, j * P:(j + 1) * P], x_b(b0 + j), ident)
                    last.then_inc(mm_tr, 1)
            pe.wait_ge(m_ready, len(GROUPS))
            for g, (b0, n) in enumerate(GROUPS):
                pe.wait_ge(gu0_ready, g + 1)
                if g == 4:
                    pe.wait_ge(tu_ready, 1)
                for j in range(n):
                    last = nc.tensor.transpose(ps[4 + g % 4][:, j * P:(j + 1) * P], gu[:, b0 + j, :], ident)
                last.then_inc(mm_t0, 1)
            pe.wait_ge(tr_read, 2 * len(GROUPS))

            def x_mm(g):
                b0, n = GROUPS[g]
                for j in range(n):
                    last = nc.tensor.matmul(ps[g % 2][:, j * P:(j + 1) * P], bn[:, b0 + j, :], gt[:, b0 + j, :], start=True, stop=True)
                last.then_inc(mm_x, 1)

            def y_mm(l, g, both=True):
                b0, n = GROUPS[g]
                pe.wait_ge(x_ready, (l - 1) * 5 + (g + 1))
                if both:
                    for j in range(n):
                        nc.tensor.matmul(ps[2 + g % 3][:, j * P:(j + 1) * P], gu[:, b0 + j, :], ex[:, b0 + j, :], start=True, stop=True)
                for j in range(n):
                    last = nc.tensor.matmul(ps[5 + g % 3][:, j * P:(j + 1) * P], ex[:, b0 + j, :], gu[:, b0 + j, :], start=True, stop=True)
                last.then_inc(mm_y, 1)

            def level(l, groups, both=True):
                pe.wait_ge(tu_ready, l * 5)
                x_mm(0)
                x_mm(1)
                for g in range(groups):
                    y_mm(l, g, both)
                    if g + 2 < groups:
                        x_mm(g + 2)

            with pe.Fori(1, LEVELS - 1) as l:
                level(l, len(GROUPS))
            level(LEVELS - 1, 4, both=False)

            pe.wait_ge(tu_ready, LEVELS * 5 - 1)
            nc.tensor.matmul(ps[4][:, 0:P], gu[:, MB, :], v_b(MB), start=True, stop=True).then_inc(mm_v0, 1)
            one(U_Z)
            pe.wait_ge(vm_ready, 1)
            for q in range(2):
                nc.tensor.matmul(ps[5 + q][:, :], ktm[:, MB, :], rr[:, 4 * q:4 * q + 4, :], start=True, stop=True).then_inc(mm_s0, 1)
            one(U_Z + 1)
            pe.wait_ge(v0_read, 1)
            nc.tensor.matmul(ps[7][:, 0:P], vn[:, 7, :], ca[:, MB, :], start=True, stop=True).then_inc(mm_o0, 1)
            for c in range(2):
                for q in range(2):
                    pe.wait_ge(s_ready, 2 * c + q + 1)
                    for j in range(4):
                        h = 4 * q + j
                        last = nc.tensor.matmul(ps[4 + q][:, j * P:(j + 1) * P], k_b(2 * h + c), st[:, h, :], start=True, stop=True)
                    last.then_inc(mm_ks, 1)
                one(U_Z + 2 * c + 2)
                for q in range(2):
                    pe.wait_ge(r_ready, 2 * c + q + 1)
                    pe.wait_ge(o_read, 1 if c == 0 else 1 + q + 1)
                    for j in range(4):
                        h = 4 * q + j
                        last = nc.tensor.matmul(ps[6 + q][:, j * P:(j + 1) * P], gu[:, 2 * h + c, :], rr[:, h, :], start=True, stop=True)
                    last.then_inc(mm_vn, 1)
                one(U_Z + 2 * c + 3)
                for q in range(2):
                    pe.wait_ge(vn_ready, 2 * c + q + 1)
                    if c == 0:
                        for j in range(4):
                            h = 4 * q + j
                            last = nc.tensor.matmul(ps[4 + q][:, j * P:(j + 1) * P], ktm[:, 2 * h, :], vn[:, h, :], start=True, stop=True)
                        last.then_inc(mm_ds, 1)
                    for j in range(4):
                        h = 4 * q + j
                        nc.tensor.matmul(ps[6 + q][:, j * P:(j + 1) * P], st[:, h, :], q_b(2 * h + c), start=True, stop=False)
                        last = nc.tensor.matmul(ps[6 + q][:, j * P:(j + 1) * P], vn[:, h, :], ca[:, 2 * h + c, :], start=False, stop=True)
                    last.then_inc(mm_o, 1)
            one(U_Z + 6)

            pe.wait_ge(sq_gdn, 3)
            for b in range(NBLK):
                last = nc.tensor.matmul(ps[7][:, b:b + 1], ex[:, b, :], ones[:, 0:1], start=True, stop=True)
            last.then_inc(mm_norm, 1)
            one(U_Z + 7)
            pe.wait_ge(tiles_read, SLOTS + U_Z + KT)
            pe.wait_ge(cols_ready, 2)
            for g in (4, 0, 1, 2, 3):
                spread([1, 2, 3, 4, 0][g], *GROUPS[g], 12).then_inc(mm_gb, 1)

            def down(name, n):
                t0 = PH[name].first // SLOTS

                def wait_for(h0, upto):
                    def k_wait(k):
                        if h0 + k in upto:
                            pe.wait_ge(hid_ready, HID_AT[name.replace("down", "up")] + h0 + k + 1)
                    return k_wait

                with pe.Fori(t0, t0 + PH[name].units // SLOTS) as t:
                    for s in range(SLOTS):
                        h0 = SLOT_BLOCKS * (s % 2)
                        unit(t, s, SLOT_BLOCKS, n, lambda k: ahi[:, k, 0:n], lambda k: alo[:, k, 0:n], out=ps[s - s % 2][:, 0:n],
                             first=s % 2 == 0, last=s % 2 == 1, k0=h0,
                             k_wait=wait_for(h0, range(FT)) if s < 2 else None)

            def mods(*vectors):
                pe.wait_ge(ada_done, (vectors[-1] + 1) * KT + 1)
                for i in vectors:
                    for m in range(KT):
                        last = nc.tensor.matmul(ps[6][:, KT * i + m:KT * i + m + 1], acc[:, i, m * P:(m + 1) * P], ones[:, 0:1], start=True, stop=True)
                last.then_inc(mods_mm, 1)

            def pe_norm(i, n):
                if i < 4:
                    pe.wait_ge(sum_ready, SUMS_AT[i] + KT)
                    nc.tensor.matmul(ps[4][:, 0:n], cm[:, C_MEAN, :], sums[:, 0:n], start=True, stop=True).then_inc(mean_mm, 1)
                if i in (5, 7):
                    pe.wait_ge(sum_ready, SUMS_AT[i] + KT)
                    nc.tensor.matmul(ps[5][:, 0:n], cm[:, C_MEAN, :], sums[:, 0:n], start=True, stop=True).then_inc(var_mm, 1)
                    return
                for m in range(KT):
                    pe.wait_ge(sq_ready, i * KT + m + 1)
                    last = nc.tensor.matmul(ps[5][:, 0:n], cm[:, C_MEAN, :], sqb[:, m, 0:n], start=m == 0, stop=m == KT - 1)
                last.then_inc(var_mm, 1)

            stream(PH["a_out"], N_A, "gdn")
            pe_norm(0, N_A)
            stream(PH["up0"], N_A, "ln0")
            down("down0", N_F0)
            pe_norm(1, N_F0)
            mods(0, 1, 2)
            stream(PH["b_cx"], N_F0, "ln1")
            stream(PH["b_gate"], N_F0, "ln1")
            t0 = PH["b_out"].first // SLOTS
            with pe.Fori(t0, t0 + 2) as t:
                for s in range(SLOTS):
                    unit(t, s, KT, N_B, lambda k: ahi[:, k, 0:N_B], lambda k: alo[:, k, 0:N_B],
                         k_wait=None if s else lambda k: pe.wait_ge(hid_ready, HID_AT["b_gate"] + k + 1))
            pe_norm(2, N_B)
            mods(3, 4, 5)
            stream(PH["up1"], N_B, "ln2")
            down("down1", N_F1)
            mods(6, 7, 8)
            pe_norm(3, N_F1)

            MIX = PH["mix"]
            M0 = MIX.first // SLOTS
            pe_norm(4, SEQ)
            stream(PH["up2"], SEQ, "rms0")
            down("down2", SEQ)
            pe_norm(5, SEQ)

            def mix_tile(u, version):
                def k_wait(k):
                    if version:
                        pe.wait_ge(rhs_ready, RHS_AT[version] + k + 1)
                    elif k % 2 == 0:
                        pe.wait_ge(y_lo, k // 2 + 1)
                unit(M0 + u // SLOTS, u % SLOTS, KT, SEQ, lambda k: hhi[:, k, 0:SEQ], lambda k: hlo[:, k, 0:SEQ],
                     k_wait=k_wait if u in (0, 40) else None)

            def mix_blocks(u, place, banks_free=None):
                s = u % SLOTS
                pe.wait_ge(lo_split, MIX.first + u + 1)
                if banks_free:
                    banks_free()
                for k in range(KT):
                    out, r_hi, r_lo, m, first, last, done = place(k)
                    w = slice(k * P, k * P + m)
                    nc.tensor.matmul(out, whi[:, s, w], r_hi, start=first, stop=False)
                    nc.tensor.matmul(out, whi[:, s, w], r_lo, start=False, stop=False)
                    ins = nc.tensor.matmul(out, wlo[:, s, w], r_hi, start=False, stop=last)
                    if done is not None and k < KT - 1:
                        ins.then_inc(done, 1)
                ins.then_inc(unit_done, 1)

            for u in range(26):
                if u == 14:
                    for j in range(5):
                        pe.wait_ge(ls_sq, j + 1)
                        at_ = 0 if j < 3 else SEQ
                        last = nc.tensor.matmul(ps[4][:, at_:at_ + SEQ], ones, lsq[:, j, :], start=j in (0, 3), stop=j in (2, 4))
                    last.then_inc(lat_mm, 1)
                mix_tile(u, "rms1")

            pe.wait_ge(ld_dft, 16)
            pe.wait_ge(tiles_read, SLOTS + MIX.first + 10)
            for j in range(4):
                for g in (2 * (j % 2), 2 * (j % 2) + 1):
                    if j == 0 and g == 0:
                        pe.wait_ge(lat_y, 5)
                    last = nc.tensor.matmul(ps[4 + j][:, (g % 2) * SEQ:(g % 2 + 1) * SEQ], uf[:, g, (j // 2) * P:(j // 2 + 1) * P], dft[:, 0, :], start=True, stop=True)
                last.then_inc(four1, 1)
            pe.wait_ge(tiles_read, SLOTS + MIX.first + 26)
            pe.wait_ge(pf_ready, 4)
            for g in range(4):
                for c in range(2):
                    nc.tensor.matmul(ps[g][:, 0:SEQ], pf[:, c, g, 0:P], dft[:, 1 + c, :], start=c == 0, stop=False)
                    last = nc.tensor.matmul(ps[g][:, 0:SEQ], pf[:, c, g, P:2 * P], dft[:, 3 + c, :], start=False, stop=c == 1)
                last.then_inc(four2, 1)

            pe.wait_ge(lat_ready, 5)

            def q_place(u):
                def place(k):
                    b = (u - 26) * KT + k
                    h, kt = b // 3, b % 3
                    return (ps[4 + h // 2][0:96, (h % 2) * SEQ:(h % 2 + 1) * SEQ], lhi[:, kt, :], llo[:, kt, :], 96, kt == 0, kt == 2, q_mm if kt == 2 else None)
                return place

            def k_place(u):
                def place(k):
                    b = (u - 29) * KT + k
                    h, kt = b // 2, b % 2
                    return (ps[h // 2][:, (h % 2) * SEQ:(h % 2 + 1) * SEQ], lhi[:, 3 + kt, :], llo[:, 3 + kt, :], P, kt == 0, kt == 1, k_mm if kt == 1 else None)
                return place

            for u in range(26, 29):
                mix_blocks(u, q_place(u))
            for u in range(29, 31):
                mix_blocks(u, k_place(u), lambda: pe.wait_ge(f_ready, 4))
            pe.wait_ge(lo_split, MIX.first + 32)
            s = 31 % SLOTS
            for c in range(2):
                pe.wait_ge(q_read, c + 1)
                out = ps[4 + c][:, :]
                cc = slice(c * P, (c + 1) * P)
                for kt in range(2):
                    w = slice(kt * 512, (kt + 1) * 512)
                    nc.tensor.matmul(out, lhi[:, 3 + kt, cc], whi[:, s, w], start=kt == 0, stop=False)
                    nc.tensor.matmul(out, llo[:, 3 + kt, cc], whi[:, s, w], start=False, stop=False)
                    last = nc.tensor.matmul(out, lhi[:, 3 + kt, cc], wlo[:, s, w], start=False, stop=kt == 1)
                if c == 0:
                    last.then_inc(v_mm, 1)
            last.then_inc(unit_done, 1)

            def out_place(u, r_hi, r_lo):
                def place(k):
                    kt = k % 4
                    return (ps[u % SLOTS][:, (k // 4) * SEQ:(k // 4 + 1) * SEQ], r_hi[:, kt, :], r_lo[:, kt, :], P, kt == 0, kt == 3, None)
                return place

            pe.wait_ge(k_read, 4)
            for u in range(32, 36):
                mix_blocks(u, out_place(u, fhi, flo), lambda: pe.wait_ge(tiles_read, SLOTS + MIX.first + 32))

            pe.wait_ge(v_read, 2)
            pe.wait_ge(tiles_read, SLOTS + MIX.first + 36)
            for h in range(HEADS + 2):
                if h < HEADS:
                    pe.wait_ge(rope_ready, h // 4 + 1)
                    if h >= 2:
                        pe.wait_ge(p_exp, h - 1)
                    for c in range(2):
                        last = nc.tensor.matmul(ps[4 + h % 2][:, c * SEQ:(c + 1) * SEQ], qt[0:96, h, c * P:(c + 1) * P], kt_[0:96, h, :], start=True, stop=True)
                    last.then_inc(s_mm, 1)
                if 0 <= h - 1 < HEADS:
                    g = h - 1
                    pe.wait_ge(p_ready, g + 1)
                    if g >= 2:
                        pe.wait_ge(t_read, g - 1)
                    for kc in range(2):
                        for c in range(2):
                            last = nc.tensor.transpose(ps[6 + g % 2][:, kc * SEQ + c * P:kc * SEQ + (c + 1) * P], pr[:, g % 2, c, kc * P:(kc + 1) * P], ident)
                    last.then_inc(t_mm, 1)
                if h >= 2:
                    g = h - 2
                    pe.wait_ge(t_read, g + 1)
                    half = (g % 2) * 64
                    for kc in range(2):
                        last = nc.tensor.matmul(ps[g // 2][half:half + 64, 0:SEQ], vt[:, kc, g * 64:(g + 1) * 64], pt[:, g % 2, kc, :], start=kc == 0, stop=kc == 1)
                    last.then_inc(o_mm, 1)
            pe.wait_ge(o_ready, 4)
            for u in range(36, 40):
                mix_blocks(u, out_place(u, ohi, olo))
            for u in range(40, 48):
                mix_tile(u, None)
            pe_norm(6, SEQ)
            stream(PH["up3"], SEQ, "rms2")
            down("down3", SEQ)
            pe_norm(7, SEQ)


def constants():
    i, j = np.arange(P)[:, None], np.arange(P)[None, :]
    same = i // META == j // META
    out = [i == j, np.full((P, P), 1.0 / D), np.ones((P, P)), i <= j, same & (i <= j), same]
    out.append(-1.0 * ((i >> 1 == j >> 1) & (i < j)))
    for l in range(1, LEVELS):
        out.append(-1.0 * ((i >> (l + 1) == j >> (l + 1)) & (i >> l & 1 == 1) & (j >> l & 1 == 0)))
    return np.ascontiguousarray(np.stack(out, 1).astype(np.float32))


def blocks_of(w):
    k, n = w.shape
    return w.reshape(k // P, P, n // P, P).transpose(2, 1, 0, 3).reshape(n // P, P, k)


def pairs_of(a, b):
    return np.stack([blocks_of(a), blocks_of(b)], 1).reshape(-1, P, a.shape[0])


def halves_of(w):
    n = w.shape[1] // P
    return blocks_of(w).reshape(n, P, 2, SLOT_BLOCKS * P).transpose(0, 2, 1, 3).reshape(2 * n, P, SLOT_BLOCKS * P)


def lay_out(a):
    f = {}
    x = np.concatenate([a["meta"], a["x"][0]], 0)
    f["x"] = x.T.reshape(KT, P, TOK).transpose(1, 0, 2)
    w = a["a_w_in"][0]
    q, k, v, z, ba = (w[:, 0:1024], w[:, 1024:2048], w[:, 2048:3072], w[:, 3072:4096], w[:, 4096:])
    f["w_a_in"] = np.concatenate([blocks_of(m) for m in (k, q, v, z)])
    f["w_ab"] = ba.reshape(KT, P, 16).transpose(1, 0, 2)
    f["w_a_out"] = blocks_of(a["a_w_out"][0])
    b, c, xv = np.split(a["b_w_in"][0], 3, axis=1)
    f["w_b_cx"] = pairs_of(c, xv)
    f["w_b_gate"] = blocks_of(b)
    f["w_b_out"] = blocks_of(a["b_w_out"][0])
    for l in range(2):
        u, g = np.split(a["ffn_w_up"][l], 2, axis=1)
        f[f"w_up{l}"] = pairs_of(u, g)
        f[f"w_down{l}"] = halves_of(a["ffn_w_down"][l])
    for l, n in ((2, "ffn1"), (3, "ffn2")):
        f[f"w_up{l}"] = pairs_of(a[n + "_w_gate_2"][0], a[n + "_w_up_2"][0])
        f[f"w_down{l}"] = halves_of(a[n + "_w_down_2"][0])
    f["ada_w"] = a["ada_w_2"][0].reshape(KT, P, 9, D).transpose(2, 0, 1, 3).reshape(ADA_OPS, P, D)

    vec = np.zeros((P, N_VEC), np.float32)
    conv = a["a_conv"][0]
    kqv = np.concatenate([conv[:, 1024:2048], conv[:, 0:1024], conv[:, 2048:]], 1)
    vec[:, V_ACONV:V_ACONV + 96] = kqv.reshape(4, 24, P).transpose(2, 1, 0).reshape(P, 96)
    vec[:, V_FCONV:V_FCONV + 132] = a["ffn_conv"].reshape(2, 3, FT, P).transpose(3, 0, 2, 1).reshape(P, 132)
    vec[:, V_BCONV:V_BCONV + 24] = a["b_conv"][0].reshape(3, KT, P).transpose(2, 1, 0).reshape(P, 24)
    ln = np.stack([a["ln_mix_g"], a["ln_mix_b"], a["ln_ffn_g"], a["ln_ffn_b"]], 1)
    vec[:, V_LN:V_LN + 64] = ln.reshape(8 * KT, P).T
    vec[:, V_ANORM] = a["a_norm"][0]
    rows = np.arange(P) // META
    for at_, v_ in ((V_ALOG, a["a_log"][0]), (V_DT, a["a_dt_bias"][0])):
        vec[:, at_:at_ + MB] = np.repeat(v_, 2)[None]
        vec[:, at_ + MB] = v_[rows]
    vec[:, V_HEAD:V_HEAD + HEADS] = rows[:, None] == np.arange(HEADS)[None]
    vec[:, V_C:V_C + KT] = a["c_2"].reshape(KT, P).T
    vec[:, V_ADAB:V_ADAB + 72] = a["ada_b_2"][0].reshape(72, P).T
    norms = np.stack([a["ffn1_norm_2"][0], a["mix_norm_2"][0], a["ffn2_norm_2"][0], a["final_norm_2"]])
    vec[:, V_NORM:V_NORM + 32] = norms.reshape(32, P).T
    vec[:, V_QN:V_QN + 3] = a["q_norm_2"][0].reshape(3, P).T
    vec[:, V_KVN:V_KVN + 2] = a["kv_norm_2"][0].reshape(2, P).T
    f["vec"] = vec
    f["cm"] = constants()
    mixing_layout(a, f)
    return {k_: np.ascontiguousarray(v_) for k_, v_ in f.items()}


def mixing_layout(a, f):
    w = a["w_in_2"][0]
    u_f, q_lat, kv_lat, k_rope, gate = np.split(w, [512, 896, 1152, 1184], axis=1)
    rope = np.zeros((D, P), np.float32)
    rope[:, 64:96] = k_rope
    q_up = a["w_q_up_2"][0].reshape(3, P, HEADS, 96)
    q_blk = np.zeros((HEADS, 3, P, P), np.float32)
    q_blk[..., 0:96] = q_up.transpose(2, 0, 1, 3)
    kv = a["w_kv_up_2"][0].reshape(2, P, HEADS, P)
    k_blk = kv.transpose(2, 0, 1, 3)
    v_blk = kv[..., 64:].reshape(2, P, 4, P).transpose(0, 2, 1, 3)

    def units(blk):
        return blk.reshape(-1, KT, P, P).transpose(0, 2, 1, 3).reshape(-1, P, KT * P)

    def out_blocks(m):
        return m.reshape(4, P, KT, P).transpose(2, 0, 1, 3)

    f["w_mix"] = np.concatenate([
        blocks_of(rope), blocks_of(q_lat), blocks_of(kv_lat), blocks_of(u_f), blocks_of(gate),
        units(q_blk), units(k_blk), units(v_blk),
        units(out_blocks(a["w_fourier_out_2"][0])), units(out_blocks(a["w_mla_out_2"][0])),
        blocks_of(a["w_out_2"][0]),
    ])
    f["pos"] = np.tile(a["positions_2"].astype(np.int32), (32, 1))
    d, s = np.arange(P), np.arange(SEQ)
    fd = 2 * np.pi * (d[:, None] * d[None] % P) / P
    fs = 2 * np.pi * (s[:, None] * s[None] % SEQ) / SEQ
    f["dft"] = np.stack([
        np.concatenate([np.cos(fd), np.sin(fd)], 1) / np.sqrt(P),
        *(np.cos(fs) / np.sqrt(SEQ)).reshape(2, P, SEQ), *(-np.sin(fs) / np.sqrt(SEQ)).reshape(2, P, SEQ),
    ], 1).astype(np.float32)
    inv = 1.0 / (np.float32(10000.0) ** (np.arange(16, dtype=np.float32) * np.float32(2.0) / np.float32(32)))
    f["vec"][64:96, V_INVF] = np.tile(inv.astype(np.float32), 2)
    f["vec"][64:80, V_SIGN] = -1.0
    f["vec"][80:96, V_SIGN] = 1.0
    f["vec"][:, V_QN:V_QN + 3] = a["q_norm_2"][0].reshape(3, P).T
    f["vec"][:, V_KVN:V_KVN + 2] = a["kv_norm_2"][0].reshape(2, P).T


def kernel(**inputs):
    import concourse.bacc as bacc
    from concourse.bass_utils import run_bass_kernel_spmd

    arrays = lay_out({k: np.asarray(v) for k, v in inputs.items()})
    nc = bacc.Bacc("TRN2", target_bir_lowering=False, num_devices=1)
    io = {n: nc.dram_tensor("in_" + n, v.shape, mybir.dt.from_np(v.dtype), kind="ExternalInput").ap() for n, v in arrays.items()}
    io["out"] = nc.dram_tensor("out", (P, KT, SEQ), F32, kind="ExternalOutput").ap()
    build(nc, io)
    r = run_bass_kernel_spmd(nc, [{"in_" + n: v for n, v in arrays.items()}], core_ids=[0])
    out = r.results[0]["out"]
    return np.ascontiguousarray(out.transpose(2, 1, 0)).reshape(1, SEQ, D)
```

```python
from contextlib import ExitStack

import numpy as np

import concourse.bass as bass
from concourse import mybir

F32 = mybir.dt.float32
F32R = mybir.dt.float32r
I32 = mybir.dt.int32
ALU = mybir.AluOpType
ACT = mybir.ActivationFunctionType
AX = mybir.AxisListType

P = 128
D = 1024
KT = D // P
SEQ = 256
META = 16
TOK = SEQ + META
D_FF = 2816
FT = D_FF // P
HEADS = 8
NBLK = 2 * HEADS + 1
MB = NBLK - 1
GROUPS = [(0, 4), (4, 4), (8, 4), (12, 4), (16, 1)]
ALPHA = (2.0 * 2) ** 0.25
LN_EPS, RMS_EPS, L2_EPS, NORM_EPS = 1e-5, 1e-6, 1e-6, 1e-6
SM_SCALE = 96 ** -0.5
PI_IN = float(np.nextafter(np.float32(np.pi), np.float32(0)))
TWO_PI = (6.28125, 0.0019350051879882812, 3.019916050e-7)
LEVELS = 7

N_A = 262
N_F0 = 260
N_B = 258
N_F1 = 256

SLOTS = 4
SLOT_BLOCKS = FT // 2

U_V, U_Z = 2 * KT, 3 * KT
U_FIRST, U_NEXT = (U_V, U_V + 1, U_V + 2), U_V + 3


class Phase:

    def __init__(self, name, first, units, blocks):
        self.name, self.first, self.units, self.blocks = name, first, units, blocks


def plan():
    first, out = 0, []
    for name, units, blocks in [
        ("a_in", 32, KT), ("a_out", 8, KT), ("up0", 2 * FT, KT), ("down0", 16, SLOT_BLOCKS),
        ("b_cx", 16, KT), ("b_gate", 8, KT), ("b_out", 8, KT), ("up1", 2 * FT, KT), ("down1", 16, SLOT_BLOCKS),
        ("up2", 2 * FT, KT), ("down2", 16, SLOT_BLOCKS), ("mix", 48, KT),
        ("up3", 2 * FT, KT), ("down3", 16, SLOT_BLOCKS),
    ]:
        out.append(Phase(name, first, units, blocks))
        first += units
    return out


PHASES = plan()
PH = {p.name: p for p in PHASES}
UNITS = PHASES[-1].first + PHASES[-1].units
BLOCKS_AFTER = {p.name: q.blocks for p, q in zip(PHASES, PHASES[1:])}
ADA_OPS = 9 * KT
ADA_AT = {"up0": 0, "down0": FT, "b_cx": FT + 16, "b_gate": FT + 24, "up1": FT + 28}
CONV_AT = {"up0": 0, "b_cx": FT, "up1": FT + KT}
GATE_AT = {"up0": 0, "up1": FT, "up2": 2 * FT, "up3": 3 * FT}
LATE_AT = {"up2": 0, "up3": FT}
Y_AT = {0: 0, 1: KT, 2: 2 * KT, 3: 3 * KT, 5: 4 * KT, 7: 5 * KT}
N_SH = SEQ + 2
HID_AT = {"up0": 0, "b_gate": FT, "up1": FT + KT, "up2": 2 * FT + KT, "up3": 3 * FT + KT}
SUMS_AT = {i: i * KT for i in range(8)}

X_LAT, X_UF, X_GA, X_Q, X_K, X_V, X_GB, X_GC, X_FO, X_MO, X_OUT = 1, 6, 10, 14, 17, 19, 20, 28, 32, 36, 40
RHS_AT = {"x": 0, "gdn": 8, "ln0": 16, "ln1": 24, "ln2": 32, "rms0": 40, "rms1": 48, "rms2": 56}

C_IDENT, C_MEAN, C_ONES, C_CAUSAL, C_CAUSAL_META, C_SAME_META, C_LEVEL = range(7)
C_PAIR = C_LEVEL
N_CONST = C_LEVEL + LEVELS

_at = 0


def _place(n):
    global _at
    _at += n
    return _at - n


V_ACONV = _place(24 * 4)
V_FCONV = _place(2 * FT * 3)
V_BCONV = _place(KT * 3)
V_LN = _place(8 * KT)
V_ANORM = _place(1)
V_ALOG = _place(NBLK)
V_DT = _place(NBLK)
V_HEAD = _place(HEADS)
V_C = _place(KT)
V_ADAB = _place(9 * KT)
V_NORM = _place(4 * KT)
V_QN = _place(3)
V_KVN = _place(2)
V_INVF = _place(1)
V_SIGN = _place(1)
N_VEC = _at


def build(nc, io):
    ctx = ExitStack()
    with ctx:
        sem = lambda name: ctx.enter_context(nc.semaphore(name))

        base = (nc.sbuf_base + 63) // 32 * 32
        spot = [base]

        def at(name, shape, dt, offset):
            return nc.alloc_sbuf_tensor_at(name, shape, dt, offset=offset)

        def new(name, shape, dt=F32):
            size = int(np.prod(shape[1:])) * 4
            spot[0] += (size + 31) // 32 * 32
            return at(name, shape, dt, spot[0] - (size + 31) // 32 * 32)

        raw = new("raw", [P, SLOTS, SLOT_BLOCKS * P])
        whi = new("whi", [P, SLOTS, SLOT_BLOCKS * P], F32R)
        wlo = new("wlo", [P, SLOTS, SLOT_BLOCKS * P], F32R)
        hf = new("hf", [P, KT, TOK])
        xb_at = spot[0]
        xb = new("xb", [P, KT, TOK])
        hhi = new("hhi", [P, KT, TOK], F32R)
        hlo_at = spot[0]
        hlo = new("hlo", [P, KT, TOK], F32R)
        sqb = at("sqb", [P, KT, TOK], F32, hlo_at)
        arena = spot[0]
        ahi = new("ahi", [P, FT, N_F0], F32R)
        alo = new("alo", [P, FT, N_F0], F32R)
        acc = new("acc", [P, 9, D])
        ring_at = spot[0]
        ring = new("ring", [P, 2, D])
        tb = new("tb", [P, 2, TOK])
        ab = new("ab", [P, 2, TOK])
        sb = new("sb", [P, 2, TOK])
        cm = new("cm", [P, N_CONST, P])
        vec = new("vec", [P, N_VEC])
        small = new("small", [P, 512])
        small_end = spot[0]
        spot[0] += 2 * SEQ * 4
        assert spot[0] <= nc.sbuf_usable_end, spot[0]

        spot[0] = arena
        kvq = new("kvq", [P, 24 * 2 * P])
        kvqm = new("kvqm", [P, 24 * META])
        zs = new("zs", [P, HEADS, N_A])
        gt = new("gt", [P, NBLK, P])
        bn = new("bn", [P, NBLK, P])
        ex = new("ex", [P, NBLK, P])
        ca = new("ca", [P, NBLK, P])
        gu = new("gu", [P, NBLK, P])
        st = new("st", [P, HEADS, P])
        assert spot[0] <= ring_at
        ktm = at("ktm", [P, NBLK, P], F32, xb_at)
        ot = gt
        rr = at("rr", [P, HEADS, P], F32, ring_at)
        vn = at("vn", [P, HEADS, P], F32, ring_at + HEADS * P * 4)
        wab = at("wab", [P, KT, 2 * HEADS], F32, ring_at)
        never = at("never", [P, 2, P], F32, ring_at + 4096)
        abt = at("abt", [P, TOK], F32, ring_at + 1024)
        abm = at("abm", [P, P], F32, ring_at + 1024 + TOK * 4)

        spot[0] = arena
        krot = new("krot", [P, SEQ])
        lat = new("lat", [P, 5, SEQ])
        uf = new("uf", [P, 4, SEQ])
        dft = new("dft", [P, 5, SEQ])
        gates = new("gates", [P, 16, SEQ])
        lhi = new("lhi", [P, 5, SEQ], F32R)
        llo = new("llo", [P, 5, SEQ], F32R)
        qt = new("qt", [P, HEADS, SEQ])
        kt_ = new("kt", [P, HEADS, SEQ])
        vt = new("vt", [P, 2, 512])
        pf = new("pf", [P, 2, 4, SEQ])
        rot = at("rot", [P, HEADS, SEQ], F32, ring_at)
        lsq = at("lsq", [P, 5, SEQ], F32, spot[0])
        fhi = new("fhi", [P, 4, SEQ], F32R)
        flo = new("flo", [P, 4, SEQ], F32R)
        assert spot[0] <= ring_at - SEQ * 4, (spot[0], ring_at)
        rt = at("rt", [P, SEQ], F32, ring_at - SEQ * 4)
        spot[0] = arena + SEQ * 4
        ohi = new("ohi", [P, 4, SEQ], F32R)
        olo = new("olo", [P, 4, SEQ], F32R)
        pr = at("pr", [P, 2, 2, SEQ], F32, ring_at)
        pt = at("pt", [P, 2, 2, SEQ], F32, ring_at + 4 * SEQ * 4)
        outb = at("outb", [P, KT, SEQ], F32, arena)
        cs = at("cs", [P, 2, SEQ], F32, small_end)
        pos = at("pos", [P, SEQ], I32, small_end)

        ps = [ctx.enter_context(nc.psum_tensor(f"ps{i}", [P, 512], F32)) for i in range(8)]

        raw_loaded = [sem(f"raw_loaded{s}") for s in range(SLOTS)]
        hi_split = sem("hi_split")
        lo_split = sem("lo_split")
        unit_done = sem("unit_done")
        tiles_read = sem("tiles_read")
        ld_x, ld_small, ld_cm, ld_ada = sem("ld_x"), sem("ld_small"), sem("ld_cm"), [sem("ld_ada0"), sem("ld_ada1")]
        ada_done = sem("ada_done")
        rhs_hi, rhs_ready = sem("rhs_hi"), sem("rhs_ready")
        a_tap, a_conv, a_act = sem("a_tap"), sem("a_conv"), sem("a_act")
        f_tap, f_conv, f_gate, hid_hi, hid_ready = sem("f_tap"), sem("f_conv"), sem("f_gate"), sem("hid_hi"), sem("hid_ready")
        mean_mm, xc_ready, sq_ready, var_mm, y_ready, hf_ready = (sem(n) for n in ("mean_mm", "xc_ready", "sq_ready", "var_mm", "y_ready", "hf_ready"))
        sum_ready, guess_ready, eps_ready = sem("sum_ready"), sem("guess_ready"), sem("eps_ready")
        dve_step, act_step = sem("dve_step"), sem("act_step")
        out_done = sem("out_done")

        sums = sb[:, 1, :]
        ident = cm[:, C_IDENT, :]
        ones = cm[:, C_ONES, :]

        mm_ab, ab_ready, mm_gate, g_dve, g_act, gl_ready, mm_cum = (sem(n) for n in ("mm_ab", "ab_ready", "mm_gate", "g_dve", "g_act", "gl_ready", "mm_cum"))
        sq_gdn, mm_norm, cols_ready, d_diff, d_exp, m_ready = (sem(n) for n in ("sq_gdn", "mm_norm", "cols_ready", "d_diff", "d_exp", "m_ready"))
        mm_gb, mm_cb, mm_tr, tr_read, mm_x, x_ready, mm_y, tu_ready, gu0_ready, mm_t0, qg_ready = (sem(n) for n in ("mm_gb", "mm_cb", "mm_tr", "tr_read", "mm_x", "x_ready", "mm_y", "tu_ready", "gu0_ready", "mm_t0", "qg_ready"))
        mm_v0, v0_read, vm_ready, mm_s0, mm_o0, s_ready = (sem(n) for n in ("mm_v0", "v0_read", "vm_ready", "mm_s0", "mm_o0", "s_ready"))
        mm_ks, r_ready, mm_vn, vn_ready, mm_ds, mm_o, o_read, og_ready = (sem(n) for n in ("mm_ks", "r_ready", "mm_vn", "vn_ready", "mm_ds", "mm_o", "o_read", "og_ready"))
        mods_mm, mods_ready, ls_sq, lat_mm, lat_y, lat_hi, lat_ready = (sem(n) for n in ("mods_mm", "mods_ready", "ls_sq", "lat_mm", "lat_y", "lat_hi", "lat_ready"))
        four1, pf_ready, four2, f_hi, f_ready = (sem(n) for n in ("four1", "pf_ready", "four2", "f_hi", "f_ready"))
        q_mm, q_read, k_mm, k_read, v_mm, v_read = (sem(n) for n in ("q_mm", "q_read", "k_mm", "k_read", "v_mm", "v_read"))
        rope_ready, s_mm, m_ready2, p_exp, p_ready, t_mm, t_read, o_mm, o_hi, o_ready, gates_ready, lat_v, lat_guess, late_g, late_u = (sem(n) for n in ("rope_ready", "s_mm", "m_ready2", "p_exp", "p_ready", "t_mm", "t_read", "o_mm", "o_hi", "o_ready", "gates_ready", "lat_v", "lat_guess", "late_g", "late_u"))
        ld_dft, ang_ready, cs_ready, y_hi, y_lo = (sem(n) for n in ("ld_dft", "ang_ready", "cs_ready", "y_hi", "y_lo"))
        c_ready, b_tap = sem("c_ready"), sem("b_tap")
        ogb = at("ogb", [P, HEADS, N_A], F32, arena)

        def wide(x):
            return x[:].rearrange("p a n -> p (a n)")[:, 0:2 * SEQ]

        def col(i):
            return vec[:, bass.ds(i, 1)]

        def eps_of(eps):
            c = 316 + (eps == RMS_EPS)
            return small[:, c:c + 1]

        def ln_shift(i):
            return lambda m: col(V_LN + (2 * i + 1) * KT + m)

        def ln_gain(i):
            return lambda m: col(V_LN + 2 * i * KT + m)

        def shifts(i):
            return small[:, 3 * KT * i:3 * KT * i + KT].unsqueeze(2).to_broadcast([P, KT, 2])

        def a_of(i):
            return lambda m: small[:, 72 + KT * i + m:73 + KT * i + m]

        def sh_of(i):
            return lambda m: small[:, 3 * KT * i + m:3 * KT * i + m + 1]

        def blocks_at(kind, b0, n):
            at_ = kind * MB * P + b0 * P
            return kvq[:, at_:at_ + n * P] if b0 < MB else kvqm[:, kind * P:(kind + 1) * P]

        def S_(i):
            return small[:, i * NBLK:(i + 1) * NBLK]


        def split_hi(act, t, s, blocks):
            if not blocks:
                return
            act.wait_ge(raw_loaded[s], t * 16 + 16)
            if not isinstance(t, int) or t:
                act.wait_ge(unit_done, t * SLOTS + (s + 1 - SLOTS))
            nc.scalar.activation(whi[:, s, 0:blocks * P], raw[:, s, 0:blocks * P], ACT.Copy).then_inc(hi_split, 1)

        def split_lo(dve, t, s, blocks):
            if not blocks:
                return
            dve.wait_ge(hi_split, t * SLOTS + (s + 1))
            nc.vector.tensor_tensor(wlo[:, s, 0:blocks * P], raw[:, s, 0:blocks * P],
                                    whi[:, s, 0:blocks * P], ALU.subtract).then_inc(lo_split, 1)

        def steps(eng, phase, body):
            t0, n = phase.first // SLOTS, phase.units // SLOTS
            after = BLOCKS_AFTER.get(phase.name, 0)
            whole = n if after == phase.blocks else n - 1
            with eng.Fori(0, whole) as i:
                body(i + t0, i, phase.blocks)
            if whole < n:
                body(n - 1 + t0, n - 1, after)

        def bcast(row, n):
            return row.unsqueeze(1).to_broadcast([P, n, row.shape[-1]])

        class Steps:

            def __init__(self, eng, s):
                self.eng, self.s, self.n = eng, s, 0

            def __call__(self, instruction):
                instruction.then_inc(self.s, 1)
                self.n += 1
                return self.n

            def after(self, n=None):
                self.eng.wait_ge(self.s, self.n if n is None else n)


        block = ctx.enter_context(nc.Block())

        @block.sync
        def _(sp):
            sp.dma_start(vec[:], io["vec"]).then_inc(ld_small, 16)
            sp.dma_start(pos[64:96, :], io["pos"]).then_inc(ld_small, 16)
            sp.dma_start(wab[:], io["w_ab"]).then_inc(ld_small, 16)
            for k in range(KT):
                sp.dma_start(hf[:, k, :], io["x"][:, k, :]).then_inc(ld_x, 16)

            def load(p, t, i):
                for s in range(SLOTS):
                    if not isinstance(t, int) or t:
                        sp.wait_ge(lo_split, t * SLOTS + (s + 1 - SLOTS))
                    sp.dma_start(raw[:, s, 0:p.blocks * P], io["w_" + p.name][i * SLOTS + s]).then_inc(raw_loaded[s], 16)

            for p in PHASES:
                t0, n = p.first // SLOTS, p.units // SLOTS
                begin = 0
                if p.first == 0:
                    load(p, 0, 0)
                    sp.dma_start(cm[:], io["cm"]).then_inc(ld_cm, 16)
                    begin = 1
                with sp.Fori(begin, n) as i:
                    load(p, i + t0, i)
            for m in range(KT):
                sp.wait_ge(y_ready, Y_AT[7] + m + 1)
                sp.dma_start(io["out"][:, m, :], outb[:, m, :]).then_inc(out_done, 16)
            sp.wait_ge(out_done, 16 * KT)

        @block.gpsimd
        def _(pool):
            for g, (b0, n) in enumerate(GROUPS):
                pool.wait_ge(mm_cb, g + 1)
                pool.wait_ge(d_exp, 2 * g + 2)
                q_ = blocks_at(1, b0, n)
                nc.gpsimd.tensor_tensor(q_, q_, gt[:, b0:b0 + n, :].rearrange("p b t -> p (b t)"), ALU.mult).then_inc(qg_ready, 1)
            pool.wait_ge(tiles_read, 4 + PH["up0"].first)
            nc.gpsimd.memset(acc[:], 0.0).then_inc(ada_done, 1)
            for o in range(2):
                pool.dma_start(ring[:, o, :], io["ada_w"][o]).then_inc(ld_ada[o], 16)
            with pool.Fori(1, ADA_OPS // 2) as i:
                for o in range(2):
                    pool.wait_ge(ada_done, i * 2 + o)
                    pool.dma_start(ring[:, o, :], io["ada_w"][i * 2 + o]).then_inc(ld_ada[o], 16)
            pool.wait_ge(tiles_read, SLOTS + PH["mix"].first)
            pool.dma_start(dft[:], io["dft"]).then_inc(ld_dft, 16)

        @block.scalar
        def _(act):
            mine = Steps(act, act_step)

            def rhs_round(version, k, src, n):
                nc.scalar.activation(hhi[:, k, 0:n], src, ACT.Copy).then_inc(rhs_hi, 1)

            act.wait_ge(ang_ready, 1)
            nc.scalar.activation(cs[64:96, 1, :], tb[64:96, 1, 0:SEQ], ACT.Sin)
            nc.scalar.activation(cs[64:96, 0, :], ab[64:96, 1, 0:SEQ], ACT.Sin).then_inc(cs_ready, 1)
            for k in range(KT):
                act.wait_ge(ld_x, 16 * KT)
                rhs_round("x", k, hf[:, k, :], TOK)
            for s in range(SLOTS):
                split_hi(act, 0, s, KT)

            def a_silu(u, p):
                act.wait_ge(tiles_read, u + (SLOTS + 1))
                nc.scalar.activation(kvq[:, bass.ds(u * 256, 256)], tb[:, p, META:TOK], ACT.Silu)
                nc.scalar.activation(kvqm[:, bass.ds(u * META, META)], tb[:, p, 0:META], ACT.Silu).then_inc(a_act, 1)

            def a_kvq(i, before=True):
                for s in range(SLOTS):
                    u = i * SLOTS + s
                    act.wait_ge(unit_done, u + 1)
                    if s > 1 or before:
                        act.wait_ge(a_act, u - 1)
                    nc.scalar.activation(tb[:, s % 2, :], ps[s][:, 0:TOK], ACT.Copy,
                                         scale=col(u * 4 + (V_ACONV + 3))).then_inc(a_tap, 1)
                    if s or before:
                        a_silu(u - 1, (s - 1) % 2)
                    split_hi(act, i + 1, s, KT)

            a_kvq(0, before=False)
            act.wait_ge(g_dve, 1)
            nc.scalar.activation(S_(4), S_(3), ACT.Exp, scale=-1.0).then_inc(g_act, 1)
            nc.scalar.activation(S_(5), S_(1), ACT.Exp, scale=-1.0).then_inc(g_act, 1)
            nc.scalar.activation(S_(6), vec[:, V_ALOG:V_ALOG + NBLK], ACT.Exp).then_inc(g_act, 1)
            act.wait_ge(g_act, 1)
            nc.scalar.activation(S_(4), S_(4), ACT.Ln, bias=1.0).then_inc(g_act, 1)
            a_kvq(1)
            act.wait_ge(g_dve, 2)
            nc.scalar.activation(S_(9), S_(7), ACT.Exp).then_inc(g_act, 1)
            nc.scalar.activation(S_(10), S_(10), ACT.Exp).then_inc(g_act, 1)
            nc.scalar.activation(S_(11), S_(8), ACT.Exp).then_inc(g_act, 1)

            with act.Fori(2, U_V // SLOTS) as i:
                a_kvq(i)
            a_silu(U_V - 1, 1)

            act.wait_ge(a_act, U_V)
            for kind, dst in enumerate((ex, ca)):
                nc.scalar.activation(dst[:, 0:MB, :], blocks_at(kind, 0, MB).rearrange("p (b t) -> p b t", t=P), ACT.Square)
                nc.scalar.activation(dst[:, MB, :], blocks_at(kind, MB, 1), ACT.Square).then_inc(sq_gdn, 1)

            def a_v(u):
                s = u % SLOTS
                act.wait_ge(unit_done, u + 1)
                nc.scalar.activation(tb[:, s % 2, :], ps[s][:, 0:TOK], ACT.Copy, scale=col(u * 4 + (V_ACONV + 3))).then_inc(a_tap, 1)
                split_hi(act, u // SLOTS + 1, s, KT)

            for u in (*U_FIRST, U_NEXT):
                a_v(u)
                a_silu(u, u % 2)
            for g, (b0, n) in enumerate(GROUPS):
                act.wait_ge(d_diff, g + 1)
                nc.scalar.activation(ex[:, b0:b0 + n, :], ex[:, b0:b0 + n, :], ACT.Exp).then_inc(d_exp, 1)
                nc.scalar.activation(gt[:, b0:b0 + n, :], ps[4][:, 0:n * P].rearrange("p (b t) -> p b t", t=P), ACT.Exp).then_inc(d_exp, 1)
                if g < 4:
                    u = U_NEXT + 1 + g
                    a_v(u)
                    a_silu(u, u % 2)

            for g, (b0, n) in enumerate(GROUPS):
                for kind, (dst, scales) in enumerate([(lambda b: ktm[:, b, :], 15), (lambda b: blocks_at(2, b, 1), 2)]):
                    act.wait_ge(mm_tr, 2 * g + kind + 1)
                    for j in range(n):
                        last = nc.scalar.activation(dst(b0 + j), ps[2 * (g % 2) + kind][:, j * P:(j + 1) * P], ACT.Copy,
                                                    scale=S_(scales)[:, b0 + j:b0 + j + 1])
                    last.then_inc(tr_read, 1)
            act.wait_ge(qg_ready, len(GROUPS))
            for g, (b0, n) in enumerate(GROUPS):
                act.wait_ge(mm_t0, g + 1)
                nc.scalar.activation(gt[:, b0:b0 + n, :], ps[4 + g % 4][:, 0:n * P].rearrange("p (b t) -> p b t", t=P), ACT.Copy).then_inc(tu_ready, 1)

            def a_z(u):
                s = u % SLOTS
                act.wait_ge(unit_done, u + 1)
                nc.scalar.activation(zs[:, u - U_Z, :], ps[s][:, TOK - N_A:TOK], ACT.Silu).then_inc(tiles_read, 1)
                split_hi(act, u // SLOTS + 1, s, KT)

            act.wait_ge(mm_v0, 1)
            nc.scalar.activation(vn[:, 7, :], ps[4][:, 0:P], ACT.Copy).then_inc(v0_read, 1)
            a_z(U_Z)
            for q in range(2):
                act.wait_ge(mm_s0, q + 1)
                nc.scalar.activation(st[:, 4 * q:4 * q + 4, :], ps[5 + q][:, :], ACT.Copy).then_inc(s_ready, 1)
            a_z(U_Z + 1)
            act.wait_ge(mm_o0, 1)
            nc.scalar.activation(ot[:, MB, :], ps[7][:, 0:P], ACT.Copy).then_inc(o_read, 1)
            for c in range(2):
                a_z(U_Z + 2 * c + 2)
                for q in range(2):
                    act.wait_ge(mm_vn, 2 * c + q + 1)
                    nc.scalar.activation(vn[:, 4 * q:4 * q + 4, :], ps[6 + q][:, :], ACT.Copy).then_inc(vn_ready, 1)
                a_z(U_Z + 2 * c + 3)
                for q in range(2):
                    act.wait_ge(mm_o, 2 * c + q + 1)
                    nc.scalar.activation(ot[:, 8 * q + c:8 * q + 8:2, :],
                                         ps[6 + q][:, :].rearrange("p (b t) -> p b t", t=P), ACT.Copy).then_inc(o_read, 1)

            act.wait_ge(o_read, 5)
            nc.scalar.activation(ex[:], ot[:], ACT.Square).then_inc(sq_gdn, 1)
            a_z(U_Z + 6)
            a_z(U_Z + 7)
            for h in range(HEADS):
                act.wait_ge(og_ready, h + 1)
                nc.scalar.activation(hhi[:, h, 0:N_A], ogb[:, h, :], ACT.Copy).then_inc(rhs_hi, 1)

            def act_splits(phase):
                def body(t, i, blocks):
                    for s in range(SLOTS):
                        split_hi(act, t + 1, s, blocks)
                steps(act, phase, body)

            def act_hidden(name, n, taps=None):
                def body(t, i, blocks):
                    for p in range(2):
                        s0, s1 = 2 * p, 2 * p + 1
                        j = i * 2 + p
                        act.wait_ge(unit_done, t * SLOTS + (s0 + 1))
                        if taps is not None:
                            c = j + CONV_AT[name]
                            nc.scalar.activation(tb[:, p, 0:n], ps[s0][:, 0:n], ACT.Copy, scale=col(j * 3 + taps)).then_inc(f_tap, 1)
                            split_hi(act, t + 1, s0, blocks)
                            act.wait_ge(f_conv, c * 2 + 2)
                            nc.scalar.activation(sb[:, p, 0:n], tb[:, p, 0:n], ACT.Silu).then_inc(f_gate, 1)
                        else:
                            nc.scalar.activation(sb[:, p, 0:n], ps[s0][:, 0:n], ACT.Silu).then_inc(f_gate, 1)
                            split_hi(act, t + 1, s0, blocks)
                        split_hi(act, t + 1, s1, blocks)
                        act.wait_ge(tiles_read, t * SLOTS + (SLOTS + s0 + 2))
                        nc.scalar.activation(ahi[:, j, 0:n], ab[:, p, 0:n], ACT.Copy).then_inc(hid_hi, 1)
                steps(act, PH[name], body)

            def act_square(m, n, src):
                nc.scalar.activation(sqb[:, m, 0:n], src[:, m, 0:n], ACT.Square).then_inc(sq_ready, 1)

            def act_norm(i, n, eps, shift, version=None, src=None, ready=None):
                mine(nc.scalar.activation(small[:, 314:315], eps_of(eps), ACT.Abs_reciprocal_sqrt))
                if src is not None:
                    for m in range(KT):
                        ready(m)
                        act_square(m, n, src)
                act.wait_ge(var_mm, i + 1)
                nc.scalar.activation(ab[:, 0, 0:n], ps[5][:, 0:n], ACT.Abs_reciprocal_sqrt, bias=eps_of(eps)).then_inc(guess_ready, 1)
                if version:
                    for m in range(KT):
                        act.wait_ge(y_ready, Y_AT[i] + m + 1)
                        nc.scalar.activation(hhi[:, m, 0:n], xb[:, m, 0:n], ACT.Identity, bias=shift(m)).then_inc(rhs_hi, 1)
                if i < 4:
                    for m in range(KT):
                        act.wait_ge(y_ready, Y_AT[i] + m + 1)
                        nc.scalar.activation(hf[:, m, 0:n], xb[:, m, 0:n], ACT.Identity, bias=shift(m)).then_inc(hf_ready, 1)

            def act_ln(i, n, version=None):
                act_norm(i, n, LN_EPS, ln_shift(i), version, xb, lambda m: act.wait_ge(xc_ready, i * KT + m + 1))

            def act_late_norm(i, which, version, ready, squares, left):
                for m in range(KT):
                    ready(m)
                    if m == 0:
                        nc.scalar.activation(hhi[:, :, SEQ:N_SH], shifts(which), ACT.Copy)
                    nc.scalar.activation(hhi[:, m, 0:SEQ], hf[:, m, 0:SEQ], ACT.Copy, scale=a_of(which)(m)).then_inc(rhs_hi, 1)
                for m in left:
                    nc.scalar.activation(squares[:, m, 0:SEQ], hf[:, m, 0:SEQ], ACT.Square).then_inc(sq_ready, 1)
                mine(nc.scalar.activation(small[:, 314:315], eps_of(RMS_EPS), ACT.Abs_reciprocal_sqrt))
                act.wait_ge(var_mm, i + 1)
                nc.scalar.activation(ab[:, 0, 0:SEQ], ps[5][:, 0:SEQ], ACT.Abs_reciprocal_sqrt, bias=eps_of(RMS_EPS)).then_inc(guess_ready, 1)

            def act_hidden_late(name):
                def body(t, i, blocks):
                    for p in range(2):
                        s0, s1 = 2 * p, 2 * p + 1
                        j = i * 2 + p
                        split_hi(act, t + 1, s0, blocks)
                        act.wait_ge(late_g, j + (LATE_AT[name] + 1))
                        nc.scalar.activation(sb[:, p, 0:SEQ], tb[:, p, 0:SEQ], ACT.Silu, bias=small[:, 302 + p:303 + p]).then_inc(f_gate, 1)
                        split_hi(act, t + 1, s1, blocks)
                        act.wait_ge(tiles_read, t * SLOTS + (SLOTS + s0 + 2))
                        nc.scalar.activation(ahi[:, j, 0:SEQ], ab[:, p, 0:SEQ], ACT.Copy).then_inc(hid_hi, 1)
                steps(act, PH[name], body)

            def act_down_squares(name, i):
                def body(t, j, blocks):
                    for s in range(0, SLOTS, 2):
                        for k in range(2):
                            split_hi(act, t + 1, s + k, blocks)
                        m = j * 2 + s // 2
                        act.wait_ge(tiles_read, t * SLOTS + (SLOTS + s + 2))
                        nc.scalar.activation(sqb[:, m, 0:SEQ], hf[:, m, 0:SEQ], ACT.Square).then_inc(sq_ready, 1)
                steps(act, PH[name], body)

            act.wait_ge(eps_ready, 1)
            nc.scalar.activation(small[:, 300:308], vec[:, V_C:V_C + KT], ACT.Silu).then_inc(c_ready, 1)
            act_splits(PH["a_out"])
            act_ln(0, N_A, "ln0")
            act_hidden("up0", N_F0, V_FCONV)
            act_splits(PH["down0"])
            act_ln(1, N_F0, "ln1")

            def b_cx(t, i, blocks):
                for p in range(2):
                    act.wait_ge(unit_done, t * SLOTS + (2 * p + 1))
                    act.wait_ge(tiles_read, t * SLOTS + (2 * p + SLOTS))
                    nc.scalar.activation(tb[:, p, 0:N_F0], ps[2 * p][:, 0:N_F0], ACT.Copy).then_inc(f_tap, 1)
                    split_hi(act, t + 1, 2 * p, blocks)
                    split_hi(act, t + 1, 2 * p + 1, blocks)

            def b_gate(t, i, blocks):
                for s in range(SLOTS):
                    split_hi(act, t + 1, s, blocks)
                    act.wait_ge(tiles_read, t * SLOTS + (SLOTS + s + 1))
                    nc.scalar.activation(ahi[:, i * SLOTS + s, 0:N_B], ab[:, s % 2, 0:N_B], ACT.Copy).then_inc(hid_hi, 1)

            steps(act, PH["b_cx"], b_cx)
            steps(act, PH["b_gate"], b_gate)
            act_splits(PH["b_out"])
            act_ln(2, N_B, "ln2")
            act_hidden("up1", N_F1, V_FCONV + FT * 3)
            act_splits(PH["down1"])
            act_ln(3, N_F1)

            MIX = PH["mix"]
            M0 = MIX.first // SLOTS

            def mix_splits(u, k=1):
                for v in range(u, u + k):
                    nxt = v + SLOTS
                    split_hi(act, M0 + nxt // SLOTS, nxt % SLOTS, KT)

            def mods_there(m):
                if m == 0:
                    act.wait_ge(mods_ready, 1)
                    act.wait_ge(hf_ready, 4 * KT)

            act_late_norm(4, 0, "rms0", mods_there, xb, range(KT))
            act_hidden_late("up2")
            act_down_squares("down2", 5)
            act_norm(5, SEQ, RMS_EPS, sh_of(1), "rms1")

            for u in range(X_GA):
                act.wait_ge(unit_done, MIX.first + u + 1)
                b_ = ps[u % SLOTS]
                if u == 0:
                    nc.scalar.activation(krot[64:96, :], b_[64:96, 0:SEQ], ACT.Copy).then_inc(tiles_read, 1)
                elif u < X_UF:
                    nc.scalar.activation(lat[:, u - X_LAT, :], b_[:, 0:SEQ], ACT.Copy).then_inc(tiles_read, 1)
                    act.wait_ge(tiles_read, SLOTS + MIX.first + u + 1)
                    nc.scalar.activation(lsq[:, u - X_LAT, :], lat[:, u - X_LAT, :], ACT.Square).then_inc(ls_sq, 1)
                else:
                    nc.scalar.activation(uf[:, u - X_UF, :], b_[:, 0:SEQ], ACT.Copy).then_inc(tiles_read, 1)
                mix_splits(u)
                if u == X_GA - 2:
                    act.wait_ge(lat_v, 1)
                    nc.scalar.activation(wide(ab), wide(tb), ACT.Abs_reciprocal_sqrt).then_inc(lat_guess, 1)
            for j in range(5):
                act.wait_ge(lat_y, j + 1)
                nc.scalar.activation(lhi[:, j, :], lat[:, j, :], ACT.Copy, scale=col(V_QN + j)).then_inc(lat_hi, 1)

            def gate_unit(u, g, func):
                act.wait_ge(unit_done, MIX.first + u + 1)
                nc.scalar.activation(gates[:, g, :], ps[u % SLOTS][:, 0:SEQ], func).then_inc(tiles_read, 1)
                mix_splits(u)

            for u in range(X_GA, X_Q):
                gate_unit(u, u - X_GA, ACT.Sigmoid)
            mix_splits(X_Q, 3)
            for j in range(4):
                if j < 3:
                    act.wait_ge(q_mm, 2 * j + 2)
                else:
                    act.wait_ge(unit_done, MIX.first + X_K)
                nc.scalar.activation(qt[0:96, 2 * j:2 * j + 2, :], ps[4 + j][0:96, :].rearrange("p (g n) -> p g n", n=SEQ), ACT.Copy).then_inc(q_read, 1)
            mix_splits(X_K, 3)
            for j in range(2):
                if j == 0:
                    act.wait_ge(v_mm, 1)
                else:
                    act.wait_ge(unit_done, MIX.first + X_V + 1)
                nc.scalar.activation(vt[:, j, :], ps[4 + j][:, :], ACT.Copy).then_inc(v_read, 1)
            act.wait_ge(tiles_read, SLOTS + MIX.first + X_GB)
            for u in range(X_GB, X_GB + 2):
                gate_unit(u, u - X_GB + 4, ACT.Sigmoid)
            for j in range(4):
                act.wait_ge(four1, j + 1)
                nc.scalar.activation(pf[:, j // 2, 2 * (j % 2):2 * (j % 2) + 2, :],
                                     ps[4 + j][:, :].rearrange("p (g n) -> p g n", n=SEQ), ACT.Copy).then_inc(pf_ready, 1)
            for u in range(X_GB + 2, X_GB + 4):
                gate_unit(u, u - X_GB + 4, ACT.Sigmoid)
            for g in range(4):
                act.wait_ge(four2, g + 1)
                nc.scalar.activation(fhi[:, g, :], ps[4 + g][:, 0:SEQ], ACT.Copy).then_inc(f_hi, 1)
            for u in range(X_GB + 4, X_GC):
                gate_unit(u, u - X_GB + 4, ACT.Sigmoid)
            for h in range(HEADS + 2):
                if h < HEADS:
                    act.wait_ge(m_ready2, h + 1)
                    if h >= 2:
                        act.wait_ge(t_mm, h - 1)
                    for c in range(2):
                        last = nc.scalar.activation(pr[:, h % 2, c, :], ps[4 + h % 2][:, c * SEQ:(c + 1) * SEQ], ACT.Exp,
                                                    scale=SM_SCALE, bias=small[:, 112 + 2 * h + c:113 + 2 * h + c],
                                                    accum_out=small[:, 128 + 2 * h + c:129 + 2 * h + c])
                    last.then_inc(p_exp, 1)
                if 1 <= h <= 4:
                    gate_unit(X_GC + h - 1, 11 + h, ACT.Copy)
                elif 4 < h <= HEADS:
                    mix_splits(X_GC + h - 1)
                if 0 <= h - 1 < HEADS:
                    g = h - 1
                    act.wait_ge(t_mm, g + 1)
                    if g >= 2:
                        act.wait_ge(o_mm, g - 1)
                    nc.scalar.activation(pt[:, g % 2, :, :], ps[6 + g % 2][:, :].rearrange("p (c n) -> p c n", n=SEQ), ACT.Copy).then_inc(t_read, 1)
                if h >= 2:
                    g = h - 2
                    half = slice((g % 2) * 64, (g % 2) * 64 + 64)
                    act.wait_ge(o_mm, g + 1)
                    nc.scalar.activation(ohi[half, g // 2, :], ps[6 + g % 2][half, 0:SEQ], ACT.Copy).then_inc(o_hi, 1)
            nc.scalar.activation(gates[:, 12:16, :], gates[:, 12:16, :], ACT.Sigmoid).then_inc(gates_ready, 1)
            for u in range(X_MO, X_OUT):
                mix_splits(u)
                act.wait_ge(tiles_read, SLOTS + MIX.first + u + 1)
                m = 2 * (u - X_MO)
                nc.scalar.activation(hhi[:, m:m + 2, 0:SEQ], xb[:, m:m + 2, 0:SEQ], ACT.Copy).then_inc(y_hi, 1)
            for u in range(X_OUT, MIX.units):
                mix_splits(u)
                if u == MIX.units - 1:
                    break
                act.wait_ge(tiles_read, SLOTS + MIX.first + u + 1)
                nc.scalar.activation(qt[:, u - X_OUT, :], hf[:, u - X_OUT, 0:SEQ], ACT.Square).then_inc(sq_ready, 1)
            def w_out_done(m):
                if m == 0:
                    act.wait_ge(unit_done, PH["up3"].first)
                if m == KT - 1:
                    act.wait_ge(tiles_read, SLOTS + PH["up3"].first)

            act_late_norm(6, 2, "rms2", w_out_done, qt, [KT - 1])
            act_hidden_late("up3")
            act_down_squares("down3", 7)
            act_norm(7, SEQ, RMS_EPS, None)

        @block.vector
        def _(dve):
            mine = Steps(dve, dve_step)

            def step(instruction):
                mine(instruction)
                mine.after()

            def rsqrt(out, x, n, tmp):
                step(nc.vector.tensor_scalar(out.bitcast(I32), x.bitcast(I32), -0.5, 1597463007.0, ALU.mult, ALU.add))
                for _ in range(3):
                    step(nc.vector.tensor_tensor(tmp, out, out, ALU.mult))
                    step(nc.vector.scalar_tensor_tensor(tmp, tmp, -0.5, x, ALU.mult, ALU.mult))
                    step(nc.vector.scalar_tensor_tensor(out, tmp, 1.5, out, ALU.add, ALU.mult))

            def rhs_rest(version, k, src, n):
                dve.wait_ge(rhs_hi, RHS_AT[version] + k + 1)
                nc.vector.tensor_tensor(hlo[:, k, 0:n], src, hhi[:, k, 0:n], ALU.subtract).then_inc(rhs_ready, 1)

            nc.vector.memset(small[:, 0:1], 0.0).then_inc(tiles_read, SLOTS)
            R = slice(64, 96)
            dve.wait_ge(ld_small, 48)
            ang, n_i, n_f, wrap = tb[R, 0, 0:SEQ], sb[R, 0, 0:SEQ], ab[R, 0, 0:SEQ], sb[R, 1, 0:SEQ]
            step(nc.vector.tensor_copy(ang, pos[R, :]))
            step(nc.vector.tensor_scalar(ang, ang, vec[R, V_INVF:V_INVF + 1], None, ALU.mult))
            step(nc.vector.tensor_scalar(n_i.bitcast(I32), ang, 1.0 / (2 * np.pi), None, ALU.mult))
            step(nc.vector.tensor_copy(n_f, n_i.bitcast(I32)))
            for part in TWO_PI:
                step(nc.vector.scalar_tensor_tensor(ang, n_f, -part, ang, ALU.mult, ALU.add))

            def into_range(x):
                for sign, test in ((-1.0, ALU.is_gt), (1.0, ALU.is_lt)):
                    step(nc.vector.tensor_scalar(wrap, x, -sign * float(np.pi), sign * 2 * float(np.pi), test, ALU.mult))
                    step(nc.vector.tensor_tensor(x, x, wrap, ALU.add))

            into_range(ang)
            step(nc.vector.tensor_scalar(ab[R, 1, 0:SEQ], ang, float(np.pi) / 2, None, ALU.add))
            into_range(ab[R, 1, 0:SEQ])
            step(nc.vector.tensor_scalar(ab[R, 1, 0:SEQ], ab[R, 1, 0:SEQ], PI_IN, -PI_IN, ALU.min, ALU.max))
            nc.vector.tensor_scalar(tb[R, 1, 0:SEQ], ang, PI_IN, -PI_IN, ALU.min, ALU.max).then_inc(ang_ready, 1)
            dve.wait_ge(cs_ready, 1)
            step(nc.vector.tensor_scalar(cs[R, 1, :], cs[R, 1, :], vec[R, V_SIGN:V_SIGN + 1], None, ALU.mult))

            nc.vector.memset(small[:, 316:317], LN_EPS)
            nc.vector.memset(small[:, 317:318], RMS_EPS).then_inc(eps_ready, 1)
            dve.wait_ge(ld_x, 16 * KT)
            for k in range(KT):
                rhs_rest("x", k, hf[:, k, :], TOK)
            for s in range(SLOTS):
                split_lo(dve, 0, s, KT)

            dve.wait_ge(mm_ab, 1)
            nc.vector.tensor_copy(abt[0:16, :], ps[7][0:16, 0:TOK]).then_inc(ab_ready, 1)
            dve.wait_ge(ab_ready, 1)
            nc.vector.tensor_copy(abm[0:16, :].rearrange("p (h t) -> p h t", t=META),
                                  abt[0:16, 0:META].unsqueeze(1).to_broadcast([16, HEADS, META])).then_inc(ab_ready, 1)

            def conv(u, i, s):
                t_ = tb[:, s % 2, :]
                dve.wait_ge(a_tap, u + 1)
                for j, tap in enumerate((2, 1, 0)):
                    if j:
                        dve.wait_ge(a_conv, u * 2 + j)
                    nc.vector.scalar_tensor_tensor(t_[:, j + 1:TOK], ps[s][:, 0:TOK - 1 - j], col(u * 4 + (V_ACONV + tap)),
                                                   t_[:, j + 1:TOK], ALU.mult, ALU.add).then_inc(a_conv if j < 2 else tiles_read, 1)
                split_lo(dve, i + 1, s, KT)

            def d_v(u):
                conv(u, u // SLOTS, u % SLOTS)

            for u in range(SLOTS):
                d_v(u)

            dve.wait_ge(ld_cm, 16)
            mine(nc.vector.tensor_scalar(never[:], cm[:, C_CAUSAL:C_CAUSAL_META + 1, :], -1.0, 200.0, ALU.add, ALU.mult))
            dve.wait_ge(mm_gate, 1)
            for which, at_col in ((1, 0), (2, HEADS)):
                for c in range(2):
                    mine(nc.vector.tensor_copy(S_(which)[:, c:MB:2], ps[7][:, c * 16 + at_col:c * 16 + at_col + HEADS]))
                step(nc.vector.tensor_tensor(S_(12)[:, 0:HEADS], ps[7][:, 32 + at_col:32 + at_col + HEADS],
                                             vec[:, V_HEAD:V_HEAD + HEADS], ALU.mult))
                step(nc.vector.reduce_sum(S_(which)[:, MB:NBLK], S_(12)[:, 0:HEADS], AX.X))
            step(nc.vector.tensor_tensor(S_(2), S_(2), vec[:, V_DT:V_DT + NBLK], ALU.add))
            step(nc.vector.tensor_scalar(S_(3), S_(2), -1.0, None, ALU.mult))
            nc.vector.tensor_tensor(S_(3), S_(3), S_(2), ALU.max).then_inc(g_dve, 1)
            dve.wait_ge(g_act, 4)
            step(nc.vector.scalar_tensor_tensor(S_(4), S_(2), 0.0, S_(4), ALU.max, ALU.add))
            nc.vector.scalar_tensor_tensor(S_(6), S_(4), -1.0, S_(6), ALU.mult, ALU.mult).then_inc(gl_ready, 1)
            step(nc.vector.tensor_scalar(S_(5), S_(5), 1.0, None, ALU.add))
            step(nc.vector.reciprocal(S_(2), S_(5)))
            d_v(SLOTS)
            d_v(SLOTS + 1)
            d_v(SLOTS + 2)
            dve.wait_ge(mm_cum, 1)
            step(nc.vector.tensor_copy(S_(7), ps[7][:, 64:64 + NBLK]))
            step(nc.vector.tensor_copy(S_(8), ps[7][:, 96:96 + NBLK]))
            nc.vector.tensor_tensor(S_(10), S_(8), S_(7), ALU.subtract).then_inc(g_dve, 1)

            def d_z(u):
                split_lo(dve, u // SLOTS + 1, u % SLOTS, KT)

            d_v(SLOTS + 3)
            with dve.Fori(2, U_V // SLOTS) as i:
                for s in range(SLOTS):
                    conv(i * SLOTS + s, i, s)
            for u in U_FIRST:
                d_v(u)

            dve.wait_ge(mm_norm, 1)
            dve.wait_ge(g_act, 7)
            nn = small[:, 320:320 + 2 * NBLK]
            step(nc.vector.tensor_scalar(nn, ps[7][:, 0:2 * NBLK], L2_EPS, None, ALU.add))
            rsqrt(small[:, 360:360 + 2 * NBLK], nn, 2 * NBLK, small[:, 400:400 + 2 * NBLK])
            rk, rq = small[:, 360:360 + NBLK], small[:, 360 + NBLK:360 + 2 * NBLK]
            mine(nc.vector.tensor_tensor(S_(12), rk, S_(2), ALU.mult))
            mine(nc.vector.tensor_scalar(S_(13), rq, float(P) ** -0.5, None, ALU.mult))
            step(nc.vector.tensor_tensor(S_(15), rk, S_(10), ALU.mult))
            nc.vector.scalar_tensor_tensor(S_(16), S_(12), -1.0, S_(9), ALU.mult, ALU.mult).then_inc(cols_ready, 1)
            d_v(U_NEXT)

            for g, (b0, n) in enumerate(GROUPS):
                w = n * P
                dve.wait_ge(mm_gb, g + 1)
                for j in range(n):
                    last = nc.vector.scalar_tensor_tensor(ex[:, b0 + j, :], ps[4][:, j * P:(j + 1) * P], S_(7)[:, b0 + j:b0 + j + 1],
                                                          never[:, int(b0 == MB), :], ALU.subtract, ALU.min)
                last.then_inc(d_diff, 1)
                dve.wait_ge(d_exp, 2 * g + 1)
                dve.wait_ge(mm_cb, g + 1)
                for j in range(n):
                    b = b0 + j
                    nc.vector.scalar_tensor_tensor(bn[:, b, :], ps[6][:, j * P:(j + 1) * P], rk[:, b:b + 1], ex[:, b, :], ALU.mult, ALU.mult)
                    last = nc.vector.scalar_tensor_tensor(ca[:, b, :], ps[7][:, j * P:(j + 1) * P], rk[:, b:b + 1], ex[:, b, :], ALU.mult, ALU.mult)
                step(last)
                nc.vector.tensor_tensor(bn[:, b0:b0 + n, :], bn[:, b0:b0 + n, :], ps[5][:, 0:w].rearrange("p (b t) -> p b t", t=P),
                                        ALU.mult).then_inc(m_ready, 1)
                if g < 4:
                    d_v(U_NEXT + 1 + g)

            for g, (b0, n) in enumerate(GROUPS):
                step(nc.vector.tensor_tensor(gu[:, b0:b0 + n, :], bn[:, b0:b0 + n, :], bcast(cm[:, C_PAIR, :], n), ALU.mult))
                nc.vector.tensor_tensor(gu[:, b0:b0 + n, :], gu[:, b0:b0 + n, :], bcast(ident, n), ALU.add).then_inc(gu0_ready, 1)

            def mask_x(l, g):
                b0, n = GROUPS[g]
                dve.wait_ge(mm_x, (l - 1) * 5 + (g + 1))
                nc.vector.tensor_tensor(ex[:, b0:b0 + n, :], ps[g % 2][:, 0:n * P].rearrange("p (b t) -> p b t", t=P),
                                        cm[:, bass.ds(l + C_LEVEL, 1), :].to_broadcast([P, n, P]), ALU.mult).then_inc(x_ready, 1)

            def add_y(l, g, both=True):
                b0, n = GROUPS[g]
                dve.wait_ge(mm_y, (l - 1) * 5 + (g + 1))
                if both:
                    nc.vector.tensor_tensor(gt[:, b0:b0 + n, :], gt[:, b0:b0 + n, :],
                                            ps[2 + g % 3][:, 0:n * P].rearrange("p (b t) -> p b t", t=P), ALU.add)
                nc.vector.tensor_tensor(gu[:, b0:b0 + n, :], gu[:, b0:b0 + n, :],
                                        ps[5 + g % 3][:, 0:n * P].rearrange("p (b t) -> p b t", t=P), ALU.add).then_inc(tu_ready, 1)

            dve.wait_ge(tu_ready, 5)
            with dve.Fori(1, LEVELS - 1) as l:
                for g in range(len(GROUPS)):
                    mask_x(l, g)
                    if g:
                        add_y(l, g - 1)
                add_y(l, len(GROUPS) - 1)
            for g in range(4):
                mask_x(LEVELS - 1, g)
                if g:
                    add_y(LEVELS - 1, g - 1, both=False)
            add_y(LEVELS - 1, 3, both=False)

            dve.wait_ge(v0_read, 1)
            for h in range(HEADS):
                last = nc.vector.tensor_scalar(rr[:, h, :], ps[4][:, 0:P], vec[:, V_HEAD + h:V_HEAD + h + 1], None, ALU.mult)
            last.then_inc(vm_ready, 1)
            d_z(U_Z)
            d_z(U_Z + 1)
            for c in range(2):
                for q in range(2):
                    r = 2 * c + q
                    dve.wait_ge(mm_ks, r + 1)
                    for j in range(4):
                        h = 4 * q + j
                        b = 2 * h + c
                        last = nc.vector.scalar_tensor_tensor(rr[:, h, :], ps[4 + q][:, j * P:(j + 1) * P], S_(16)[:, b:b + 1],
                                                              blocks_at(2, b, 1), ALU.mult, ALU.add)
                    last.then_inc(r_ready, 1)
                d_z(U_Z + 2 * c + 2)
                d_z(U_Z + 2 * c + 3)
                if c == 0:
                    for q in range(2):
                        dve.wait_ge(mm_ds, q + 1)
                        dve.wait_ge(mm_o, q + 1)
                        for j in range(4):
                            h = 4 * q + j
                            last = nc.vector.scalar_tensor_tensor(st[:, h, :], st[:, h, :], S_(11)[:, 2 * h:2 * h + 1],
                                                                  ps[4 + q][:, j * P:(j + 1) * P], ALU.mult, ALU.add)
                        last.then_inc(s_ready, 1)
            d_z(U_Z + 6)

            dve.wait_ge(mm_norm, 2)
            nn = small[:, 320:320 + NBLK]
            step(nc.vector.tensor_tensor(nn, ps[7][:, 0:NBLK], S_(13), ALU.mult))
            step(nc.vector.tensor_tensor(nn, nn, S_(13), ALU.mult))
            step(nc.vector.tensor_scalar(nn, nn, 1.0 / P, RMS_EPS, ALU.mult, ALU.add))
            rsqrt(small[:, 360:360 + NBLK], nn, NBLK, small[:, 400:400 + NBLK])
            nc.vector.tensor_tensor(S_(12), small[:, 360:360 + NBLK], S_(13), ALU.mult).then_inc(cols_ready, 1)
            for g in (4, 0, 1, 2, 3):
                b0, n = GROUPS[g]
                dve.wait_ge(mm_gb, len(GROUPS) + (1 if g == 4 else g + 2))
                step(nc.vector.tensor_tensor(bn[:, b0:b0 + n, :], ot[:, b0:b0 + n, :],
                                             ps[[1, 2, 3, 4, 0][g]][:, 0:n * P].rearrange("p (b t) -> p b t", t=P), ALU.mult))
                if g == 4:
                    step(nc.vector.scalar_tensor_tensor(
                        ogb[:, :, 0:6], bn[:, MB, :].rearrange("p (h t) -> p h t", t=META)[:, :, META - 6:META],
                        col(V_ANORM), zs[:, :, 0:6], ALU.mult, ALU.mult))
                else:
                    for h in (2 * g, 2 * g + 1):
                        nc.vector.scalar_tensor_tensor(
                            ogb[:, h, 6:N_A].rearrange("p (c t) -> p c t", t=P), bn[:, 2 * h:2 * h + 2, :], col(V_ANORM),
                            zs[:, h, 6:N_A].rearrange("p (c t) -> p c t", t=P), ALU.mult, ALU.mult).then_inc(og_ready, 1)
            d_z(U_Z + 7)
            for h in range(HEADS):
                rhs_rest("gdn", h, ogb[:, h, :], N_A)

            def dve_ada(o, r):
                dve.wait_ge(ld_ada[r], (o // 2) * 16 + 16)
                dve.wait_ge(ada_done, o + 1)
                a_ = acc[:, o // KT, :] if isinstance(o, int) else acc[:, bass.ds(o // KT, 1), :].rearrange("p a n -> p (a n)")
                nc.vector.scalar_tensor_tensor(a_, ring[:, r, :], small[:, bass.ds(o + 440, 1)], a_, ALU.mult, ALU.add).then_inc(ada_done, 1)

            def dve_residual(name, n, off):
                phase = PH[name]
                per = 2 if phase.blocks == SLOT_BLOCKS else 1

                def rest(t, i, s, blocks):
                    for j in range(per):
                        split_lo(dve, t + 1, s + j, blocks)

                def body(t, i, blocks, last=False):
                    for s in range(0, SLOTS, per):
                        m = i * (SLOTS // per) + s // per
                        dve.wait_ge(unit_done, t * SLOTS + (s + per))
                        nc.vector.scalar_tensor_tensor(xb[:, m, 0:n], hf[:, m, off:off + n], ALPHA, ps[s][:, 0:n],
                                                       ALU.mult, ALU.add).then_inc(tiles_read, per)
                        dve.wait_ge(tiles_read, t * SLOTS + (SLOTS + s + per))
                        nc.vector.tensor_tensor(sums[:, 0:n], sums[:, 0:n], xb[:, m, 0:n], ALU.add).then_inc(sum_ready, 1)
                        if not last or s < SLOTS - per:
                            rest(t, i, s, blocks)
                            if name in ADA_AT:
                                for j in range(2):
                                    dve_ada(i * 4 + (ADA_AT[name] + s + j), j)
                step(nc.vector.memset(sums[:, 0:n], 0.0))
                t0, k = phase.first // SLOTS, phase.units // SLOTS
                with dve.Fori(0, k - 1) as i:
                    body(i + t0, i, phase.blocks)
                body(k - 1 + t0, k - 1, BLOCKS_AFTER[name], last=True)
                return lambda: rest(k - 1 + t0, k - 1, SLOTS - per, BLOCKS_AFTER[name])

            def dve_hidden(name, n, taps=None):
                def body(t, i, blocks):
                    for p in range(2):
                        s0, s1 = 2 * p, 2 * p + 1
                        j = i * 2 + p
                        if taps is not None:
                            c = j + CONV_AT[name]
                            dve.wait_ge(f_tap, c + 1)
                            nc.vector.scalar_tensor_tensor(tb[:, p, 0:n], ps[s0][:, 1:n + 1], col(j * 3 + (taps + 1)),
                                                           tb[:, p, 0:n], ALU.mult, ALU.add).then_inc(f_conv, 1)
                            dve.wait_ge(f_conv, c * 2 + 1)
                            nc.vector.scalar_tensor_tensor(tb[:, p, 0:n], ps[s0][:, 2:n + 2], col(j * 3 + (taps + 2)),
                                                           tb[:, p, 0:n], ALU.mult, ALU.add).then_inc(f_conv, 1)
                        split_lo(dve, t + 1, s0, blocks)
                        dve.wait_ge(f_gate, j + (GATE_AT[name] + 1))
                        dve.wait_ge(unit_done, t * SLOTS + (s1 + 1))
                        off = 0 if taps is None else 2
                        nc.vector.tensor_tensor(ab[:, p, 0:n], sb[:, p, 0:n], ps[s1][:, off:off + n], ALU.mult).then_inc(tiles_read, 2)
                        if name in ADA_AT:
                            dve_ada(i * 2 + (ADA_AT[name] + p), p)
                        dve.wait_ge(hid_hi, j + (HID_AT[name] + 1))
                        nc.vector.tensor_tensor(alo[:, j, 0:n], ab[:, p, 0:n], ahi[:, j, 0:n], ALU.subtract).then_inc(hid_ready, 1)
                        split_lo(dve, t + 1, s1, blocks)
                steps(dve, PH[name], body)

            def dve_norm(i, n, src, eps, gain, shift, version=None, dst=None, meanwhile=None):
                if i < 4:
                    dve.wait_ge(mean_mm, i + 1)
                    for m in range(KT):
                        nc.vector.tensor_tensor(xb[:, m, 0:n], xb[:, m, 0:n], ps[4][:, 0:n], ALU.subtract).then_inc(xc_ready, 1)
                if meanwhile:
                    meanwhile()
                dve.wait_ge(guess_ready, i + 1)
                v_, y_, t_ = tb[:, 0, 0:n], ab[:, 0, 0:n], sb[:, 0, 0:n]
                step(nc.vector.tensor_tensor(t_, y_, y_, ALU.mult))
                step(nc.vector.scalar_tensor_tensor(v_, ps[5][:, 0:n], eps, t_, ALU.add, ALU.mult))
                step(nc.vector.scalar_tensor_tensor(y_, v_, 3.0, y_, ALU.subtract, ALU.mult))
                dst = xb if dst is None else dst
                for m in range(KT):
                    nc.vector.scalar_tensor_tensor(dst[:, m, 0:n], src[:, m, 0:n], gain(m), y_, ALU.mult, ALU.mult).then_inc(y_ready, 1)
                if version:
                    for m in range(KT):
                        dve.wait_ge(rhs_hi, RHS_AT[version] + m + 1)
                        nc.vector.scalar_tensor_tensor(hlo[:, m, 0:n], xb[:, m, 0:n], shift(m), hhi[:, m, 0:n],
                                                       ALU.add, ALU.subtract).then_inc(rhs_ready, 1)

            def dve_ln(i, n, version=None, meanwhile=None):
                dve_norm(i, n, xb, LN_EPS, ln_gain(i), ln_shift(i), version, meanwhile=meanwhile)

            for i in range(4):
                mine(nc.vector.tensor_scalar(vec[:, V_LN + 2 * i * KT:V_LN + (2 * i + 1) * KT], vec[:, V_LN + 2 * i * KT:V_LN + (2 * i + 1) * KT],
                                             -0.5, None, ALU.mult))
            mine(nc.vector.tensor_scalar(vec[:, V_NORM + 3 * KT:V_NORM + 4 * KT], vec[:, V_NORM + 3 * KT:V_NORM + 4 * KT], -0.5, None, ALU.mult))
            step(nc.vector.tensor_scalar(vec[:, V_QN:V_QN + 5], vec[:, V_QN:V_QN + 5], -0.5, None, ALU.mult))
            dve.wait_ge(c_ready, 1)
            step(nc.vector.tensor_copy(small[:, 440:512].rearrange("p (n k) -> p n k", k=KT), bcast(small[:, 300:308], 9)))
            rest_of_splits = dve_residual("a_out", N_A, TOK - N_A)
            dve_ln(0, N_A, "ln0", meanwhile=rest_of_splits)
            dve_hidden("up0", N_F0, V_FCONV)
            rest_of_splits = dve_residual("down0", N_F0, N_A - N_F0)
            dve_ln(1, N_F0, "ln1", meanwhile=rest_of_splits)
            for j in range(2):
                dve_ada(ADA_AT["b_cx"] - 2 + j, j)

            def b_cx(t, i, blocks):
                for p in range(2):
                    m = i * 2 + p
                    c = m + CONV_AT["b_cx"]
                    dve.wait_ge(f_tap, c + 1)
                    dve.wait_ge(unit_done, t * SLOTS + (2 * p + 2))
                    nc.vector.tensor_tensor(tb[:, p, 0:N_F0], tb[:, p, 0:N_F0], ps[2 * p + 1][:, 0:N_F0], ALU.mult).then_inc(f_conv, 1)
                    split_lo(dve, t + 1, 2 * p, blocks)
                    dve.wait_ge(f_conv, c * 2 + 1)
                    nc.vector.tensor_scalar(xb[:, m, 0:N_B], tb[:, p, 0:N_B], col(m * 3 + V_BCONV), None, ALU.mult).then_inc(b_tap, 1)
                    dve.wait_ge(b_tap, m + 1)
                    nc.vector.scalar_tensor_tensor(xb[:, m, 0:N_B], tb[:, p, 1:N_B + 1], col(m * 3 + (V_BCONV + 1)),
                                                   xb[:, m, 0:N_B], ALU.mult, ALU.add).then_inc(f_conv, 1)
                    dve.wait_ge(f_conv, c * 2 + 2)
                    nc.vector.scalar_tensor_tensor(xb[:, m, 0:N_B], tb[:, p, 2:N_B + 2], col(m * 3 + (V_BCONV + 2)),
                                                   xb[:, m, 0:N_B], ALU.mult, ALU.add).then_inc(tiles_read, 2)
                    split_lo(dve, t + 1, 2 * p + 1, blocks)
                    dve_ada(i * 2 + (ADA_AT["b_cx"] + p), p)

            def b_gate(t, i, blocks):
                for s in range(SLOTS):
                    m = i * SLOTS + s
                    dve.wait_ge(unit_done, t * SLOTS + (s + 1))
                    nc.vector.tensor_tensor(ab[:, s % 2, 0:N_B], xb[:, m, 0:N_B], ps[s][:, 2:N_F0], ALU.mult).then_inc(tiles_read, 1)
                    split_lo(dve, t + 1, s, blocks)
                    if s % 2:
                        dve_ada(i * 2 + (ADA_AT["b_gate"] + s // 2), s // 2)
                    dve.wait_ge(hid_hi, m + (HID_AT["b_gate"] + 1))
                    nc.vector.tensor_tensor(alo[:, m, 0:N_B], ab[:, s % 2, 0:N_B], ahi[:, m, 0:N_B], ALU.subtract).then_inc(hid_ready, 1)

            steps(dve, PH["b_cx"], b_cx)
            dve.wait_ge(tiles_read, SLOTS + PH["b_gate"].first)
            steps(dve, PH["b_gate"], b_gate)
            rest_of_splits = dve_residual("b_out", N_B, N_F0 - N_B)
            dve_ln(2, N_B, "ln2", meanwhile=rest_of_splits)
            dve_hidden("up1", N_F1, V_FCONV + FT * 3)
            rest_of_splits = dve_residual("down1", N_F1, N_B - N_F1)
            dve_ln(3, N_F1, meanwhile=rest_of_splits)

            MIX = PH["mix"]
            M0 = MIX.first // SLOTS

            def mix_splits(u, k=1):
                for v in range(u, u + k):
                    nxt = v + SLOTS
                    split_lo(dve, M0 + nxt // SLOTS, nxt % SLOTS, KT)

            step(nc.vector.memset(sums[:, 0:SEQ], 0.0))
            dve.wait_ge(mods_mm, 3)
            step(nc.vector.tensor_tensor(small[:, 0:72], ps[6][:, 0:72], vec[:, V_ADAB:V_ADAB + 72], ALU.add))
            for i in range(3):
                step(nc.vector.scalar_tensor_tensor(small[:, 72 + KT * i:80 + KT * i], small[:, (3 * i + 1) * KT:(3 * i + 2) * KT], 1.0,
                                                    vec[:, V_NORM + KT * i:V_NORM + KT * (i + 1)], ALU.add, ALU.mult))
            mine(nc.vector.tensor_scalar(small[:, 72 + KT:72 + 2 * KT], small[:, 72 + KT:72 + 2 * KT], -0.5, None, ALU.mult))
            for g in (2, 8):
                last = nc.vector.tensor_scalar(small[:, g * KT:(g + 1) * KT], small[:, g * KT:(g + 1) * KT], 0.5, None, ALU.mult)
                if g == 2:
                    mine(last)
            last.then_inc(mods_ready, 1)
            dve.wait_ge(mods_ready, 1)

            def gated_residual(t, i, blocks, per, gate, squares=None):
                for s in range(0, SLOTS, per):
                    m = i * (SLOTS // per) + s // per
                    dve.wait_ge(unit_done, t * SLOTS + (s + per))
                    nc.vector.scalar_tensor_tensor(hf[:, m, 0:SEQ], ps[s][:, 0:SEQ], small[:, bass.ds(m + gate * KT, 1)],
                                                   hf[:, m, 0:SEQ], ALU.mult, ALU.add).then_inc(tiles_read, per)
                    for j in range(per):
                        split_lo(dve, t + 1, s + j, blocks)
                    if squares is not None and (squares != 6 or m < KT - 1):
                        add_squares(squares, m)

            def add_squares(norm, m):
                dve.wait_ge(sq_ready, m + (norm * KT + 1))
                dve.wait_ge(sum_ready, m + (SUMS_AT[norm]))
                nc.vector.tensor_tensor(sums[:, 0:SEQ], sums[:, 0:SEQ], {4: xb, 6: qt}.get(norm, sqb)[:, m, 0:SEQ], ALU.add).then_inc(sum_ready, 1)

            def down_squares(name, gate, norm):
                step(nc.vector.memset(sums[:, 0:SEQ], 0.0))
                steps(dve, PH[name], lambda t, i, blocks: gated_residual(t, i, blocks, 2, gate, norm))

            def dve_late_norm(i, which, version, left):
                for m in range(KT):
                    dve.wait_ge(rhs_hi, RHS_AT[version] + m + 1)
                    if m == 0:
                        nc.vector.tensor_tensor(hlo[:, :, SEQ:N_SH], shifts(which), hhi[:, :, SEQ:N_SH], ALU.subtract)
                    nc.vector.scalar_tensor_tensor(hlo[:, m, 0:SEQ], hf[:, m, 0:SEQ], a_of(which)(m), hhi[:, m, 0:SEQ],
                                                   ALU.mult, ALU.subtract).then_inc(rhs_ready, 1)
                for m in left:
                    add_squares(i, m)
                dve.wait_ge(guess_ready, i + 1)
                v_, y_, t_ = tb[:, 0, 0:SEQ], ab[:, 0, 0:SEQ], sb[:, 0, 0:SEQ]
                step(nc.vector.tensor_tensor(t_, y_, y_, ALU.mult))
                step(nc.vector.scalar_tensor_tensor(v_, ps[5][:, 0:SEQ], NORM_EPS, t_, ALU.add, ALU.mult))
                step(nc.vector.scalar_tensor_tensor(rt[:], v_, 3.0, y_, ALU.subtract, ALU.mult))

            def dve_hidden_late(name):
                def body(t, i, blocks):
                    for p in range(2):
                        s0, s1 = 2 * p, 2 * p + 1
                        j = i * 2 + p
                        dve.wait_ge(unit_done, t * SLOTS + (s0 + 1))
                        nc.vector.tensor_copy(small[:, 302 + p:303 + p], ps[s0][:, SEQ:SEQ + 1])
                        nc.vector.scalar_tensor_tensor(tb[:, p, 0:SEQ], ps[s0][:, 0:SEQ], -0.5, rt[:], ALU.mult, ALU.mult).then_inc(late_g, 1)
                        split_lo(dve, t + 1, s0, blocks)
                        dve.wait_ge(unit_done, t * SLOTS + (s1 + 1))
                        nc.vector.tensor_copy(small[:, 304 + p:305 + p], ps[s1][:, SEQ:SEQ + 1])
                        nc.vector.scalar_tensor_tensor(ab[:, p, 0:SEQ], ps[s1][:, 0:SEQ], -0.5, rt[:], ALU.mult, ALU.mult).then_inc(late_u, 1)
                        dve.wait_ge(f_gate, j + (GATE_AT[name] + 1))
                        dve.wait_ge(late_u, j + (LATE_AT[name] + 1))
                        nc.vector.scalar_tensor_tensor(ab[:, p, 0:SEQ], ab[:, p, 0:SEQ], small[:, 304 + p:305 + p], sb[:, p, 0:SEQ],
                                                       ALU.add, ALU.mult).then_inc(tiles_read, 2)
                        split_lo(dve, t + 1, s1, blocks)
                        dve.wait_ge(hid_hi, j + (HID_AT[name] + 1))
                        nc.vector.tensor_tensor(alo[:, j, 0:SEQ], ab[:, p, 0:SEQ], ahi[:, j, 0:SEQ], ALU.subtract).then_inc(hid_ready, 1)
                steps(dve, PH[name], body)

            dve_late_norm(4, 0, "rms0", range(KT))
            dve_hidden_late("up2")
            down_squares("down2", 2, 5)
            dve_norm(5, SEQ, hf, NORM_EPS, a_of(1), sh_of(1), "rms1")

            mix_splits(0, X_UF + 2)
            dve.wait_ge(lat_mm, 1)
            for f0, f1, at_ in ((0, 3, 0), (3, 5, SEQ)):
                last = nc.vector.tensor_scalar(wide(tb)[:, at_:at_ + SEQ], ps[4][:, at_:at_ + SEQ], 1.0 / ((f1 - f0) * P), NORM_EPS, ALU.mult, ALU.add)
            last.then_inc(lat_v, 1)
            mix_splits(X_UF + 2)
            dve.wait_ge(lat_guess, 1)
            step(nc.vector.tensor_tensor(wide(sb), wide(ab), wide(ab), ALU.mult))
            step(nc.vector.tensor_tensor(wide(tb), wide(tb), wide(sb), ALU.mult))
            step(nc.vector.scalar_tensor_tensor(wide(ab), wide(tb), 3.0, wide(ab), ALU.subtract, ALU.mult))
            for j in range(5):
                at_ = 0 if j < 3 else SEQ
                nc.vector.tensor_tensor(lat[:, j, :], lat[:, j, :], wide(ab)[:, at_:at_ + SEQ], ALU.mult).then_inc(lat_y, 1)
            mix_splits(X_UF + 3)
            for j in range(5):
                dve.wait_ge(lat_hi, j + 1)
                nc.vector.scalar_tensor_tensor(llo[:, j, :], lat[:, j, :], col(V_QN + j), lhi[:, j, :], ALU.mult, ALU.subtract).then_inc(lat_ready, 1)
            mix_splits(X_GA, X_K - X_GA)
            for j in range(4):
                if j % 2 == 0:
                    dve.wait_ge(k_mm, 3 * (j // 2) + 2)
                else:
                    dve.wait_ge(unit_done, MIX.first + X_K + 1 + j // 2)
                nc.vector.tensor_copy(kt_[0:64, 2 * j:2 * j + 2, :], ps[j][0:64, :].rearrange("p (g n) -> p g n", n=SEQ)).then_inc(k_read, 1)
            mix_splits(X_K, 3)
            dve.wait_ge(v_read, 2)
            dve.wait_ge(q_read, 4)
            nc.vector.memset(small[:, 310:311], 0.0).then_inc(tiles_read, 6)
            swap = [(i + 16) % 32 for i in range(32)]
            c_, s_ = cs[R, 0, :], cs[R, 1, :]

            def bc(x, n):
                return x.unsqueeze(1).to_broadcast([32, n, SEQ])

            step(nc.vector.stream_shuffle(rot[R, 0, :], krot[R, :], swap))
            mine(nc.vector.tensor_tensor(rot[R, 0, :], rot[R, 0, :], s_, ALU.mult))
            step(nc.vector.tensor_tensor(krot[R, :], krot[R, :], c_, ALU.mult))
            step(nc.vector.tensor_tensor(krot[R, :], krot[R, :], rot[R, 0, :], ALU.add))
            mine(nc.vector.tensor_copy(kt_[R, :, :], bc(krot[R, :], HEADS)))
            mix_splits(X_GB, 2)
            for h in range(0, HEADS, 2):
                q_, r_ = qt[R, h:h + 2, :], rot[R, h:h + 2, :]
                step(nc.vector.stream_shuffle(r_.rearrange("p h n -> p (h n)"), q_.rearrange("p h n -> p (h n)"), swap))
                mine(nc.vector.tensor_tensor(r_, r_, bc(s_, 2), ALU.mult))
                step(nc.vector.tensor_tensor(q_, q_, bc(c_, 2), ALU.mult))
                last = nc.vector.tensor_tensor(q_, q_, r_, ALU.add)
                last.then_inc(rope_ready, 1)
                mix_splits(X_GB + 2 + h // 2)
                if h == 4:
                    for g in range(4):
                        dve.wait_ge(f_hi, g + 1)
                        nc.vector.tensor_tensor(flo[:, g, :], ps[4 + g][:, 0:SEQ], fhi[:, g, :], ALU.subtract).then_inc(f_ready, 1)
            mix_splits(X_GB + 6, 2)
            for h in range(HEADS + 2):
                if h < HEADS:
                    dve.wait_ge(s_mm, h + 1)
                    step(nc.vector.reduce_max(small[:, 144 + 2 * h:146 + 2 * h], ps[4 + h % 2][:, :].rearrange("p (c n) -> p c n", n=SEQ), AX.X))
                    nc.vector.tensor_scalar(small[:, 112 + 2 * h:114 + 2 * h], small[:, 144 + 2 * h:146 + 2 * h], -SM_SCALE, None,
                                            ALU.mult).then_inc(m_ready2, 1)
                if 0 <= h - 1 < HEADS:
                    g = h - 1
                    dve.wait_ge(p_exp, g + 1)
                    step(nc.vector.reciprocal(small[:, 160 + 2 * g:162 + 2 * g], small[:, 128 + 2 * g:130 + 2 * g]))
                    for c in range(2):
                        last = nc.vector.tensor_scalar(pr[:, g % 2, c, :], pr[:, g % 2, c, :], small[:, 160 + 2 * g + c:161 + 2 * g + c], None, ALU.mult)
                    last.then_inc(p_ready, 1)
                if 1 <= h <= HEADS:
                    u = X_GC + h - 1
                    if u >= X_FO:
                        dve.wait_ge(unit_done, MIX.first + u + 1)
                        dve.wait_ge(tiles_read, SLOTS + MIX.first + u)
                        m = 2 * (u - X_FO)
                        nc.vector.tensor_tensor(xb[:, m:m + 2, 0:SEQ], gates[:, m:m + 2, :], ps[u % SLOTS][:, :].rearrange("p (g n) -> p g n", n=SEQ),
                                                ALU.mult).then_inc(tiles_read, 1)
                    mix_splits(u)
                if h >= 2:
                    g = h - 2
                    half = slice((g % 2) * 64, (g % 2) * 64 + 64)
                    dve.wait_ge(o_hi, g + 1)
                    nc.vector.tensor_tensor(olo[half, g // 2, :], ps[6 + g % 2][half, 0:SEQ], ohi[half, g // 2, :], ALU.subtract).then_inc(o_ready, 1)
            dve.wait_ge(gates_ready, 1)
            for u in range(X_MO, X_OUT + 1):
                if u < X_OUT:
                    dve.wait_ge(unit_done, MIX.first + u + 1)
                    m = 2 * (u - X_MO)
                    t_ = gates[:, 8 + m:10 + m, :]
                    step(nc.vector.tensor_tensor(t_, t_, ps[u % SLOTS][:, :].rearrange("p (g n) -> p g n", n=SEQ), ALU.mult))
                    nc.vector.tensor_tensor(xb[:, m:m + 2, 0:SEQ], xb[:, m:m + 2, 0:SEQ], t_, ALU.add).then_inc(tiles_read, 1)
                    mix_splits(u)
                if u > X_MO:
                    m = 2 * (u - 1 - X_MO)
                    dve.wait_ge(y_hi, u - X_MO)
                    nc.vector.tensor_tensor(hlo[:, m:m + 2, 0:SEQ], xb[:, m:m + 2, 0:SEQ], hhi[:, m:m + 2, 0:SEQ], ALU.subtract).then_inc(y_lo, 1)
            step(nc.vector.memset(sums[:, 0:SEQ], 0.0))
            for i in range(2):
                gated_residual(M0 + X_OUT // SLOTS + i, i, KT, 1, 5, squares=6)
            dve_late_norm(6, 2, "rms2", [KT - 1])
            dve_hidden_late("up3")
            down_squares("down3", 8, 7)
            dve_norm(7, SEQ, hf, NORM_EPS, lambda m: col(V_NORM + 3 * KT + m), None, dst=outb)

        @block.tensor
        def _(pe):
            def unit(t, s, blocks, n, rhi, rlo, out=None, first=True, last=True, k0=0, k_wait=None):
                pe.wait_ge(lo_split, t * SLOTS + (s + 1))
                if first:
                    pe.wait_ge(tiles_read, t * SLOTS + (s + 1))
                out = ps[s][:, 0:n] if out is None else out
                for k in range(blocks):
                    if k_wait is not None:
                        k_wait(k)
                    w = slice(k * P, (k + 1) * P)
                    nc.tensor.matmul(out, whi[:, s, w], rhi(k0 + k), start=first and k == 0, stop=False)
                    nc.tensor.matmul(out, whi[:, s, w], rlo(k0 + k), start=False, stop=False)
                    ins = nc.tensor.matmul(out, wlo[:, s, w], rhi(k0 + k), start=False, stop=last and k == blocks - 1)
                ins.then_inc(unit_done, 1)

            def first_step(t, n, version, norm=None):
                for s in range(2):
                    pe.wait_ge(lo_split, t * SLOTS + s + 1)
                    pe.wait_ge(tiles_read, t * SLOTS + s + 1)
                    for k in range(KT):
                        if s == 0:
                            pe.wait_ge(rhs_hi, RHS_AT[version] + k + 1)
                        w = slice(k * P, (k + 1) * P)
                        nc.tensor.matmul(ps[s][:, 0:n], whi[:, s, w], hhi[:, k, 0:n], start=k == 0, stop=False)
                        nc.tensor.matmul(ps[s][:, 0:n], wlo[:, s, w], hhi[:, k, 0:n], start=False, stop=False)
                for s in range(2):
                    for k in range(KT):
                        if s == 0:
                            pe.wait_ge(rhs_ready, RHS_AT[version] + k + 1)
                        ins = nc.tensor.matmul(ps[s][:, 0:n], whi[:, s, k * P:(k + 1) * P], hlo[:, k, 0:n], start=False, stop=k == KT - 1)
                    ins.then_inc(unit_done, 1)
                for s in range(2, SLOTS):
                    if s == {4: 3, 6: 2}.get(norm):
                        pe_norm(norm, SEQ)
                    unit(t, s, KT, n, lambda k: hhi[:, k, 0:n], lambda k: hlo[:, k, 0:n])

            def stream(phase, n, version=None, norm=None):
                t0 = phase.first // SLOTS
                if version:
                    first_step(t0, n, version, norm)
                with pe.Fori(t0 + (1 if version else 0), t0 + phase.units // SLOTS) as t:
                    for s in range(SLOTS):
                        unit(t, s, KT, n, lambda k: hhi[:, k, 0:n], lambda k: hlo[:, k, 0:n])

            def one(u):
                a_unit(u // SLOTS, u % SLOTS)

            def a_unit(t, s):
                unit(t, s, KT, TOK, lambda k: hhi[:, k, 0:TOK], lambda k: hlo[:, k, 0:TOK])

            pe.wait_ge(ld_small, 48)
            pe.wait_ge(ld_x, 16 * KT)
            for k in range(KT):
                last = nc.tensor.matmul(ps[7][0:2 * HEADS, 0:TOK], wab[:, k, :], hf[:, k, :], start=k == 0, stop=k == KT - 1)
            last.then_inc(mm_ab, 1)
            first_step(0, TOK, "x")
            pe.wait_ge(ld_cm, 16)
            pe.wait_ge(ab_ready, 2)
            for j in range(3):
                lhs = abm[0:16, :] if j == 2 else abt[0:16, META + j * P:META + (j + 1) * P]
                last = nc.tensor.matmul(ps[7][:, 16 * j:16 * j + 16], lhs, cm[0:16, C_IDENT, 0:16], start=True, stop=True)
            last.then_inc(mm_gate, 1)
            one(SLOTS)
            one(SLOTS + 1)
            one(SLOTS + 2)
            pe.wait_ge(gl_ready, 1)
            g_ = S_(6)
            nc.tensor.matmul(ps[7][:, 64:64 + MB], cm[:, C_CAUSAL, :], g_[:, 0:MB], start=True, stop=True)
            nc.tensor.matmul(ps[7][:, 64 + MB:64 + NBLK], cm[:, C_CAUSAL_META, :], g_[:, MB:NBLK], start=True, stop=True)
            nc.tensor.matmul(ps[7][:, 96:96 + MB], ones, g_[:, 0:MB], start=True, stop=True)
            nc.tensor.matmul(ps[7][:, 96 + MB:96 + NBLK], cm[:, C_SAME_META, :], g_[:, MB:NBLK], start=True, stop=True).then_inc(mm_cum, 1)
            one(SLOTS + 3)
            with pe.Fori(2, U_V // SLOTS) as t:
                for s in range(SLOTS):
                    a_unit(t, s)

            k_b = lambda b: blocks_at(0, b, 1)
            q_b = lambda b: blocks_at(1, b, 1)
            v_b = lambda b: blocks_at(2, b, 1)

            for u in U_FIRST:
                one(u)
            for i, sq in enumerate((ex, ca)):
                pe.wait_ge(sq_gdn, i + 1)
                for b in range(NBLK):
                    last = nc.tensor.matmul(ps[7][:, i * NBLK + b:i * NBLK + b + 1], sq[:, b, :], ones[:, 0:1], start=True, stop=True)
            last.then_inc(mm_norm, 1)
            one(U_NEXT)

            def spread(bank, b0, n, which):
                for j in range(n):
                    last = nc.tensor.matmul(ps[bank][:, j * P:(j + 1) * P], S_(which)[:, b0 + j:b0 + j + 1].to_broadcast([P, P]),
                                            ident, start=True, stop=True)
                return last

            pe.wait_ge(cols_ready, 1)
            for g, (b0, n) in enumerate(GROUPS):
                if g:
                    pe.wait_ge(m_ready, g)
                    pe.wait_ge(d_exp, 2 * g)
                spread(4, b0, n, 7).then_inc(mm_gb, 1)
                spread(5, b0, n, 12)
                for j in range(n):
                    b = b0 + j
                    nc.tensor.matmul(ps[6][:, j * P:(j + 1) * P], k_b(b), k_b(b), start=True, stop=True)
                    last = nc.tensor.matmul(ps[7][:, j * P:(j + 1) * P], k_b(b), q_b(b), start=True, stop=True)
                last.then_inc(mm_cb, 1)
                if g < 4:
                    one(U_NEXT + 1 + g)

            pe.wait_ge(a_act, 3 * KT)
            for g, (b0, n) in enumerate(GROUPS):
                for kind, x_b in enumerate((k_b, v_b)):
                    if g > 1:
                        pe.wait_ge(tr_read, 2 * (g - 2) + kind + 1)
                    for j in range(n):
                        last = nc.tensor.transpose(ps[2 * (g % 2) + kind][:, j * P:(j + 1) * P], x_b(b0 + j), ident)
                    last.then_inc(mm_tr, 1)
            pe.wait_ge(m_ready, len(GROUPS))
            pe.wait_ge(d_exp, 2 * len(GROUPS))
            for g, (b0, n) in enumerate(GROUPS):
                pe.wait_ge(gu0_ready, g + 1)
                if g == 4:
                    pe.wait_ge(tu_ready, 1)
                for j in range(n):
                    last = nc.tensor.transpose(ps[4 + g % 4][:, j * P:(j + 1) * P], gu[:, b0 + j, :], ident)
                last.then_inc(mm_t0, 1)
            pe.wait_ge(tr_read, 2 * len(GROUPS))

            def x_mm(l, g):
                b0, n = GROUPS[g]
                pe.wait_ge(tu_ready, (l - 1) * 5 + (g + 1))
                for j in range(n):
                    last = nc.tensor.matmul(ps[g % 2][:, j * P:(j + 1) * P], bn[:, b0 + j, :], gt[:, b0 + j, :], start=True, stop=True)
                last.then_inc(mm_x, 1)

            def y_mm(l, g, both=True):
                b0, n = GROUPS[g]
                pe.wait_ge(x_ready, (l - 1) * 5 + (g + 1))
                if both:
                    for j in range(n):
                        nc.tensor.matmul(ps[2 + g % 3][:, j * P:(j + 1) * P], gu[:, b0 + j, :], ex[:, b0 + j, :], start=True, stop=True)
                for j in range(n):
                    last = nc.tensor.matmul(ps[5 + g % 3][:, j * P:(j + 1) * P], ex[:, b0 + j, :], gu[:, b0 + j, :], start=True, stop=True)
                last.then_inc(mm_y, 1)

            def level(l, groups, both=True):
                x_mm(l, 0)
                x_mm(l, 1)
                for g in range(groups):
                    if g < 2:
                        pe.wait_ge(tu_ready, (l - 1) * 5 + (g + 4))
                    y_mm(l, g, both)
                    if g + 2 < groups:
                        x_mm(l, g + 2)

            with pe.Fori(1, LEVELS - 1) as l:
                level(l, len(GROUPS))
            level(LEVELS - 1, 4, both=False)

            pe.wait_ge(tu_ready, LEVELS * 5 - 1)
            pe.wait_ge(qg_ready, len(GROUPS))
            nc.tensor.matmul(ps[4][:, 0:P], gu[:, MB, :], v_b(MB), start=True, stop=True).then_inc(mm_v0, 1)
            one(U_Z)
            pe.wait_ge(vm_ready, 1)
            for q in range(2):
                nc.tensor.matmul(ps[5 + q][:, :], ktm[:, MB, :], rr[:, 4 * q:4 * q + 4, :], start=True, stop=True).then_inc(mm_s0, 1)
            one(U_Z + 1)
            pe.wait_ge(v0_read, 1)
            nc.tensor.matmul(ps[7][:, 0:P], vn[:, 7, :], ca[:, MB, :], start=True, stop=True).then_inc(mm_o0, 1)
            for c in range(2):
                for q in range(2):
                    pe.wait_ge(s_ready, 2 * c + q + 1)
                    for j in range(4):
                        h = 4 * q + j
                        last = nc.tensor.matmul(ps[4 + q][:, j * P:(j + 1) * P], k_b(2 * h + c), st[:, h, :], start=True, stop=True)
                    last.then_inc(mm_ks, 1)
                one(U_Z + 2 * c + 2)
                for q in range(2):
                    pe.wait_ge(r_ready, 2 * c + q + 1)
                    pe.wait_ge(o_read, 1 if c == 0 else 1 + q + 1)
                    for j in range(4):
                        h = 4 * q + j
                        last = nc.tensor.matmul(ps[6 + q][:, j * P:(j + 1) * P], gu[:, 2 * h + c, :], rr[:, h, :], start=True, stop=True)
                    last.then_inc(mm_vn, 1)
                one(U_Z + 2 * c + 3)
                for q in range(2):
                    pe.wait_ge(vn_ready, 2 * c + q + 1)
                    if c == 0:
                        for j in range(4):
                            h = 4 * q + j
                            last = nc.tensor.matmul(ps[4 + q][:, j * P:(j + 1) * P], ktm[:, 2 * h, :], vn[:, h, :], start=True, stop=True)
                        last.then_inc(mm_ds, 1)
                    for j in range(4):
                        h = 4 * q + j
                        nc.tensor.matmul(ps[6 + q][:, j * P:(j + 1) * P], st[:, h, :], q_b(2 * h + c), start=True, stop=False)
                        last = nc.tensor.matmul(ps[6 + q][:, j * P:(j + 1) * P], vn[:, h, :], ca[:, 2 * h + c, :], start=False, stop=True)
                    last.then_inc(mm_o, 1)
            one(U_Z + 6)

            pe.wait_ge(sq_gdn, 3)
            for b in range(NBLK):
                last = nc.tensor.matmul(ps[7][:, b:b + 1], ex[:, b, :], ones[:, 0:1], start=True, stop=True)
            last.then_inc(mm_norm, 1)
            one(U_Z + 7)
            pe.wait_ge(tiles_read, SLOTS + U_Z + KT)
            pe.wait_ge(cols_ready, 2)
            for g in (4, 0, 1, 2, 3):
                spread([1, 2, 3, 4, 0][g], *GROUPS[g], 12).then_inc(mm_gb, 1)

            def down(name, n):
                t0 = PH[name].first // SLOTS

                def wait_for(h0, upto):
                    def k_wait(k):
                        if h0 + k in upto:
                            pe.wait_ge(hid_ready, HID_AT[name.replace("down", "up")] + h0 + k + 1)
                    return k_wait

                with pe.Fori(t0, t0 + PH[name].units // SLOTS) as t:
                    for s in range(SLOTS):
                        h0 = SLOT_BLOCKS * (s % 2)
                        unit(t, s, SLOT_BLOCKS, n, lambda k: ahi[:, k, 0:n], lambda k: alo[:, k, 0:n], out=ps[s - s % 2][:, 0:n],
                             first=s % 2 == 0, last=s % 2 == 1, k0=h0,
                             k_wait=wait_for(h0, range(FT)) if s < 2 else None)

            def mods(*vectors):
                pe.wait_ge(ada_done, (vectors[-1] + 1) * KT + 1)
                for i in vectors:
                    for m in range(KT):
                        last = nc.tensor.matmul(ps[6][:, KT * i + m:KT * i + m + 1], acc[:, i, m * P:(m + 1) * P], ones[:, 0:1], start=True, stop=True)
                last.then_inc(mods_mm, 1)

            def pe_norm(i, n):
                if i < 4:
                    pe.wait_ge(sum_ready, SUMS_AT[i] + KT)
                    nc.tensor.matmul(ps[4][:, 0:n], cm[:, C_MEAN, :], sums[:, 0:n], start=True, stop=True).then_inc(mean_mm, 1)
                if i >= 4:
                    pe.wait_ge(sum_ready, SUMS_AT[i] + KT)
                    nc.tensor.matmul(ps[5][:, 0:n], cm[:, C_MEAN, :], sums[:, 0:n], start=True, stop=True).then_inc(var_mm, 1)
                    return
                for m in range(KT):
                    pe.wait_ge(sq_ready, i * KT + m + 1)
                    last = nc.tensor.matmul(ps[5][:, 0:n], cm[:, C_MEAN, :], sqb[:, m, 0:n], start=m == 0, stop=m == KT - 1)
                last.then_inc(var_mm, 1)

            stream(PH["a_out"], N_A, "gdn")
            pe_norm(0, N_A)
            stream(PH["up0"], N_A, "ln0")
            down("down0", N_F0)
            pe_norm(1, N_F0)
            mods(0, 1, 2)
            stream(PH["b_cx"], N_F0, "ln1")
            stream(PH["b_gate"], N_F0)
            t0 = PH["b_out"].first // SLOTS
            with pe.Fori(t0, t0 + 2) as t:
                for s in range(SLOTS):
                    unit(t, s, KT, N_B, lambda k: ahi[:, k, 0:N_B], lambda k: alo[:, k, 0:N_B],
                         k_wait=None if s else lambda k: pe.wait_ge(hid_ready, HID_AT["b_gate"] + k + 1))
            pe_norm(2, N_B)
            mods(3, 4, 5)
            stream(PH["up1"], N_B, "ln2")
            down("down1", N_F1)
            pe_norm(3, N_F1)
            mods(6, 7, 8)

            MIX = PH["mix"]
            M0 = MIX.first // SLOTS
            stream(PH["up2"], N_SH, "rms0", norm=4)
            down("down2", SEQ)
            pe_norm(5, SEQ)

            def mix_tile(u):
                def k_wait(k):
                    if k % 2 == 0:
                        pe.wait_ge(y_lo, k // 2 + 1)
                unit(M0 + u // SLOTS, u % SLOTS, KT, SEQ, lambda k: hhi[:, k, 0:SEQ], lambda k: hlo[:, k, 0:SEQ],
                     k_wait=k_wait if u == X_OUT else None)

            def mix_blocks(u, place, banks_free=None):
                s = u % SLOTS
                pe.wait_ge(lo_split, MIX.first + u + 1)
                if banks_free:
                    banks_free()
                for k in range(KT):
                    out, r_hi, r_lo, m, first, last, done = place(k)
                    w = slice(k * P, k * P + m)
                    nc.tensor.matmul(out, whi[:, s, w], r_hi, start=first, stop=False)
                    nc.tensor.matmul(out, whi[:, s, w], r_lo, start=False, stop=False)
                    ins = nc.tensor.matmul(out, wlo[:, s, w], r_hi, start=False, stop=last)
                    if done is not None and k < KT - 1:
                        ins.then_inc(done, 1)
                ins.then_inc(unit_done, 1)

            def q_place(u):
                def place(k):
                    b = (u - X_Q) * KT + k
                    h, kt = b // 3, b % 3
                    return (ps[4 + h // 2][0:96, (h % 2) * SEQ:(h % 2 + 1) * SEQ], lhi[:, kt, :], llo[:, kt, :], 96, kt == 0, kt == 2, q_mm if kt == 2 else None)
                return place

            def k_place(u):
                def place(k):
                    b = (u - X_K) * KT + k
                    h, kt = b // 2, b % 2
                    return (ps[h // 2][:, (h % 2) * SEQ:(h % 2 + 1) * SEQ], lhi[:, 3 + kt, :], llo[:, 3 + kt, :], P, kt == 0, kt == 1, k_mm if kt == 1 else None)
                return place

            first_step(M0, SEQ, "rms1")
            for u in range(SLOTS, X_GA + 2):
                mix_tile(u)
                if u == X_UF + 1:
                    for j in range(5):
                        pe.wait_ge(ls_sq, j + 1)
                        at_ = 0 if j < 3 else SEQ
                        last = nc.tensor.matmul(ps[4][:, at_:at_ + SEQ], ones, lsq[:, j, :], start=j in (0, 3), stop=j in (2, 4))
                    last.then_inc(lat_mm, 1)
            for u in range(X_GA + 2, X_Q):
                mix_tile(u)
            pe.wait_ge(lat_ready, 5)
            for u in range(X_Q, X_K):
                mix_blocks(u, q_place(u))
            for u in range(X_K, X_V):
                mix_blocks(u, k_place(u), lambda: pe.wait_ge(tiles_read, SLOTS + MIX.first + X_Q))
            pe.wait_ge(lo_split, MIX.first + X_V + 1)
            s = X_V % SLOTS
            for c in range(2):
                pe.wait_ge(q_read, c + 1)
                out = ps[4 + c][:, :]
                cc = slice(c * P, (c + 1) * P)
                for kt in range(2):
                    w = slice(kt * 512, (kt + 1) * 512)
                    nc.tensor.matmul(out, lhi[:, 3 + kt, cc], whi[:, s, w], start=kt == 0, stop=False)
                    nc.tensor.matmul(out, llo[:, 3 + kt, cc], whi[:, s, w], start=False, stop=False)
                    last = nc.tensor.matmul(out, lhi[:, 3 + kt, cc], wlo[:, s, w], start=False, stop=kt == 1)
                if c == 0:
                    last.then_inc(v_mm, 1)
            last.then_inc(unit_done, 1)

            pe.wait_ge(k_read, 4)
            for u in range(X_GB, X_GB + 2):
                mix_tile(u)
            pe.wait_ge(ld_dft, 16)
            pe.wait_ge(v_read, 2)
            pe.wait_ge(q_read, 4)
            for j in range(4):
                for g in (2 * (j % 2), 2 * (j % 2) + 1):
                    last = nc.tensor.matmul(ps[4 + j][:, (g % 2) * SEQ:(g % 2 + 1) * SEQ], uf[:, g, (j // 2) * P:(j // 2 + 1) * P], dft[:, 0, :], start=True, stop=True)
                last.then_inc(four1, 1)
            for u in range(X_GB + 2, X_GB + 4):
                mix_tile(u)
            pe.wait_ge(pf_ready, 4)
            for g in range(4):
                for c in range(2):
                    nc.tensor.matmul(ps[4 + g][:, 0:SEQ], pf[:, c, g, 0:P], dft[:, 1 + c, :], start=c == 0, stop=False)
                    last = nc.tensor.matmul(ps[4 + g][:, 0:SEQ], pf[:, c, g, P:2 * P], dft[:, 3 + c, :], start=False, stop=c == 1)
                last.then_inc(four2, 1)
            for u in range(X_GB + 4, X_GC):
                mix_tile(u)

            def out_place(u, r_hi, r_lo):
                def place(k):
                    kt = k % 4
                    return (ps[u % SLOTS][:, (k // 4) * SEQ:(k // 4 + 1) * SEQ], r_hi[:, kt, :], r_lo[:, kt, :], P, kt == 0, kt == 3, None)
                return place

            pe.wait_ge(f_ready, 4)
            for h in range(HEADS + 2):
                if h < HEADS:
                    pe.wait_ge(rope_ready, h // 2 + 1)
                    if h >= 2:
                        pe.wait_ge(p_exp, h - 1)
                    for c in range(2):
                        last = nc.tensor.matmul(ps[4 + h % 2][:, c * SEQ:(c + 1) * SEQ], qt[0:96, h, c * P:(c + 1) * P], kt_[0:96, h, :], start=True, stop=True)
                    last.then_inc(s_mm, 1)
                if 1 <= h <= HEADS:
                    u = X_GC + h - 1
                    if u < X_FO:
                        mix_tile(u)
                    else:
                        mix_blocks(u, out_place(u, fhi, flo), lambda: pe.wait_ge(tiles_read, MIX.first + u + 1))
                if 0 <= h - 1 < HEADS:
                    g = h - 1
                    pe.wait_ge(p_ready, g + 1)
                    if g >= 2:
                        pe.wait_ge(o_ready, g - 1)
                    for kc in range(2):
                        for c in range(2):
                            last = nc.tensor.transpose(ps[6 + g % 2][:, kc * SEQ + c * P:kc * SEQ + (c + 1) * P], pr[:, g % 2, c, kc * P:(kc + 1) * P], ident)
                    last.then_inc(t_mm, 1)
                if h >= 2:
                    g = h - 2
                    pe.wait_ge(t_read, g + 1)
                    half = (g % 2) * 64
                    for kc in range(2):
                        last = nc.tensor.matmul(ps[6 + g % 2][half:half + 64, 0:SEQ], vt[:, kc, g * 64:(g + 1) * 64], pt[:, g % 2, kc, :], start=kc == 0, stop=kc == 1)
                    last.then_inc(o_mm, 1)
            pe.wait_ge(o_ready, HEADS)
            for u in range(X_MO, X_OUT):
                mix_blocks(u, out_place(u, ohi, olo), lambda: pe.wait_ge(tiles_read, MIX.first + u + 1))
            for u in range(X_OUT, MIX.units):
                mix_tile(u)
            stream(PH["up3"], N_SH, "rms2", norm=6)
            down("down3", SEQ)
            pe_norm(7, SEQ)


def constants():
    i, j = np.arange(P)[:, None], np.arange(P)[None, :]
    same = i // META == j // META
    out = [i == j, np.full((P, P), 1.0 / D), np.ones((P, P)), i <= j, same & (i <= j), same]
    out.append(-1.0 * ((i >> 1 == j >> 1) & (i < j)))
    for l in range(1, LEVELS):
        out.append(-1.0 * ((i >> (l + 1) == j >> (l + 1)) & (i >> l & 1 == 1) & (j >> l & 1 == 0)))
    return np.ascontiguousarray(np.stack(out, 1).astype(np.float32))


def blocks_of(w):
    k, n = w.shape
    return w.reshape(k // P, P, n // P, P).transpose(2, 1, 0, 3).reshape(n // P, P, k)


def pairs_of(a, b):
    return np.stack([blocks_of(a), blocks_of(b)], 1).reshape(-1, P, a.shape[0])


def halves_of(w):
    n = w.shape[1] // P
    return blocks_of(w).reshape(n, P, 2, SLOT_BLOCKS * P).transpose(0, 2, 1, 3).reshape(2 * n, P, SLOT_BLOCKS * P)


def lay_out(a):
    f = {}
    x = np.concatenate([a["meta"], a["x"][0]], 0)
    f["x"] = x.T.reshape(KT, P, TOK).transpose(1, 0, 2)
    w = a["a_w_in"][0]
    q, k, v, z, ba = (w[:, 0:1024], w[:, 1024:2048], w[:, 2048:3072], w[:, 3072:4096], w[:, 4096:])
    f["w_a_in"] = np.concatenate([blocks_of(m) for m in (k, q, v, z)])
    f["w_ab"] = ba.reshape(KT, P, 16).transpose(1, 0, 2)
    f["w_a_out"] = blocks_of(a["a_w_out"][0])
    b, c, xv = np.split(a["b_w_in"][0], 3, axis=1)
    f["w_b_cx"] = pairs_of(c, xv)
    f["w_b_gate"] = blocks_of(b)
    f["w_b_out"] = blocks_of(a["b_w_out"][0])
    for l in range(2):
        u, g = np.split(a["ffn_w_up"][l], 2, axis=1)
        f[f"w_up{l}"] = pairs_of(u, g)
        f[f"w_down{l}"] = halves_of(a["ffn_w_down"][l])
    for l, n in ((2, "ffn1"), (3, "ffn2")):
        f[f"w_up{l}"] = pairs_of(a[n + "_w_gate_2"][0], a[n + "_w_up_2"][0])
        f[f"w_down{l}"] = halves_of(a[n + "_w_down_2"][0])
    f["ada_w"] = a["ada_w_2"][0].reshape(KT, P, 9, D).transpose(2, 0, 1, 3).reshape(ADA_OPS, P, D)

    vec = np.zeros((P, N_VEC), np.float32)
    conv = a["a_conv"][0]
    kqv = np.concatenate([conv[:, 1024:2048], conv[:, 0:1024], conv[:, 2048:]], 1)
    vec[:, V_ACONV:V_ACONV + 96] = kqv.reshape(4, 24, P).transpose(2, 1, 0).reshape(P, 96)
    vec[:, V_FCONV:V_FCONV + 132] = a["ffn_conv"].reshape(2, 3, FT, P).transpose(3, 0, 2, 1).reshape(P, 132)
    vec[:, V_BCONV:V_BCONV + 24] = a["b_conv"][0].reshape(3, KT, P).transpose(2, 1, 0).reshape(P, 24)
    ln = np.stack([a["ln_mix_g"], a["ln_mix_b"], a["ln_ffn_g"], a["ln_ffn_b"]], 1)
    vec[:, V_LN:V_LN + 64] = ln.reshape(8 * KT, P).T
    vec[:, V_ANORM] = a["a_norm"][0]
    rows = np.arange(P) // META
    for at_, v_ in ((V_ALOG, a["a_log"][0]), (V_DT, a["a_dt_bias"][0])):
        vec[:, at_:at_ + MB] = np.repeat(v_, 2)[None]
        vec[:, at_ + MB] = v_[rows]
    vec[:, V_HEAD:V_HEAD + HEADS] = rows[:, None] == np.arange(HEADS)[None]
    vec[:, V_C:V_C + KT] = a["c_2"].reshape(KT, P).T
    vec[:, V_ADAB:V_ADAB + 72] = a["ada_b_2"][0].reshape(72, P).T
    norms = np.stack([a["ffn1_norm_2"][0], a["mix_norm_2"][0], a["ffn2_norm_2"][0], a["final_norm_2"]])
    vec[:, V_NORM:V_NORM + 32] = norms.reshape(32, P).T
    vec[:, V_QN:V_QN + 3] = a["q_norm_2"][0].reshape(3, P).T
    vec[:, V_KVN:V_KVN + 2] = a["kv_norm_2"][0].reshape(2, P).T
    f["vec"] = vec
    f["cm"] = constants()
    mixing_layout(a, f)
    return {k_: np.ascontiguousarray(v_) for k_, v_ in f.items()}


def mixing_layout(a, f):
    w = a["w_in_2"][0]
    u_f, q_lat, kv_lat, k_rope, gate = np.split(w, [512, 896, 1152, 1184], axis=1)
    rope = np.zeros((D, P), np.float32)
    rope[:, 64:96] = k_rope
    q_up = a["w_q_up_2"][0].reshape(3, P, HEADS, 96)
    q_blk = np.zeros((HEADS, 3, P, P), np.float32)
    q_blk[..., 0:96] = q_up.transpose(2, 0, 1, 3)
    kv = a["w_kv_up_2"][0].reshape(2, P, HEADS, P)
    k_blk = kv.transpose(2, 0, 1, 3)
    v_blk = kv[..., 64:].reshape(2, P, 4, P).transpose(0, 2, 1, 3)

    def units(blk):
        return blk.reshape(-1, KT, P, P).transpose(0, 2, 1, 3).reshape(-1, P, KT * P)

    def out_blocks(m):
        return m.reshape(4, P, KT, P).transpose(2, 0, 1, 3)

    gates = blocks_of(gate)
    f["w_mix"] = np.concatenate([
        blocks_of(rope), blocks_of(q_lat), blocks_of(kv_lat), blocks_of(u_f), gates[0:4],
        units(q_blk), units(k_blk), units(v_blk), gates[4:],
        units(out_blocks(a["w_fourier_out_2"][0])), units(out_blocks(a["w_mla_out_2"][0])),
        blocks_of(a["w_out_2"][0]),
    ])
    f["pos"] = np.tile(a["positions_2"].astype(np.int32), (32, 1))
    d, s = np.arange(P), np.arange(SEQ)
    fd = 2 * np.pi * (d[:, None] * d[None] % P) / P
    fs = 2 * np.pi * (s[:, None] * s[None] % SEQ) / SEQ
    f["dft"] = np.stack([
        np.concatenate([np.cos(fd), np.sin(fd)], 1) / np.sqrt(P),
        *(np.cos(fs) / np.sqrt(SEQ)).reshape(2, P, SEQ), *(-np.sin(fs) / np.sqrt(SEQ)).reshape(2, P, SEQ),
    ], 1).astype(np.float32)
    inv = 1.0 / (np.float32(10000.0) ** (np.arange(16, dtype=np.float32) * np.float32(2.0) / np.float32(32)))
    f["vec"][64:96, V_INVF] = np.tile(inv.astype(np.float32), 2)
    f["vec"][64:80, V_SIGN] = -1.0
    f["vec"][80:96, V_SIGN] = 1.0
    f["vec"][:, V_QN:V_QN + 3] = a["q_norm_2"][0].reshape(3, P).T
    f["vec"][:, V_KVN:V_KVN + 2] = a["kv_norm_2"][0].reshape(2, P).T


def kernel(**inputs):
    import concourse.bacc as bacc
    from concourse.bass_utils import run_bass_kernel_spmd

    arrays = lay_out({k: np.asarray(v) for k, v in inputs.items()})
    nc = bacc.Bacc("TRN2", target_bir_lowering=False, num_devices=1)
    io = {n: nc.dram_tensor("in_" + n, v.shape, mybir.dt.from_np(v.dtype), kind="ExternalInput").ap() for n, v in arrays.items()}
    io["out"] = nc.dram_tensor("out", (P, KT, SEQ), F32, kind="ExternalOutput").ap()
    build(nc, io)
    r = run_bass_kernel_spmd(nc, [{"in_" + n: v for n, v in arrays.items()}], core_ids=[0])
    out = r.results[0]["out"]
    return np.ascontiguousarray(out.transpose(2, 1, 0)).reshape(1, SEQ, D)
```
